# Optimizing a Trainium2 kernel written in Bass

```python
import math
import jax, jax.numpy as jnp
from jax import lax
import numpy as np

D_MODEL = 2048
BATCH = 1
SEQ = 256
DEPTH = 1

N_HGRN_HEADS = 8
HGRN_KEY_DIM = 128
HGRN_VAL_DIM = 128
HGRN_FORGET_WIDTH = N_HGRN_HEADS * HGRN_KEY_DIM
HGRN_WIDTH = N_HGRN_HEADS * HGRN_VAL_DIM
CHUNK = 64
N_DIFF_HEADS = 8
DIFF_HEAD_DIM = 64
DIFF_QK_WIDTH = N_DIFF_HEADS * 2 * DIFF_HEAD_DIM
DIFF_V_DIM = 2 * DIFF_HEAD_DIM
DIFF_V_WIDTH = N_DIFF_HEADS * DIFF_V_DIM
ROPE_DIM = DIFF_HEAD_DIM // 4
ROPE_THETA = 500000.0
Q_BLOCK = 128
D_FF = 5632
N_MOD = 9
EPS = 1e-6
MIX_SIZES = (HGRN_FORGET_WIDTH, HGRN_FORGET_WIDTH, HGRN_WIDTH, HGRN_WIDTH,
             DIFF_QK_WIDTH, DIFF_QK_WIDTH, DIFF_V_WIDTH, D_MODEL, D_MODEL)
MIX_WIDTH = 4 * 1024 + 3 * 1024 + 2 * D_MODEL

kernel_name = "hybrid_hgrn2_diffattn_macaron_adaln"

def _split(t, sizes):
    idx = []
    acc = 0
    for s in sizes[:-1]:
        acc += s
        idx.append(acc)
    return jnp.split(t, idx, axis=-1)

def rmsnorm(x, w):
    xf = x.astype(jnp.float32)
    y = xf * lax.rsqrt(jnp.mean(xf * xf, axis=-1, keepdims=True) + EPS)
    return (y * w.astype(jnp.float32)).astype(x.dtype)

def modulate(n, shift, scale):
    return n * (1 + scale[:, None, :]) + shift[:, None, :]

def swiglu(x, w_in, w_out):
    g, u = jnp.split(x @ w_in, 2, axis=-1)
    return (jax.nn.silu(g) * u) @ w_out

def partial_rope(x, positions):
    half = ROPE_DIM // 2
    inv_freq = ROPE_THETA ** (-jnp.arange(half, dtype=jnp.float32) / half)
    ang = positions.astype(jnp.float32)[..., None] * inv_freq
    cos = jnp.cos(ang)[:, :, None, None, :]
    sin = jnp.sin(ang)[:, :, None, None, :]
    xr = x[..., :ROPE_DIM].astype(jnp.float32)
    x1, x2 = xr[..., :half], xr[..., half:]
    rot = jnp.concatenate([x1 * cos - x2 * sin, x2 * cos + x1 * sin], axis=-1)
    return jnp.concatenate([rot.astype(x.dtype), x[..., ROPE_DIM:]], axis=-1)

def hgrn2(q, f_pre, inp, lb):
    B, S, H, K = q.shape
    V = inp.shape[-1]
    N = S // CHUNK
    f = lb + (1 - lb) * jax.nn.sigmoid(f_pre.astype(jnp.float32))
    logf = jnp.log(f)
    k = 1 - f

    def to_chunks(t):
        return t.reshape(B, N, CHUNK, H, t.shape[-1]).transpose(1, 0, 3, 2, 4)

    qc = to_chunks(q.astype(jnp.float32))
    kc = to_chunks(k)
    vc = to_chunks(inp.astype(jnp.float32))
    bc = jnp.cumsum(to_chunks(logf), axis=3)
    causal = jnp.tril(jnp.ones((CHUNK, CHUNK), dtype=bool))

    def step(state, xs):
        qh, kh, vh, bh = xs
        inter = jnp.einsum('bhck,bhkv->bhcv', qh * jnp.exp(bh), state)
        diff = bh[:, :, :, None, :] - bh[:, :, None, :, :]
        decay = jnp.where(causal[:, :, None], jnp.exp(jnp.minimum(diff, 0.0)), 0.0)
        scores = jnp.einsum('bhtk,bhtsk,bhsk->bhts', qh, decay, kh)
        o = inter + jnp.einsum('bhts,bhsv->bhtv', scores, vh)
        b_last = bh[:, :, -1, :]
        new_state = jnp.exp(b_last)[..., None] * state + jnp.einsum(
            'bhsk,bhsv->bhkv', kh * jnp.exp(b_last[:, :, None, :] - bh), vh)
        return new_state, o

    s0 = jnp.zeros((B, H, K, V), jnp.float32)
    _, o = lax.scan(step, s0, (qc, kc, vc, bc))
    return o.transpose(1, 0, 3, 2, 4).reshape(B, S, H, V)

def diff_attention(q, k, v, lam):
    B, S, H, _, dh = q.shape
    scale = 1.0 / math.sqrt(dh)
    qt = q.transpose(0, 2, 3, 1, 4)
    kt = k.transpose(0, 2, 3, 1, 4)
    vt = v.transpose(0, 2, 1, 3)
    kpos = jnp.arange(S)

    def block(i):
        start = i * Q_BLOCK
        qb = lax.dynamic_slice_in_dim(qt, start, Q_BLOCK, axis=3)
        s = jnp.einsum('bhcqd,bhckd->bhcqk', qb, kt).astype(jnp.float32) * scale
        qpos = start + jnp.arange(Q_BLOCK)
        mask = kpos[None, :] <= qpos[:, None]
        p = jax.nn.softmax(jnp.where(mask, s, -jnp.inf), axis=-1)
        w = p[:, :, 0] - lam * p[:, :, 1]
        return jnp.einsum('bhqk,bhkv->bhqv', w.astype(vt.dtype), vt)

    out = lax.map(block, jnp.arange(S // Q_BLOCK))
    return out.transpose(1, 0, 3, 2, 4).reshape(B, S, H, v.shape[-1])

def setup_inputs(seed: int = 0) -> dict:
    key = jax.random.key(seed)
    ks = jax.random.split(key, 32)
    L = DEPTH
    f32 = jnp.float32

    def w(k, shape, fan_in, mult=1.0):
        return jax.random.normal(k, shape, f32) * (mult * fan_in ** -0.5)

    def gain(k, shape):
        return 1.0 + 0.02 * jax.random.normal(k, shape, f32)

    return {
        "x": jax.random.normal(ks[0], (BATCH, SEQ, D_MODEL), f32),
        "c": jax.random.normal(ks[1], (BATCH, D_MODEL), f32),
        "positions": jnp.broadcast_to(jnp.arange(SEQ, dtype=jnp.int32), (BATCH, SEQ)),
        "ada_w": w(ks[2], (L, D_MODEL, N_MOD * D_MODEL), D_MODEL, 0.5),
        "ada_b": 0.02 * jax.random.normal(ks[3], (L, N_MOD * D_MODEL), f32),
        "norm1_w": gain(ks[4], (L, D_MODEL)),
        "ffn1_w_in": w(ks[5], (L, D_MODEL, 2 * D_FF), D_MODEL),
        "ffn1_w_out": w(ks[6], (L, D_FF, D_MODEL), D_FF),
        "norm2_w": gain(ks[7], (L, D_MODEL)),
        "mix_w_in": w(ks[8], (L, D_MODEL, MIX_WIDTH), D_MODEL),
        "hgrn_lb": 0.5 * jax.random.normal(ks[9], (L + 1, HGRN_FORGET_WIDTH), f32),
        "hgrn_norm_w": gain(ks[10], (L, HGRN_VAL_DIM)),
        "hgrn_w_out": w(ks[11], (L, HGRN_WIDTH, D_MODEL), HGRN_WIDTH),
        "diff_q_norm_w": gain(ks[12], (L, DIFF_HEAD_DIM)),
        "diff_k_norm_w": gain(ks[13], (L, DIFF_HEAD_DIM)),
        "diff_lq1": 0.1 * jax.random.normal(ks[14], (L, DIFF_HEAD_DIM), f32),
        "diff_lk1": 0.1 * jax.random.normal(ks[15], (L, DIFF_HEAD_DIM), f32),
        "diff_lq2": 0.1 * jax.random.normal(ks[16], (L, DIFF_HEAD_DIM), f32),
        "diff_lk2": 0.1 * jax.random.normal(ks[17], (L, DIFF_HEAD_DIM), f32),
        "diff_subln_w": gain(ks[18], (L, DIFF_V_DIM)),
        "diff_w_out": w(ks[19], (L, DIFF_V_WIDTH, D_MODEL), DIFF_V_WIDTH),
        "mix_w_o": w(ks[20], (L, D_MODEL, D_MODEL), D_MODEL),
        "norm3_w": gain(ks[21], (L, D_MODEL)),
        "ffn2_w_in": w(ks[22], (L, D_MODEL, 2 * D_FF), D_MODEL),
        "ffn2_w_out": w(ks[23], (L, D_FF, D_MODEL), D_FF),
    }

def reference(x, c, positions, ada_w, ada_b, norm1_w, ffn1_w_in, ffn1_w_out, norm2_w,
              mix_w_in, hgrn_lb, hgrn_norm_w, hgrn_w_out, diff_q_norm_w, diff_k_norm_w,
              diff_lq1, diff_lk1, diff_lq2, diff_lk2, diff_subln_w, diff_w_out, mix_w_o,
              norm3_w, ffn2_w_in, ffn2_w_out):
    B, S, D = x.shape
    lb_all = jnp.cumsum(jax.nn.softmax(hgrn_lb.astype(jnp.float32), axis=0), axis=0)
    h = x
    for l in range(DEPTH):
        mods = jnp.split(jax.nn.silu(c) @ ada_w[l] + ada_b[l], N_MOD, axis=-1)
        sh1, sc1, g1, sh2, sc2, g2, sh3, sc3, g3 = mods

        n1 = modulate(rmsnorm(h, norm1_w[l]), sh1, sc1)
        h = h + 0.5 * g1[:, None, :] * swiglu(n1, ffn1_w_in[l], ffn1_w_out[l])

        u = modulate(rmsnorm(h, norm2_w[l]), sh2, sc2)
        hq, hf, hi, hg, dq, dk, dv, ga, gb = _split(u @ mix_w_in[l], MIX_SIZES)

        lb = lb_all[l].reshape(N_HGRN_HEADS, HGRN_KEY_DIM)
        o_a = hgrn2(hq.reshape(B, S, N_HGRN_HEADS, HGRN_KEY_DIM),
                    hf.reshape(B, S, N_HGRN_HEADS, HGRN_KEY_DIM),
                    hi.reshape(B, S, N_HGRN_HEADS, HGRN_VAL_DIM), lb).astype(u.dtype)
        o_a = rmsnorm(o_a, hgrn_norm_w[l]) * jax.nn.silu(hg.reshape(B, S, N_HGRN_HEADS, HGRN_VAL_DIM))
        y_a = o_a.reshape(B, S, HGRN_WIDTH) @ hgrn_w_out[l]

        q = dq.reshape(B, S, N_DIFF_HEADS, 2, DIFF_HEAD_DIM)
        k = dk.reshape(B, S, N_DIFF_HEADS, 2, DIFF_HEAD_DIM)
        q = partial_rope(rmsnorm(q, diff_q_norm_w[l]), positions)
        k = partial_rope(rmsnorm(k, diff_k_norm_w[l]), positions)
        v = dv.reshape(B, S, N_DIFF_HEADS, DIFF_V_DIM)
        lam_init = 0.8 - 0.6 * math.exp(-0.3 * l)
        lam = (jnp.exp(jnp.sum(diff_lq1[l].astype(jnp.float32) * diff_lk1[l].astype(jnp.float32)))
               - jnp.exp(jnp.sum(diff_lq2[l].astype(jnp.float32) * diff_lk2[l].astype(jnp.float32)))
               + lam_init)
        o_b = diff_attention(q, k, v, lam)
        o_b = rmsnorm(o_b, diff_subln_w[l]) * (1 - lam_init)
        y_b = o_b.reshape(B, S, DIFF_V_WIDTH) @ diff_w_out[l]

        mix = jax.nn.sigmoid(ga) * y_a + jax.nn.sigmoid(gb) * y_b
        h = h + g2[:, None, :] * (mix @ mix_w_o[l])

        n3 = modulate(rmsnorm(h, norm3_w[l]), sh3, sc3)
        h = h + 0.5 * g3[:, None, :] * swiglu(n3, ffn2_w_in[l], ffn2_w_out[l])
    return h


_drawn_inputs = setup_inputs


def setup_inputs(seed=0):
    import zlib

    import numpy as np

    out = dict(_drawn_inputs(seed))
    spreads = {}
    factors = {'ada_b': 2.939,
     'norm1_w': 8.0,
     'norm2_w': 8.0,
     'hgrn_norm_w': 22.775,
     'diff_q_norm_w': 26.687,
     'diff_k_norm_w': 25.624,
     'diff_lq1': 64.0,
     'diff_lk1': 6.148,
     'diff_lq2': 6.096,
     'diff_lk2': 3.181,
     'diff_subln_w': 64.0,
     'norm3_w': 30.607}
    for name, (base, spread) in spreads.items():
        noise = np.random.default_rng([zlib.crc32(name.encode()), seed]).standard_normal(out[name].shape)
        drawn = base * np.exp(spread * noise) if base else spread * noise
        out[name] = __import__('jax').numpy.asarray(drawn.astype(out[name].dtype))
    for name, factor in factors.items():
        out[name] = (out[name] * factor).astype(out[name].dtype)
    return out
```

```python
from contextlib import ExitStack

import numpy as np

import concourse.bass as bass
from concourse import mybir

F32 = mybir.dt.float32
F32R = mybir.dt.float32r
I32 = mybir.dt.int32
ALU = mybir.AluOpType
ACT = mybir.ActivationFunctionType
AX_X = mybir.AxisListType.X

P = 128
D = 2048
SEQ = 256
D_FF = 5632
MIX_WIDTH = 11264
HEADS = 8
HGRN_CHUNK = 64
DH = 64
ROPE_HALF = 8
ROPE_THETA = 500000.0
EPS = 1e-6
LAM_INIT = 0.2

KD = D // P
KF = D_FF // P
COLS = 512
BLK = COLS // P
KU = 2
RING = 4
LEAD = RING

U_IN = KD // KU
U_OUT = KF // KU
U_HEAD = HEADS // KU
PAIRS = D_FF // COLS
DJOBS = D // COLS
assert MIX_WIDTH == 2 * PAIRS * COLS

UNIT0, JOB0 = {}, {}
_u = _j = 0
for _name, _jobs, _units in (("ffn1_in", 2 * PAIRS, U_IN), ("ffn1_out", DJOBS, U_OUT), ("mix_in", 2 * PAIRS, U_IN),
                             ("heads_out", 2 * DJOBS, U_HEAD), ("mix_out", DJOBS, U_IN),
                             ("ffn2_in", 2 * PAIRS, U_IN), ("ffn2_out", DJOBS, U_OUT)):
    UNIT0[_name], JOB0[_name] = _u, _j
    _u += _jobs * _units
    _j += _jobs
UNITS = _u

N_MOD = 9
ADA_CHUNKS = N_MOD * D // COLS
ADA_PRE = 2 * D // COLS
ADA_PER_OUT = 3
ADA0 = {"ffn1_in": ADA_PRE, "ffn1_out": ADA_PRE + PAIRS, "mix_in": ADA_PRE + PAIRS + 2 * ADA_PER_OUT}
assert ADA0["mix_in"] + PAIRS == ADA_CHUNKS
ADA_STEPS = (0, 1, 3, 4, 6, 8, 9, 11)
ADA_SUM_STEP = 13
ADA_TAKE_STEP = 15
ADA_OUT_STRIDE = 14
ADA_OUT_SUM = tuple(ADA_OUT_STRIDE * p + 12 for p in range(ADA_PER_OUT))
ADA_UNITS = KD // KU
PRE_SLOTS, PRE_K = 8, 4
SH1, SC1, G1, SH2, SC2, G2, SH3, SC3, G3 = (m * KD for m in range(N_MOD))

V_ADAB = 0
V_C = N_MOD * KD
V_N1, V_N2, V_N3, V_LB0, V_LB1 = V_C + KD, V_C + 2 * KD, V_C + 3 * KD, V_C + 4 * KD, V_C + 4 * KD + HEADS
V_HN = V_C + 5 * KD
V_QN, V_KN, V_SUB = V_HN + 1, V_HN + 2, V_HN + 3
V_END = V_HN + 4
V_ROWS2 = V_END - P

B_HQ, B_HF, B_HI, B_HG, B_DQ, B_DK, B_DV, B_GA, B_GB = 0, 8, 16, 24, 32, 40, 48, 56, 72
MIX_BLOCKS = 88
LEVELS = 8

C_IDENT, C_ONES, C_HALF, C_ROT, C_FREQ = 0, P, 2 * P, 3 * P, 4 * P
C_CAUSAL = 4 * P + 1
C_RESET = C_CAUSAL + 3 * P
C_LEVEL = C_RESET + SEQ
C_END = C_LEVEL + LEVELS * P
MASKED = -1e30


def constants():
    c = np.zeros((P, C_END), np.float32)
    r = np.arange(P)
    c[:, C_IDENT:C_IDENT + P] = np.eye(P)
    c[:, C_ONES:C_ONES + P] = 1.0
    c[:, C_HALF:C_HALF + P] = (r[:, None] // DH) == (r[None, :] // DH)
    for half in range(2):
        for d in range(ROPE_HALF):
            lo, hi = half * DH + d, half * DH + d + ROPE_HALF
            c[hi, C_ROT + lo] = -1.0
            c[lo, C_ROT + hi] = 1.0
            f = np.float32(ROPE_THETA) ** np.float32(-d / ROPE_HALF)
            c[lo, C_FREQ] = c[hi, C_FREQ] = f
    tri = np.where(r[None, :] <= r[:, None], 0.0, MASKED)
    c[:, C_CAUSAL:C_CAUSAL + P] = tri
    c[:, C_CAUSAL + 2 * P:C_CAUSAL + 3 * P] = tri
    c[:, C_RESET:C_RESET + SEQ] = (np.arange(SEQ) % HGRN_CHUNK != 0)[None, :]
    s, t = r[:, None], r[None, :]
    for j in range(LEVELS - 1):
        m = 1 << j
        c[:, C_LEVEL + j * P:C_LEVEL + (j + 1) * P] = (s // (2 * m) == t // (2 * m)) & ((s // m) % 2 == 0) & ((t // m) % 2 == 1)
    c[:, C_LEVEL + (LEVELS - 1) * P:C_END] = s == t
    return c


class Chain:

    def __init__(self, eng, sem, base=0):
        self.eng, self.sem, self.base, self.k = eng, sem, base, 0

    def mark(self, ins):
        self.k += 1
        ins.then_inc(self.sem, 1)

    def wait(self):
        self.eng.wait_ge(self.sem, self.base + self.k)

    def link(self, ins):
        self.mark(ins)
        self.wait()


def build(nc, x, c, positions, ada_w, ada_b, norm1_w, ffn1_w_in, ffn1_w_out, norm2_w, mix_w_in, hgrn_lb,
          hgrn_norm_w, hgrn_w_out, diff_q_norm_w, diff_k_norm_w, diff_lq1, diff_lk1, diff_lq2, diff_lk2,
          diff_subln_w, diff_w_out, mix_w_o, norm3_w, ffn2_w_in, ffn2_w_out, consts, out):
    ds = bass.ds

    def blk(t, i):
        return t[:, ds(i, 1), :].rearrange("p a t -> p (a t)")

    with ExitStack() as ctx:
        def sb(name, shape, dt=F32):
            return ctx.enter_context(nc.sbuf_tensor(name, shape, dt))

        def sem(name):
            return ctx.enter_context(nc.semaphore(name))

        raw = sb("raw", [P, RING, KU, COLS])
        w_hi = sb("w_hi", [P, RING, KU, COLS], F32R)
        w_lo = sb("w_lo", [P, RING, KU, COLS], F32R)
        ada_raw = sb("ada_raw", [P, 2, KU, COLS])
        h = sb("h", [P, KD, SEQ])
        n = sb("n", [P, KD, 2, SEQ], F32R)
        hid = sb("hid", [P, KF, 2, SEQ], F32R)
        tmp = sb("tmp", [P, BLK, SEQ])
        tmp2 = sb("tmp2", [P, BLK, SEQ])
        ada_acc = sb("ada_acc", [P, COLS])
        mods = sb("mods", [P, N_MOD * KD])
        vec = sb("vec", [P, V_END])
        silu_c = sb("silu_c", [P, KD])
        gain = sb("gain", [P, KD])
        gate = sb("gate", [P, KD])
        rstd = sb("rstd", [P, SEQ])
        eps = sb("eps", [P, 1])
        expo = sb("expo", [P, 2 * HEADS + 2])
        bound = sb("bound", [P, 3 * HEADS])
        neg_lam = sb("neg_lam", [P, 1])
        sub_gain = sb("sub_gain", [P, 1])
        row_max = sb("row_max", [P, 4])
        row_sum = sb("row_sum", [P, 4])
        cst = sb("cst", [P, C_FREQ + 1])
        ident, ones, half_ones, rot, freq = (cst[:, a:a + w] for a, w in (
            (C_IDENT, P), (C_ONES, P), (C_HALF, P), (C_ROT, P), (C_FREQ, 1)))

        class Region:
            def __init__(self, host, size):
                self.at = nc.lookup_mloc(host).addr
                self.end = self.at + size

            def take(self, name, shape, dt=F32):
                t = nc.alloc_sbuf_tensor_at(name, [P] + shape, dt, offset=self.at)
                self.at += 4 * int(np.prod(shape))
                assert self.at <= self.end, name
                return t

        before = Region(hid, 8 * KF * SEQ)
        ada_pre = before.take("ada_pre", [PRE_SLOTS, PRE_K, COLS])
        x_in = before.take("x_in", [2, D])
        vec_in = before.take("vec_in", [2, P])
        mixs = Region(hid, 8 * KF * SEQ).take("mixs", [MIX_BLOCKS, SEQ])
        heads = Region(n, 8 * KD * SEQ)
        late = heads.take("late", [C_END - C_CAUSAL])
        causal = late[:, 0:3 * P]
        reset = late[:, C_RESET - C_CAUSAL:C_RESET - C_CAUSAL + SEQ]
        level_mask = late[:, C_LEVEL - C_CAUSAL:C_END - C_CAUSAL].rearrange("p (j t) -> p j t", j=LEVELS)
        X = heads.take("X", [LEVELS, SEQ])
        kk = heads.take("kk", [SEQ])
        bcum = heads.take("bcum", [SEQ])
        v_t = heads.take("v_t", [SEQ])
        v_tok = heads.take("v_tok", [2, P])
        S = heads.take("S", [3, P])
        qk = heads.take("qk", [2, SEQ])
        w_att = heads.take("w_att", [3, P])
        w_key = heads.take("w_key", [3, P])
        cos_t = heads.take("cos_t", [SEQ])
        sin_t = heads.take("sin_t", [SEQ])
        pos = heads.take("pos", [SEQ], I32)
        lvec = heads.take("lvec", [4, DH])
        out_tile = Region(n, 8 * KD * SEQ).take("out_tile", [DJOBS, 2, COLS])
        score = X[:].rearrange("p l t -> p (l t)")[:, 0:2 * 3 * P]

        acc = [ctx.enter_context(nc.psum_tensor(f"acc{i}", [P, BLK, SEQ], F32)) for i in range(2)]
        pm = ctx.enter_context(nc.psum_tensor("pm", [P, 4, COLS], F32))

        raw_landed = [sem(f"raw_landed{i}") for i in range(RING)]
        hi_ready = sem("hi_ready")
        split_ready = sem("split_ready")
        unit_done = sem("unit_done")
        half_free = [sem(f"half_free{i}") for i in range(2)]
        ada_landed = [sem(f"ada_landed{i}") for i in range(2)]
        ada_mac = sem("ada_mac")
        ada_cols = sem("ada_cols")
        ada_taken = sem("ada_taken")
        pre_landed = [sem(f"pre_landed{i}") for i in range(PRE_SLOTS)]
        x_landed, vec_landed, cst_landed, late_landed = (sem(s) for s in ("x_landed", "vec_landed", "cst_landed", "late_landed"))
        vec_turned, vec_ready, silu_ready, eps_ready = (sem(s) for s in ("vec_turned", "vec_ready", "silu_ready", "eps_ready"))
        x_turned, x_taken = sem("x_turned"), sem("x_taken")
        hid_hi, hid_ready = sem("hid_hi"), sem("hid_ready")
        sq_ready, sq_used = sem("sq_ready"), sem("sq_used")
        ss_part, ss_ready, root_ready, rstd_ready, gain_ready, gate_ready = (
            sem(s) for s in ("ss_part", "ss_ready", "root_ready", "rstd_ready", "gain_ready", "gate_ready"))
        t_ready, n_hi, n_ready = sem("t_ready"), sem("n_hi"), sem("n_ready")
        sig_ready, hg_ready, f_ready = sem("sig_ready"), sem("hg_ready"), sem("f_ready")
        expo_ready, expo_done, angle_ready, trig_ready = (sem(s) for s in ("expo_ready", "expo_done", "angle_ready", "trig_ready"))
        dve_step = sem("dve_step")
        act_step = sem("act_step")
        a_logf, a_vt, a_turn, a_vtok, a_b, a_arg, a_exp, a_x, a_sc, a_masked, a_full, a_s, a_o, a_taken = (
            sem(f"a_{s}") for s in ("logf", "vt", "turn", "vtok", "b", "arg", "exp", "x", "sc", "masked", "full", "s", "o", "taken"))
        b_sq, b_ss, b_rstd, b_vt, b_turn, b_vtok, b_norm, b_rot, b_rope, b_sc, b_max, b_exp, b_w, b_wturn, b_wkey, b_o, b_taken = (
            sem(f"b_{s}") for s in ("sq", "ss", "rstd", "vt", "turn", "vtok", "norm", "rot", "rope", "sc", "max", "exp", "w",
                                    "wturn", "wkey", "o", "taken"))
        o_sq, o_ss, o_rstd, o_t, o_hi, o_ready = (sem(f"o_{s}") for s in ("sq", "ss", "rstd", "t", "hi", "ready"))
        mix_a, mix_sum, mix_hi, mix_ready = (sem(f"mix_{s}") for s in ("a", "sum", "hi", "ready"))
        fin_turned, fin_taken, stored = sem("fin_turned"), sem("fin_taken"), sem("stored")

        def units_of(w, k=KU):
            return w[0].rearrange("(a k p) n -> a p k n", p=P, k=k)

        block = ctx.enter_context(nc.Block())

        @block.sync
        def _(sp):
            def rows_of(v):
                return v.rearrange("(r q) -> r q", q=P)

            sp.dma_start(cst[:], consts[:, 0:C_FREQ + 1]).then_inc(cst_landed, 16)
            adab = rows_of(ada_b[0])
            for tile, row, src in ((0, 0, adab[0:P]), (1, 0, adab[P:N_MOD * KD]), (1, V_C - P, rows_of(c[0])),
                                   (1, V_N1 - P, rows_of(norm1_w[0])), (1, V_N2 - P, rows_of(norm2_w[0])),
                                   (1, V_N3 - P, rows_of(norm3_w[0])), (1, V_LB0 - P, rows_of(hgrn_lb[0])),
                                   (1, V_LB1 - P, rows_of(hgrn_lb[1])), (1, V_HN - P, hgrn_norm_w), (1, V_SUB - P, diff_subln_w)):
                sp.dma_start(vec_in[row:row + src.shape[0], tile, :], src).then_inc(vec_landed, 16)
            for row, w in ((V_QN - P, diff_q_norm_w), (V_KN - P, diff_k_norm_w)):
                for s in range(2):
                    sp.dma_start(vec_in[row:row + 1, 1, s * DH:(s + 1) * DH], w).then_inc(vec_landed, 16)

            ada4 = units_of(ada_w, PRE_K)
            for u in range(PRE_SLOTS):
                sp.dma_start(ada_pre[:, u], ada4[u % 4, :, :, u // 4 * COLS:(u // 4 + 1) * COLS]).then_inc(pre_landed[u], 16)
            sp.dma_start(x_in[:], x[0].rearrange("(t p) d -> p t d", p=P)).then_inc(x_landed, 16)
            with sp.Fori(1, ADA_PRE // 2) as i:
                for u in range(PRE_SLOTS):
                    sp.wait_ge(ada_mac, (i - 1) * (PRE_SLOTS * PRE_K) + PRE_K * (u + 1))
                    sp.dma_start(ada_pre[:, u], ada4[u % 4, :, :, ds(i * (2 * COLS) + u // 4 * COLS, COLS)])\
                      .then_inc(pre_landed[u], 16)

            def pair(name, i, units, jobs, started=True):
                for s in range(2 * units):
                    src, col = jobs[s // units]
                    if started or s >= RING:
                        sp.wait_ge(split_ready, UNIT0[name] + i * (2 * units) + s - (RING - 1))
                    sp.dma_start(raw[:, s % RING], src[s % units, :, :, ds(col, COLS)]).then_inc(raw_landed[s % RING], 16)

            in1, out1, mixw, in2, out2 = (units_of(w) for w in (ffn1_w_in, ffn1_w_out, mix_w_in, ffn2_w_in, ffn2_w_out))
            how, dow, mow = (units_of(w) for w in (hgrn_w_out, diff_w_out, mix_w_o))
            pair("ffn1_in", 0, U_IN, ((in1, 0), (in1, D_FF)), started=False)
            with sp.Fori(1, PAIRS) as i:
                pair("ffn1_in", i, U_IN, ((in1, i * COLS), (in1, i * COLS + D_FF)))
            with sp.Fori(0, DJOBS // 2) as i:
                pair("ffn1_out", i, U_OUT, ((out1, i * (2 * COLS)), (out1, i * (2 * COLS) + COLS)))
            with sp.Fori(0, PAIRS) as i:
                pair("mix_in", i, U_IN, ((mixw, i * (2 * COLS)), (mixw, i * (2 * COLS) + COLS)))
            sp.wait_ge(unit_done, UNIT0["heads_out"])
            sp.dma_start(late[:], consts[:, C_CAUSAL:C_END]).then_inc(late_landed, 16)
            sp.dma_start(pos[:], positions[0].partition_broadcast(P)).then_inc(late_landed, 16)
            for k, w in enumerate((diff_lq1, diff_lk1, diff_lq2, diff_lk2)):
                sp.dma_start(lvec[:, k, :], w[0].partition_broadcast(P)).then_inc(late_landed, 16)
            with sp.Fori(0, DJOBS) as i:
                pair("heads_out", i, U_HEAD, ((how, i * COLS), (dow, i * COLS)))
            with sp.Fori(0, DJOBS // 2) as i:
                pair("mix_out", i, U_IN, ((mow, i * (2 * COLS)), (mow, i * (2 * COLS) + COLS)))
            with sp.Fori(0, PAIRS) as i:
                pair("ffn2_in", i, U_IN, ((in2, i * COLS), (in2, i * COLS + D_FF)))
            with sp.Fori(0, DJOBS // 2) as i:
                pair("ffn2_out", i, U_OUT, ((out2, i * (2 * COLS)), (out2, i * (2 * COLS) + COLS)))

            for j in range(DJOBS):
                for t in range(2):
                    sp.wait_ge(fin_taken, 2 * j + t + 1)
                    sp.dma_start(out[0, t * P:(t + 1) * P, j * COLS:(j + 1) * COLS], out_tile[:, j, t, :])\
                      .then_inc(stored, 16)
            sp.wait_ge(stored, 16 * 2 * DJOBS)

        @block.gpsimd
        def _(pool):
            ada2 = units_of(ada_w)
            used = ADA_PRE * KD

            def fetch(a, i, started=True):
                if started:
                    pool.wait_ge(ada_mac, i * KD + (used + KU * (a - 1)))
                pool.dma_start(ada_raw[:, a % 2], ada2[a % ADA_UNITS, :, :, ds((i + ADA_PRE + a // ADA_UNITS) * COLS, COLS)])\
                    .then_inc(ada_landed[a % 2], 16)

            for a in range(2):
                fetch(a, 0, started=False)
            with pool.Fori(0, ADA_CHUNKS - ADA_PRE - 1) as i:
                for a in range(2, ADA_UNITS + 2):
                    fetch(a, i)
            for a in range(2, ADA_UNITS):
                fetch(a, ADA_CHUNKS - ADA_PRE - 1)

        @block.scalar
        def _(act):
            def settled():
                act.wait_ge(eps_ready, 1)

            def split(slot, u, started=True):
                act.wait_ge(raw_landed[slot], 4 * (u - slot) + 16)
                if started:
                    act.wait_ge(unit_done, u - (RING - 1))
                nc.scalar.activation(w_hi[:, slot], raw[:, slot], ACT.Copy).then_inc(hi_ready, 1)

            act.wait_ge(vec_turned, 1)
            nc.scalar.activation(vec[:], pm[:, 0, 0:V_END], ACT.Copy).then_inc(vec_ready, 1)
            act.wait_ge(vec_ready, 1)
            nc.scalar.activation(silu_c[:], vec[:, V_C:V_C + KD], ACT.Silu).then_inc(silu_ready, 1)
            for g in range(KD // 2):
                act.wait_ge(x_turned, g + 1)
                nc.scalar.activation(h[:, 2 * g:2 * g + 2, :], pm[:, 2 + g % 2, :].rearrange("p (c t) -> p c t", c=2),
                                     ACT.Copy).then_inc(x_taken, 1)
            for j in range(DJOBS):
                act.wait_ge(x_taken, 2 * (j + 1))
                if j:
                    act.wait_ge(sq_used, j)
                nc.scalar.activation(tmp[:], h[:, BLK * j:BLK * (j + 1), :], ACT.Square).then_inc(sq_ready, 1)
            for slot in range(RING):
                split(slot, slot, started=False)
            act.wait_ge(eps_ready, 1)

            def normalise(m, shift):
                act.wait_ge(ss_ready, m + 1)
                nc.scalar.activation(rstd[:], rstd[:], ACT.Sqrt, scale=1.0 / D, bias=eps[:]).then_inc(root_ready, 1)
                for k in range(KD):
                    act.wait_ge(t_ready, m * KD + k + 1)
                    nc.scalar.activation(n[:, k, 0, :], tmp[:, k % BLK, :], ACT.Identity,
                                         bias=mods[:, shift + k:shift + k + 1]).then_inc(n_hi, 1)

            def ffn_in(name, ffn):
                with act.Fori(0, PAIRS) as i:
                    for s in range(2 * U_IN):
                        u = UNIT0[name] + i * (2 * U_IN) + s
                        split(s % RING, u + LEAD)
                        if s == U_IN - 1:
                            act.wait_ge(unit_done, u + 1)
                            act.wait_ge(n_ready, (2 * ffn + 1) * KD)
                            nc.scalar.activation(tmp[:], acc[0][:], ACT.Silu).then_inc(half_free[0], 1)
                        if s == 2 * U_IN - 1:
                            act.wait_ge(half_free[1], JOB0[name] // 2 + i + 1)
                            settled()
                            nc.scalar.activation(hid[:, ds(i * BLK, BLK), 0, :], tmp[:], ACT.Copy).then_inc(hid_hi, 1)
                            act.wait_ge(hid_ready, ffn * PAIRS + i + 1)

            def residual_out(name, units, m):
                with act.Fori(0, DJOBS // 2) as i:
                    for s in range(2 * units):
                        split(s % RING, UNIT0[name] + i * (2 * units) + s + LEAD)
                        if s % units == units - 1:
                            b = s // units
                            act.wait_ge(half_free[b], JOB0[name] // 2 + i + 1)
                            act.wait_ge(sq_used, m * DJOBS + 2 * i + b)
                            settled()
                            nc.scalar.activation(tmp[:], h[:, ds(i * (2 * BLK) + b * BLK, BLK), :], ACT.Square)\
                                .then_inc(sq_ready, 1)

            normalise(0, SH1)
            ffn_in("ffn1_in", 0)
            residual_out("ffn1_out", U_OUT, 1)
            normalise(1, SH2)

            with act.Fori(0, PAIRS) as i:
                for s in range(2 * U_IN):
                    u = UNIT0["mix_in"] + i * (2 * U_IN) + s
                    split(s % RING, u + LEAD)
                    if s % U_IN == U_IN - 1:
                        b = s // U_IN
                        act.wait_ge(unit_done, u + 1)
                        settled()
                        nc.scalar.activation(mixs[:, ds(i * (2 * BLK) + b * BLK, BLK), :], acc[b][:], ACT.Copy)\
                            .then_inc(half_free[b], 1)

            act.wait_ge(half_free[1], JOB0["heads_out"] // 2)
            nc.scalar.activation(mixs[:, B_HF:B_HF + HEADS, :], mixs[:, B_HF:B_HF + HEADS, :], ACT.Sigmoid).then_inc(sig_ready, 1)
            nc.scalar.activation(mixs[:, B_GA:B_GA + 2 * KD, :], mixs[:, B_GA:B_GA + 2 * KD, :], ACT.Sigmoid).then_inc(sig_ready, 1)
            nc.scalar.activation(mixs[:, B_HG:B_HG + HEADS, :], mixs[:, B_HG:B_HG + HEADS, :], ACT.Silu).then_inc(hg_ready, 1)
            act.wait_ge(angle_ready, 1)
            nc.scalar.activation(sin_t[:], sin_t[:], ACT.Sin)
            nc.scalar.activation(cos_t[:], cos_t[:], ACT.Sin).then_inc(trig_ready, 1)
            act.wait_ge(expo_ready, 1)
            nc.scalar.activation(expo[:], expo[:], ACT.Exp).then_inc(expo_done, 1)

            act.wait_ge(f_ready, 1)
            with act.Fori(0, HEADS) as i:
                nc.scalar.activation(tmp2[:, 0, :], blk(mixs, i + B_HF), ACT.Ln).then_inc(a_logf, 1)
                nc.scalar.activation(v_t[:], blk(mixs, i + B_HI), ACT.Copy).then_inc(a_vt, 1)
                act.wait_ge(a_turn, i + 1)
                nc.scalar.activation(v_tok[:], pm[:, 3, 0:SEQ].rearrange("p (a v) -> p a v", a=2), ACT.Copy).then_inc(a_vtok, 1)
                act.wait_ge(a_arg, i + 1)
                nc.scalar.activation(X[:], X[:], ACT.Exp).then_inc(a_exp, 1)
                settled()
                act.wait_ge(a_o, i + 1)
                nc.scalar.activation(blk(mixs, i + B_HF), pm[:, 2, SEQ:2 * SEQ], ACT.Copy).then_inc(a_taken, 1)

            with act.Fori(0, HEADS) as i:
                nc.scalar.activation(tmp2[:, 0, :], blk(mixs, i + B_DQ), ACT.Square)
                nc.scalar.activation(tmp2[:, 1, :], blk(mixs, i + B_DK), ACT.Square).then_inc(b_sq, 1)
                nc.scalar.activation(v_t[:], blk(mixs, i + B_DV), ACT.Copy).then_inc(b_vt, 1)
                act.wait_ge(b_ss, i + 1)
                nc.scalar.activation(tmp2[:, 2:4, :], pm[:, 0, :].rearrange("p (a t) -> p a t", a=2), ACT.Ln, scale=1.0 / DH,
                                     bias=eps[:]).then_inc(act_step, 1)
                act.wait_ge(act_step, i + 1)
                nc.scalar.activation(tmp2[:, 0:2, :], tmp2[:, 2:4, :], ACT.Exp, scale=-0.5).then_inc(b_rstd, 1)
                act.wait_ge(b_turn, i + 1)
                nc.scalar.activation(v_tok[:], pm[:, 3, 0:SEQ].rearrange("p (a v) -> p a v", a=2), ACT.Copy).then_inc(b_vtok, 1)
                act.wait_ge(b_max, i + 1)
                for m in range(2):
                    for t in range(2):
                        part = score[:, m * 3 * P + t * P:m * 3 * P + (1 + 2 * t) * P]
                        ins = nc.scalar.activation(part, part, ACT.Exp, bias=row_max[:, 2 * m + t:2 * m + t + 1],
                                                   accum_out=row_sum[:, 2 * m + t:2 * m + t + 1])
                ins.then_inc(b_exp, 1)
                act.wait_ge(b_wturn, i + 1)
                nc.scalar.activation(w_key[:], pm[:, 2, 0:3 * P].rearrange("p (a t) -> p a t", a=3), ACT.Copy).then_inc(b_wkey, 1)
                settled()
                act.wait_ge(b_o, i + 1)
                nc.scalar.activation(blk(mixs, i + B_DQ), pm[:, 3, 0:SEQ], ACT.Copy).then_inc(b_taken, 1)

            act.wait_ge(a_taken, HEADS)
            act.wait_ge(b_taken, HEADS)
            for kind, at in ((0, B_HF), (1, B_DQ)):
                with act.Fori(kind * HEADS, (kind + 1) * HEADS) as i:
                    nc.scalar.activation(tmp2[:, 0, :], blk(mixs, i + (at - kind * HEADS)), ACT.Square).then_inc(o_sq, 1)
                    act.wait_ge(o_ss, i + 1)
                    nc.scalar.activation(tmp2[:, 1, :], pm[:, 2, 0:SEQ], ACT.Ln, scale=1.0 / P, bias=eps[:]).then_inc(act_step, 1)
                    act.wait_ge(act_step, i + (HEADS + 1))
                    nc.scalar.activation(tmp2[:, 2, :], tmp2[:, 1, :], ACT.Exp, scale=-0.5).then_inc(o_rstd, 1)
                    act.wait_ge(o_t, i + 1)
                    settled()
                    nc.scalar.activation(n[:, ds(i, 1), 0, :].rearrange("p a t -> p (a t)"), tmp2[:, 3, :], ACT.Copy).then_inc(o_hi, 1)

            with act.Fori(0, DJOBS) as i:
                for s in range(2 * U_HEAD):
                    split(s % RING, UNIT0["heads_out"] + i * (2 * U_HEAD) + s + LEAD)
                act.wait_ge(mix_sum, i + 1)
                settled()
                nc.scalar.activation(hid[:, ds(i * BLK, BLK), 0, :], tmp[:], ACT.Copy).then_inc(mix_hi, 1)

            act.wait_ge(mix_ready, DJOBS)
            residual_out("mix_out", U_IN, 2)
            normalise(2, SH3)
            ffn_in("ffn2_in", 1)

            for s in range(DJOBS * U_OUT):
                if UNIT0["ffn2_out"] + s + LEAD < UNITS:
                    split(s % RING, UNIT0["ffn2_out"] + s + LEAD)
                if s % U_OUT == U_OUT - 1:
                    j = s // U_OUT
                    for t in range(2):
                        act.wait_ge(fin_turned, 2 * j + t + 1)
                        nc.scalar.activation(out_tile[:, j, t, :], pm[:, 2 * (j % 2) + t, :], ACT.Copy).then_inc(fin_taken, 1)

        @block.tensor
        def _(pe):
            pe.wait_ge(cst_landed, 16)
            pe.wait_ge(vec_landed, 16 * 14)
            nc.tensor.transpose(pm[:, 0, 0:P], vec_in[:, 0, :], ident)
            nc.tensor.transpose(pm[:, 0, P:V_END], vec_in[0:V_ROWS2, 1, :], ident[0:V_ROWS2, 0:V_ROWS2]).then_inc(vec_turned, 1)
            pe.wait_ge(x_landed, 16)
            for g in range(KD // 2):
                if g >= 2:
                    pe.wait_ge(x_taken, g - 1)
                for k in range(2):
                    for t in range(2):
                        ins = nc.tensor.transpose(pm[:, 2 + g % 2, (2 * k + t) * P:(2 * k + t + 1) * P],
                                                  x_in[:, t, (2 * g + k) * P:(2 * g + k + 1) * P], ident)
                ins.then_inc(x_turned, 1)

            def ada_sum(chunk):
                pe.wait_ge(ada_mac, chunk * KD + KD)
                for f in range(BLK):
                    ins = nc.tensor.matmul(pm[:, 0, f:f + 1], ada_acc[:, f * P:(f + 1) * P], ones[:, 0:1], start=True, stop=True)
                ins.then_inc(ada_cols, 1)

            def square_sum(m, i, b):
                pe.wait_ge(sq_ready, m * DJOBS + 2 * i + b + 1)
                for f in range(BLK):
                    ins = nc.tensor.matmul(pm[:, 1, ds(i * SEQ, SEQ)], ones, tmp[:, f, :], start=(b == 0 and f == 0),
                                           stop=(b == 1 and f == BLK - 1))
                ins.then_inc(sq_used, 1)

            for j in range(DJOBS):
                square_sum(0, j // 2, j % 2)
            pe.wait_ge(vec_ready, 1)
            ada_sum(0)
            with pe.Fori(1, ADA_PRE) as i:
                ada_sum(i)

            def unit(slot, u, half, rhs, k0, first, last):
                pe.wait_ge(split_ready, u + 1)
                for k in range(KU):
                    for f in range(BLK):
                        w, o = slice(f * P, (f + 1) * P), acc[half][:, f, :]
                        nc.tensor.matmul(o, w_hi[:, slot, k, w], rhs[:, k0 + k, 0, :], start=(first and k == 0 and f % 2 == 0), stop=False)
                        nc.tensor.matmul(o, w_hi[:, slot, k, w], rhs[:, k0 + k, 1, :], start=False, stop=False)
                        ins = nc.tensor.matmul(o, w_lo[:, slot, k, w], rhs[:, k0 + k, 0, :], start=False,
                                               stop=(last and k == KU - 1 and f % 2 == 1))
                ins.then_inc(unit_done, 1)

            def pair(name, i, units, rhs, ready, after=None, started=True, at=(0, 0)):
                for s in range(2 * units):
                    b, k = divmod(s, units)
                    if k == 0 and started:
                        pe.wait_ge(half_free[b], JOB0[name] // 2 + i)
                    ready(s)
                    unit(s % RING, UNIT0[name] + i * (2 * units) + s, b, rhs, at[b] + KU * k, k == 0, k == units - 1)
                    if after is not None:
                        after(s)

            def normed(m):
                return lambda s: pe.wait_ge(n_ready, m * KD + KU * (s % U_IN + 1))

            def with_ada(name, i):
                return lambda s: ada_sum(ADA0[name] + i) if s == ADA_SUM_STEP else None

            def residual_out(name, units, ready, m, ada):
                with pe.Fori(0, DJOBS // 2) as i:
                    def after(s):
                        if s == units + 2:
                            square_sum(m, i, 0)
                        if s == 2 * units - 1:
                            square_sum(m, i, 1)
                        if ada and s in ADA_OUT_SUM:
                            ada_sum(ADA0[name] + i * ADA_PER_OUT + ADA_OUT_SUM.index(s))
                    pair(name, i, units, hid, ready, after)

            pair("ffn1_in", 0, U_IN, n, normed(0), with_ada("ffn1_in", 0), started=False)
            with pe.Fori(1, PAIRS) as i:
                pair("ffn1_in", i, U_IN, n, normed(0), with_ada("ffn1_in", i))
            residual_out("ffn1_out", U_OUT, lambda s: pe.wait_ge(hid_ready, PAIRS), 1, True)
            with pe.Fori(0, PAIRS) as i:
                pair("mix_in", i, U_IN, n, normed(1), with_ada("mix_in", i))

            with pe.Fori(0, HEADS) as i:
                pe.wait_ge(a_vt, i + 1)
                for g in range(2):
                    ins = nc.tensor.transpose(pm[:, 3, g * P:(g + 1) * P], v_t[:, g * P:(g + 1) * P], ident)
                ins.then_inc(a_turn, 1)
                pe.wait_ge(a_x, i + 1)
                for g in range(2):
                    if g:
                        pe.wait_ge(a_masked, i + 1)
                    for j in range(LEVELS - 1):
                        xg = X[:, j, g * P:(g + 1) * P]
                        nc.tensor.matmul(pm[:, j // 4, j % 4 * P:(j % 4 + 1) * P], xg, xg, start=True, stop=True)
                    nc.tensor.matmul(pm[:, 1, 3 * P:4 * P], kk[:, g * P:(g + 1) * P],
                                     mixs[:, ds(i + B_HQ, 1), g * P:(g + 1) * P].rearrange("p a t -> p (a t)"),
                                     start=True, stop=True).then_inc(a_sc, 1)
                    if g == 0:
                        nc.tensor.matmul(pm[:, 2, 0:P], X[:, LEVELS - 1, 0:P], X[:, LEVELS - 1, P:2 * P], start=True, stop=True)\
                            .then_inc(a_full, 1)
                pe.wait_ge(a_s, i + 1)
                pe.wait_ge(a_vtok, i + 1)
                nc.tensor.matmul(pm[:, 2, SEQ:SEQ + P], v_tok[:, 0, :], S[:, 0, :], start=True, stop=True)
                nc.tensor.matmul(pm[:, 2, SEQ + P:2 * SEQ], v_tok[:, 0, :], S[:, 1, :], start=True, stop=False)
                nc.tensor.matmul(pm[:, 2, SEQ + P:2 * SEQ], v_tok[:, 1, :], S[:, 2, :], start=False, stop=True).then_inc(a_o, 1)
                pe.wait_ge(a_taken, i + 1)

            with pe.Fori(0, HEADS) as i:
                pe.wait_ge(b_sq, i + 1)
                nc.tensor.matmul(pm[:, 0, :], half_ones, tmp2[:, 0:2, :].rearrange("p a t -> p (a t)"), start=True, stop=True)\
                    .then_inc(b_ss, 1)
                pe.wait_ge(b_vt, i + 1)
                for g in range(2):
                    ins = nc.tensor.transpose(pm[:, 3, g * P:(g + 1) * P], v_t[:, g * P:(g + 1) * P], ident)
                ins.then_inc(b_turn, 1)
                pe.wait_ge(b_norm, i + 1)
                nc.tensor.matmul(pm[:, 1, :], rot, qk[:].rearrange("p a t -> p (a t)"), start=True, stop=True).then_inc(b_rot, 1)
                pe.wait_ge(b_rope, i + 1)
                for m in range(2):
                    r = slice(m * DH, (m + 1) * DH)
                    nc.tensor.matmul(pm[:, m, 0:P], qk[r, 0, 0:P], qk[r, 1, 0:P], start=True, stop=True)
                    ins = nc.tensor.matmul(pm[:, m, P:3 * P], qk[r, 0, P:2 * P], qk[r, 1, :], start=True, stop=True)
                ins.then_inc(b_sc, 1)
                pe.wait_ge(b_w, i + 1)
                for g in range(3):
                    ins = nc.tensor.transpose(pm[:, 2, g * P:(g + 1) * P], w_att[:, g, :], ident)
                ins.then_inc(b_wturn, 1)
                pe.wait_ge(b_wkey, i + 1)
                pe.wait_ge(b_vtok, i + 1)
                nc.tensor.matmul(pm[:, 3, 0:P], v_tok[:, 0, :], w_key[:, 0, :], start=True, stop=True)
                nc.tensor.matmul(pm[:, 3, P:SEQ], v_tok[:, 0, :], w_key[:, 1, :], start=True, stop=False)
                nc.tensor.matmul(pm[:, 3, P:SEQ], v_tok[:, 1, :], w_key[:, 2, :], start=False, stop=True).then_inc(b_o, 1)
                pe.wait_ge(b_taken, i + 1)

            with pe.Fori(0, 2 * HEADS) as i:
                pe.wait_ge(o_sq, i + 1)
                nc.tensor.matmul(pm[:, 2, 0:SEQ], ones, tmp2[:, 0, :], start=True, stop=True).then_inc(o_ss, 1)

            with pe.Fori(0, DJOBS) as i:
                pair("heads_out", i, U_HEAD, n, lambda s: pe.wait_ge(o_ready, 2 * HEADS), at=(0, HEADS))
            residual_out("mix_out", U_IN, lambda s: pe.wait_ge(mix_ready, DJOBS), 2, False)
            with pe.Fori(0, PAIRS) as i:
                pair("ffn2_in", i, U_IN, n, normed(2))

            with pe.Fori(0, DJOBS // 2) as i:
                def turn(b):
                    pe.wait_ge(half_free[b], JOB0["ffn2_out"] // 2 + i + 1)
                    for t in range(2):
                        for f in range(BLK):
                            ins = nc.tensor.transpose(pm[:, 2 * b + t, f * P:(f + 1) * P], tmp2[:, f, t * P:(t + 1) * P], ident)
                        ins.then_inc(fin_turned, 1)

                def after(s):
                    if s == U_OUT + 2:
                        turn(0)
                    if s == 2 * U_OUT - 1:
                        turn(1)
                        pe.wait_ge(fin_taken, 4 * i + 4)
                pair("ffn2_out", i, U_OUT, hid, lambda s: pe.wait_ge(hid_ready, 2 * PAIRS), after)

        @block.vector
        def _(dve):
            own = Chain(dve, dve_step)

            def split(slot, u):
                dve.wait_ge(hi_ready, u + 1)
                nc.vector.tensor_tensor(w_lo[:, slot], raw[:, slot], w_hi[:, slot], ALU.subtract).then_inc(split_ready, 1)

            def ada_add(w, k, chunk):
                if k == 0:
                    nc.vector.tensor_scalar(ada_acc[:], w, silu_c[:, 0:1], None, ALU.mult).then_inc(ada_mac, 1)
                else:
                    dve.wait_ge(ada_mac, chunk * KD + k)
                    nc.vector.scalar_tensor_tensor(out=ada_acc[:], in0=w, scalar=silu_c[:, k:k + 1], in1=ada_acc[:],
                                                   op0=ALU.mult, op1=ALU.add).then_inc(ada_mac, 1)

            def ada_take(chunk):
                dve.wait_ge(ada_cols, chunk + 1)
                nc.vector.tensor_tensor(mods[:, ds(chunk * BLK, BLK)], pm[:, 0, 0:BLK], vec[:, ds(chunk * BLK + V_ADAB, BLK)],
                                        ALU.add).then_inc(ada_taken, 1)

            def ada_unit(a, name, i):
                g = (ADA0[name] - ADA_PRE + i) * ADA_UNITS + a
                dve.wait_ge(ada_landed[a % 2], 8 * (g - a % 2) + 16)
                for k in range(KU):
                    ada_add(ada_raw[:, a % 2, k, :], KU * a + k, ADA0[name] + i)

            nc.vector.memset(eps[:], EPS).then_inc(eps_ready, 1)
            dve.wait_ge(silu_ready, 1)
            with dve.Fori(0, ADA_PRE // 2) as i:
                for s in range(PRE_SLOTS):
                    chunk, a = 2 * i + s // 4, s % 4
                    dve.wait_ge(pre_landed[s], 16 * i + 16)
                    for k in range(PRE_K):
                        ada_add(ada_pre[:, s, k, :], PRE_K * a + k, chunk)
                    if a == 3:
                        ada_take(chunk)
            for u in range(RING):
                split(u, u)

            def normalise(m, weight, scale):
                dve.wait_ge(ada_taken, (scale + KD) // BLK)
                nc.vector.scalar_tensor_tensor(out=gain[:], in0=mods[:, scale:scale + KD], scalar=1.0,
                                               in1=vec[:, weight:weight + KD], op0=ALU.add, op1=ALU.mult).then_inc(gain_ready, 1)
                dve.wait_ge(sq_used, (m + 1) * DJOBS)
                nc.vector.tensor_copy(rstd[:], pm[:, 1, 0:SEQ]).then_inc(ss_part, 1)
                dve.wait_ge(ss_part, m + 1)
                nc.vector.tensor_tensor(rstd[:], rstd[:], pm[:, 1, SEQ:2 * SEQ], ALU.add).then_inc(ss_ready, 1)
                dve.wait_ge(root_ready, m + 1)
                nc.vector.reciprocal(rstd[:], rstd[:]).then_inc(rstd_ready, 1)
                dve.wait_ge(rstd_ready, m + 1)
                dve.wait_ge(gain_ready, m + 1)
                shift = scale - KD

                def lo(k):
                    dve.wait_ge(n_hi, m * KD + k + 1)
                    nc.vector.scalar_tensor_tensor(out=n[:, k, 1, :], in0=tmp[:, k % BLK, :], scalar=mods[:, shift + k:shift + k + 1],
                                                   in1=n[:, k, 0, :], op0=ALU.add, op1=ALU.subtract).then_inc(n_ready, 1)

                for k in range(KD):
                    if k >= BLK:
                        dve.wait_ge(n_ready, m * KD + k - BLK + 1)
                    nc.vector.scalar_tensor_tensor(out=tmp[:, k % BLK, :], in0=h[:, k, :], scalar=gain[:, k:k + 1],
                                                   in1=rstd[:], op0=ALU.mult, op1=ALU.mult).then_inc(t_ready, 1)
                    if k >= 2:
                        lo(k - 2)
                lo(KD - 2)
                lo(KD - 1)

            def ffn_in(name, ffn, ada):
                with dve.Fori(0, PAIRS) as i:
                    for s in range(2 * U_IN):
                        u = UNIT0[name] + i * (2 * U_IN) + s
                        split(s % RING, u + LEAD)
                        if s == 2 * U_IN - 1:
                            dve.wait_ge(unit_done, u + 1)
                            dve.wait_ge(half_free[0], JOB0[name] // 2 + i + 1)
                            nc.vector.tensor_tensor(tmp[:], acc[1][:], tmp[:], ALU.mult).then_inc(half_free[1], 1)
                            dve.wait_ge(hid_hi, ffn * PAIRS + i + 1)
                            nc.vector.tensor_tensor(hid[:, ds(i * BLK, BLK), 1, :], tmp[:], hid[:, ds(i * BLK, BLK), 0, :],
                                                    ALU.subtract).then_inc(hid_ready, 1)
                        if ada and s in ADA_STEPS:
                            ada_unit(ADA_STEPS.index(s), name, i)
                        if ada and s == ADA_TAKE_STEP:
                            ada_take(ADA0[name] + i)

            def add_residual(dst, block0, b, factor, at):
                for f in range(BLK):
                    ins = nc.vector.scalar_tensor_tensor(out=dst(f), in0=acc[b][:, f, :], scalar=factor[:, ds(block0 + at + f, 1)],
                                                         in1=blk(h, block0 + f), op0=ALU.mult, op1=ALU.add)
                return ins

            def half_gate(g, count):
                dve.wait_ge(ada_taken, (g + KD) // BLK)
                nc.vector.tensor_scalar(gate[:], mods[:, g:g + KD], 0.5, None, ALU.mult).then_inc(gate_ready, 1)
                dve.wait_ge(gate_ready, count)

            def residual_out(name, units, factor, at, ada):
                with dve.Fori(0, DJOBS // 2) as i:
                    for s in range(2 * units):
                        u = UNIT0[name] + i * (2 * units) + s
                        split(s % RING, u + LEAD)
                        if s % units == units - 1:
                            b = s // units
                            dve.wait_ge(unit_done, u + 1)
                            block0 = i * (2 * BLK) + b * BLK
                            add_residual(lambda f: blk(h, block0 + f), block0, b, factor, at).then_inc(half_free[b], 1)
                        if ada:
                            part, step = divmod(s, ADA_OUT_STRIDE)
                            if part < ADA_PER_OUT and step in ADA_STEPS:
                                ada_unit(ADA_STEPS.index(step), name, i * ADA_PER_OUT + part)
                            if s - 1 in ADA_OUT_SUM:
                                ada_take(ADA0[name] + i * ADA_PER_OUT + ADA_OUT_SUM.index(s - 1))

            normalise(0, V_N1, SC1)
            ffn_in("ffn1_in", 0, True)
            half_gate(G1, 1)
            residual_out("ffn1_out", U_OUT, gate, 0, True)
            normalise(1, V_N2, SC2)
            with dve.Fori(0, PAIRS) as i:
                for s in range(2 * U_IN):
                    split(s % RING, UNIT0["mix_in"] + i * (2 * U_IN) + s + LEAD)
                    if s in ADA_STEPS:
                        ada_unit(ADA_STEPS.index(s), "mix_in", i)
                    if s == ADA_TAKE_STEP:
                        ada_take(ADA0["mix_in"] + i)

            dve.wait_ge(unit_done, UNIT0["heads_out"])
            dve.wait_ge(late_landed, 16 * 6)
            turn = (6.28125, 0.0019350051879882812)
            turn += (2 * np.pi - sum(turn),)
            big = 1.5 * 2.0 ** 23
            own.link(nc.vector.tensor_copy(bcum[:], pos[:]))
            own.link(nc.vector.tensor_scalar(bcum[:], bcum[:], freq, None, ALU.mult))
            for quarter, dst in ((0.0, sin_t), (0.25, cos_t)):
                own.link(nc.vector.tensor_scalar(kk[:], bcum[:], 1.0 / (2 * np.pi), quarter, ALU.mult, ALU.add))
                own.link(nc.vector.tensor_scalar(kk[:], kk[:], big, None, ALU.add))
                own.link(nc.vector.tensor_scalar(kk[:], kk[:], big, None, ALU.subtract))
                src = bcum
                for part in turn:
                    own.link(nc.vector.scalar_tensor_tensor(out=dst[:], in0=kk[:], scalar=-float(part), in1=src[:], op0=ALU.mult, op1=ALU.add))
                    src = dst
                own.link(nc.vector.tensor_scalar(dst[:], dst[:], quarter * 2 * np.pi, None, ALU.add))
                ins = nc.vector.tensor_scalar(dst[:], dst[:], 3.1415925, -3.1415925, ALU.min, ALU.max)
            ins.then_inc(angle_ready, 1)

            lb, one_less, div = (bound[:, k * HEADS:(k + 1) * HEADS] for k in range(3))
            rows = [vec[:, a:a + HEADS] for a in (V_LB0, V_LB1)]
            own.link(nc.vector.tensor_tensor(div, rows[0], rows[1], ALU.max))
            for k in range(2):
                nc.vector.tensor_tensor(expo[:, k * HEADS:(k + 1) * HEADS], rows[k], div, ALU.subtract)
            for k in range(2):
                ins = nc.vector.tensor_tensor_reduce(out=v_t[:, k * DH:(k + 1) * DH], in0=lvec[:, 2 * k, :], in1=lvec[:, 2 * k + 1, :],
                                                     scale=1.0, scalar=0.0, op0=ALU.mult, op1=ALU.add,
                                                     accum_out=expo[:, 2 * HEADS + k:2 * HEADS + k + 1])
            ins.then_inc(expo_ready, 1)
            own.link(nc.vector.tensor_scalar(sub_gain[:], vec[:, V_SUB:V_SUB + 1], 1.0 - LAM_INIT, None, ALU.mult))
            dve.wait_ge(expo_done, 1)
            own.link(nc.vector.tensor_tensor(div, expo[:, 0:HEADS], expo[:, HEADS:2 * HEADS], ALU.add))
            own.link(nc.vector.reciprocal(div, div))
            own.link(nc.vector.tensor_tensor(lb, expo[:, 0:HEADS], div, ALU.mult))
            own.link(nc.vector.tensor_scalar(one_less, lb, -1.0, 1.0, ALU.mult, ALU.add))
            own.link(nc.vector.tensor_tensor(neg_lam[:], expo[:, 2 * HEADS + 1:], expo[:, 2 * HEADS:2 * HEADS + 1], ALU.subtract))
            own.link(nc.vector.tensor_scalar(neg_lam[:], neg_lam[:], LAM_INIT, None, ALU.subtract))
            dve.wait_ge(sig_ready, 1)
            for k in range(HEADS):
                ins = nc.vector.tensor_scalar(mixs[:, B_HF + k, :], mixs[:, B_HF + k, :], one_less[:, k:k + 1], lb[:, k:k + 1],
                                              ALU.mult, ALU.add)
            ins.then_inc(f_ready, 1)
            dve.wait_ge(f_ready, 1)

            steps = 5
            masked = tmp[:].rearrange("p a t -> p (a t)").rearrange("p (j t) -> p j t", j=LEVELS)
            C = HGRN_CHUNK
            with dve.Fori(0, HEADS) as i:
                head = Chain(dve, dve_step, i * steps + own.k)
                nc.vector.tensor_scalar(kk[:], blk(mixs, i + B_HF), -1.0, 1.0, ALU.mult, ALU.add)
                dve.wait_ge(a_logf, i + 1)
                nc.vector.tensor_tensor_scan(bcum[:], reset, tmp2[:, 0, :], 0.0, ALU.mult, ALU.add).then_inc(a_b, 1)
                dve.wait_ge(a_b, i + 1)
                for j in range(6):
                    m = 1 << j
                    bv = bcum[:].rearrange("p (n two m) -> p n two m", two=2, m=m)
                    xv = X[:, j, :].rearrange("p (n two m) -> p n two m", two=2, m=m)
                    r = bv[:, :, 0, m - 1:m].to_broadcast([P, SEQ // (2 * m), m])
                    nc.vector.tensor_tensor(xv[:, :, 0, :], r, bv[:, :, 0, :], ALU.subtract)
                    nc.vector.tensor_tensor(xv[:, :, 1, :], bv[:, :, 1, :], r, ALU.subtract)
                b_at = [bcum[:, C * q:C * (q + 1)] for q in range(4)]
                last = [bcum[:, C * (q + 1) - 1:C * (q + 1)] for q in range(4)]
                for q in (0, 2):
                    nc.vector.tensor_scalar(X[:, 6, C * q:C * (q + 1)], b_at[q], -1.0, last[q], ALU.mult, ALU.add)
                    nc.vector.tensor_copy(X[:, 6, C * (q + 1):C * (q + 2)], b_at[q + 1])
                nc.vector.tensor_scalar(X[:, 7, C:2 * C], b_at[1], -1.0, last[1], ALU.mult, ALU.add)
                nc.vector.tensor_copy(X[:, 7, 2 * C:3 * C], b_at[2])
                head.link(nc.vector.tensor_scalar(X[:, 7, 3 * C:4 * C], b_at[3], last[2], None, ALU.add))
                head.link(nc.vector.tensor_scalar(X[:, 7, 0:C], X[:, 6, 0:C], last[1], None, ALU.add))
                nc.vector.tensor_scalar(X[:], X[:], 0.0, None, ALU.min).then_inc(a_arg, 1)
                dve.wait_ge(a_exp, i + 1)
                for j in range(LEVELS):
                    m = 1 << j
                    xv, kv = (t.rearrange("p (n two m) -> p n two m", two=2, m=m) for t in (X[:, j, :], kk[:]))
                    qv = mixs[:, ds(i + B_HQ, 1), :].rearrange("p a (n two m) -> p (a n) two m", two=2, m=m)
                    nc.vector.tensor_tensor(xv[:, :, 0, :], xv[:, :, 0, :], kv[:, :, 0, :], ALU.mult)
                    ins = nc.vector.tensor_tensor(xv[:, :, 1, :], xv[:, :, 1, :], qv[:, :, 1, :], ALU.mult)
                ins.then_inc(a_x, 1)
                for g in range(2):
                    dve.wait_ge(a_sc, 2 * i + g + 1)
                    ins = nc.vector.tensor_tensor(masked, pm[:, 0:2, :].rearrange("p b (j t) -> p (b j) t", t=P), level_mask, ALU.mult)
                    if g == 0:
                        ins.then_inc(a_masked, 1)
                        dve.wait_ge(a_masked, i + 1)
                        head.link(nc.vector.tensor_reduce(S[:, 0, :], masked.rearrange("p j t -> p t j"), AX_X, ALU.add))
                        dve.wait_ge(a_full, i + 1)
                        nc.vector.tensor_copy(S[:, 1, :], pm[:, 2, 0:P])
                    else:
                        head.link(ins)
                        nc.vector.tensor_reduce(S[:, 2, :], masked.rearrange("p j t -> p t j"), AX_X, ALU.add).then_inc(a_s, 1)
                head.link(nc.vector.memset(row_max[:], 0.0))
            assert head.k == steps
            first = own.k + HEADS * steps

            steps = 8
            dve.wait_ge(trig_ready, 1)
            with dve.Fori(0, HEADS) as i:
                head = Chain(dve, dve_step, i * steps + first)
                dve.wait_ge(b_rstd, i + 1)
                for w in range(2):
                    ins = nc.vector.scalar_tensor_tensor(out=qk[:, w, :], in0=blk(mixs, i + (B_DQ, B_DK)[w]),
                                                         scalar=vec[:, V_QN + w:V_QN + w + 1], in1=tmp2[:, w, :], op0=ALU.mult, op1=ALU.mult)
                ins.then_inc(b_norm, 1)
                dve.wait_ge(b_norm, i + 1)
                dve.wait_ge(b_rot, i + 1)
                for w in range(2):
                    nc.vector.tensor_tensor(tmp[:, w, :], qk[:, w, :], cos_t[:], ALU.mult)
                    ins = nc.vector.tensor_tensor(tmp[:, 2 + w, :], pm[:, 1, w * SEQ:(w + 1) * SEQ], sin_t[:], ALU.mult)
                head.link(ins)
                nc.vector.tensor_tensor(qk[:], tmp[:, 0:2, :], tmp[:, 2:4, :], ALU.add).then_inc(b_rope, 1)
                dve.wait_ge(b_sc, i + 1)
                for m in range(2):
                    ins = nc.vector.scalar_tensor_tensor(out=score[:, m * 3 * P:(m + 1) * 3 * P], in0=pm[:, m, 0:3 * P], scalar=DH ** -0.5,
                                                         in1=causal, op0=ALU.mult, op1=ALU.add)
                head.link(ins)
                sv = score.rearrange("p (m k) -> p m k", m=2)
                mv = row_max[:].rearrange("p (m t) -> p m t", m=2)
                nc.vector.tensor_reduce(mv[:, :, 0], sv[:, :, 0:P], AX_X, ALU.max)
                head.link(nc.vector.tensor_reduce(mv[:, :, 1], sv[:, :, P:3 * P], AX_X, ALU.max))
                nc.vector.tensor_scalar(row_max[:], row_max[:], -1.0, None, ALU.mult).then_inc(b_max, 1)
                dve.wait_ge(b_exp, i + 1)
                head.link(nc.vector.reciprocal(row_sum[:], row_sum[:]))
                head.link(nc.vector.tensor_scalar(row_sum[:, 2:4], row_sum[:, 2:4], neg_lam[:], None, ALU.mult))
                flat = tmp[:].rearrange("p a t -> p (a t)")
                for t in range(2):
                    a, b = t * P, (1 + 2 * t) * P
                    ins = nc.vector.tensor_scalar(flat[:, a:b], score[:, 3 * P + a:3 * P + b], row_sum[:, 2 + t:3 + t], None, ALU.mult)
                head.link(ins)
                wv = w_att[:].rearrange("p a t -> p (a t)")
                for t in range(2):
                    a, b = t * P, (1 + 2 * t) * P
                    ins = nc.vector.scalar_tensor_tensor(out=wv[:, a:b], in0=score[:, a:b], scalar=row_sum[:, t:t + 1], in1=flat[:, a:b],
                                                         op0=ALU.mult, op1=ALU.add)
                ins.then_inc(b_w, 1)
                head.link(nc.vector.memset(rstd[:, 0:1], 0.0))
                head.link(nc.vector.memset(rstd[:, 0:1], 0.0))
            assert head.k == steps
            first += HEADS * steps

            for kind, at in ((0, B_HF), (1, B_DQ)):
                w_o = sub_gain[:] if kind else vec[:, V_HN:V_HN + 1]
                if kind == 0:
                    dve.wait_ge(hg_ready, 1)
                with dve.Fori(kind * HEADS, (kind + 1) * HEADS) as i:
                    dve.wait_ge(o_rstd, i + 1)
                    ins = nc.vector.scalar_tensor_tensor(out=tmp2[:, 3, :], in0=blk(mixs, i + (at - kind * HEADS)), scalar=w_o,
                                                         in1=tmp2[:, 2, :], op0=ALU.mult, op1=ALU.mult)
                    if kind == 0:
                        ins.then_inc(dve_step, 1)
                        dve.wait_ge(dve_step, i + (first + 1))
                        ins = nc.vector.tensor_tensor(tmp2[:, 3, :], tmp2[:, 3, :], blk(mixs, i + B_HG), ALU.mult)
                    ins.then_inc(o_t, 1)
                    dve.wait_ge(o_hi, i + 1)
                    nc.vector.tensor_tensor(n[:, ds(i, 1), 1, :].rearrange("p a t -> p (a t)"), tmp2[:, 3, :],
                                            n[:, ds(i, 1), 0, :].rearrange("p a t -> p (a t)"), ALU.subtract).then_inc(o_ready, 1)
                    dve.wait_ge(o_ready, i + 1)

            dve.wait_ge(sig_ready, 2)
            with dve.Fori(0, DJOBS) as i:
                for s in range(2 * U_HEAD):
                    u = UNIT0["heads_out"] + i * (2 * U_HEAD) + s
                    split(s % RING, u + LEAD)
                    if s == U_HEAD - 1:
                        dve.wait_ge(unit_done, u + 1)
                        nc.vector.tensor_tensor(tmp2[:], acc[0][:], mixs[:, ds(i * BLK + B_GA, BLK), :], ALU.mult).then_inc(half_free[0], 1)
                    if s == 2 * U_HEAD - 1:
                        dve.wait_ge(unit_done, u + 1)
                        nc.vector.tensor_tensor(tmp[:], acc[1][:], mixs[:, ds(i * BLK + B_GB, BLK), :], ALU.mult).then_inc(half_free[1], 1)
                        dve.wait_ge(half_free[0], JOB0["heads_out"] // 2 + i + 1)
                        dve.wait_ge(half_free[1], JOB0["heads_out"] // 2 + i + 1)
                        nc.vector.tensor_tensor(tmp[:], tmp[:], tmp2[:], ALU.add).then_inc(mix_sum, 1)
                dve.wait_ge(mix_hi, i + 1)
                dve.wait_ge(mix_sum, i + 1)
                nc.vector.tensor_tensor(hid[:, ds(i * BLK, BLK), 1, :], tmp[:], hid[:, ds(i * BLK, BLK), 0, :], ALU.subtract)\
                    .then_inc(mix_ready, 1)
                dve.wait_ge(mix_ready, i + 1)

            residual_out("mix_out", U_IN, mods, G2, False)
            normalise(2, V_N3, SC3)
            ffn_in("ffn2_in", 1, False)
            half_gate(G3, 2)
            for s in range(DJOBS * U_OUT):
                u = UNIT0["ffn2_out"] + s
                if u + LEAD < UNITS:
                    split(s % RING, u + LEAD)
                if s % U_OUT == U_OUT - 1:
                    j = s // U_OUT
                    dve.wait_ge(unit_done, u + 1)
                    if j:
                        dve.wait_ge(fin_turned, 2 * j)
                    add_residual(lambda f: tmp2[:, f, :], j * BLK, j % 2, gate, 0).then_inc(half_free[j % 2], 1)


_INS = ["x", "c", "positions", "ada_w", "ada_b", "norm1_w", "ffn1_w_in", "ffn1_w_out", "norm2_w", "mix_w_in", "hgrn_lb",
        "hgrn_norm_w", "hgrn_w_out", "diff_q_norm_w", "diff_k_norm_w", "diff_lq1", "diff_lk1", "diff_lq2", "diff_lk2",
        "diff_subln_w", "diff_w_out", "mix_w_o", "norm3_w", "ffn2_w_in", "ffn2_w_out"]


def kernel(**inputs):
    import concourse.bacc as bacc
    from concourse.bass_utils import run_bass_kernel_spmd

    nc = bacc.Bacc("TRN2", target_bir_lowering=False, num_devices=1)
    arrays, args = {}, []
    for name in _INS + ["consts"]:
        a = constants() if name == "consts" else np.ascontiguousarray(inputs[name])
        arrays[f"in_{name}"] = a
        args.append(nc.dram_tensor(f"in_{name}", a.shape, mybir.dt.from_np(a.dtype), kind="ExternalInput").ap())
    args.append(nc.dram_tensor("out_0", (1, SEQ, D), F32, kind="ExternalOutput").ap())
    build(nc, *args)
    r = run_bass_kernel_spmd(nc, [arrays], core_ids=[0])
    return r.results[0]["out_0"]
```

```python
from contextlib import ExitStack

import numpy as np

import concourse.bass as bass
from concourse import mybir

F32 = mybir.dt.float32
F32R = mybir.dt.float32r
I32 = mybir.dt.int32
ALU = mybir.AluOpType
ACT = mybir.ActivationFunctionType
AX_X = mybir.AxisListType.X

P = 128
D = 2048
SEQ = 256
D_FF = 5632
MIX_WIDTH = 11264
HEADS = 8
HGRN_CHUNK = 64
DH = 64
ROPE_HALF = 8
ROPE_THETA = 500000.0
EPS = 1e-6
LAM_INIT = 0.2

KD = D // P
KF = D_FF // P
COLS = 512
BLK = COLS // P
KU = 2
RING = 4
LEAD = RING

U_IN = KD // KU
U_OUT = KF // KU
U_HEAD = HEADS // KU
PAIRS = D_FF // COLS
DJOBS = D // COLS
assert MIX_WIDTH == 2 * PAIRS * COLS

UNIT0, JOB0 = {}, {}
_u = _j = 0
for _name, _jobs, _units in (("ffn1_in", 2 * PAIRS, U_IN), ("ffn1_out", DJOBS, U_OUT), ("mix_in", 2 * PAIRS, U_IN),
                             ("heads_out", 2 * DJOBS, U_HEAD), ("mix_out", DJOBS, U_IN),
                             ("ffn2_in", 2 * PAIRS, U_IN), ("ffn2_out", DJOBS, U_OUT)):
    UNIT0[_name], JOB0[_name] = _u, _j
    _u += _jobs * _units
    _j += _jobs
UNITS = _u

N_MOD = 9
ADA_CHUNKS = N_MOD * D // COLS
ADA_PRE = 2 * D // COLS
ADA_PER_OUT = 3
ADA0 = {"ffn1_in": ADA_PRE, "ffn1_out": ADA_PRE + PAIRS, "mix_in": ADA_PRE + PAIRS + 2 * ADA_PER_OUT}
assert ADA0["mix_in"] + PAIRS == ADA_CHUNKS
ADA_STEPS = (0, 1, 3, 4, 6, 7, 9, 10)
ADA_SUM_STEP = 13
ADA_TAKE_STEP = 14
HEADS_ADA_STEPS, HEADS_SUM_STEP = (0, 2, 3, 4, 7, 9, 11, 13), 14
ADA_OUT_STRIDE = 14
ADA_OUT_SUM = tuple(ADA_OUT_STRIDE * p + 12 for p in range(ADA_PER_OUT))
ADA_UNITS = KD // KU
PRE_SLOTS, PRE_K = 8, 4
SH1, SC1, G1, SH2, SC2, G2, SH3, SC3, G3 = (m * KD for m in range(N_MOD))

V_ADAB = 0
V_C = N_MOD * KD
V_N1, V_N2, V_N3, V_LB0, V_LB1 = V_C + KD, V_C + 2 * KD, V_C + 3 * KD, V_C + 4 * KD, V_C + 4 * KD + HEADS
V_HN = V_C + 5 * KD
V_QN, V_KN, V_SUB = V_HN + 1, V_HN + 2, V_HN + 3
V_END = V_HN + 4
V_ROWS2 = V_END - P

B_HQ, B_HF, B_HI, B_HG, B_DQ, B_DK, B_DV, B_GA = 0, 8, 16, 24, 32, 40, 48, 56
MIX_BLOCKS = 72
B_GB, GB_STRIDE = B_HQ, 16
HGRN_PAIR = 3
DIFF_PAIR = 7
GB_PAIR = 9
assert PAIRS - HGRN_PAIR == HEADS and 2 * (PAIRS - DIFF_PAIR) == HEADS
LEVELS = 8

C_IDENT, C_ONES, C_HALF, C_ROT, C_FREQ = 0, P, 2 * P, 3 * P, 4 * P
C_CAUSAL = 4 * P + 1
C_RESET = C_CAUSAL + 3 * P
C_LEVEL = C_RESET + SEQ
C_END = C_LEVEL + LEVELS * P
MASKED = -1e30


def constants():
    c = np.zeros((P, C_END), np.float32)
    r = np.arange(P)
    c[:, C_IDENT:C_IDENT + P] = np.eye(P)
    c[:, C_ONES:C_ONES + P] = 1.0
    c[:, C_HALF:C_HALF + P] = (r[:, None] // DH) == (r[None, :] // DH)
    for half in range(2):
        for d in range(ROPE_HALF):
            lo, hi = half * DH + d, half * DH + d + ROPE_HALF
            c[hi, C_ROT + lo] = -1.0
            c[lo, C_ROT + hi] = 1.0
            f = np.float32(ROPE_THETA) ** np.float32(-d / ROPE_HALF)
            c[lo, C_FREQ] = c[hi, C_FREQ] = f
    tri = np.where(r[None, :] <= r[:, None], 0.0, MASKED)
    c[:, C_CAUSAL:C_CAUSAL + P] = tri
    c[:, C_CAUSAL + 2 * P:C_CAUSAL + 3 * P] = tri
    c[:, C_RESET:C_RESET + SEQ] = (np.arange(SEQ) % HGRN_CHUNK != 0)[None, :]
    s, t = r[:, None], r[None, :]
    for j in range(LEVELS - 1):
        m = 1 << j
        c[:, C_LEVEL + j * P:C_LEVEL + (j + 1) * P] = (s // (2 * m) == t // (2 * m)) & ((s // m) % 2 == 0) & ((t // m) % 2 == 1)
    c[:, C_LEVEL + (LEVELS - 1) * P:C_END] = s == t
    return c


class Chain:

    def __init__(self, eng, sem, base=0):
        self.eng, self.sem, self.base, self.k = eng, sem, base, 0

    def mark(self, ins):
        self.k += 1
        ins.then_inc(self.sem, 1)

    def wait(self):
        self.eng.wait_ge(self.sem, self.base + self.k)

    def link(self, ins):
        self.mark(ins)
        self.wait()


def build(nc, x, c, positions, ada_w, ada_b, norm1_w, ffn1_w_in, ffn1_w_out, norm2_w, mix_w_in, hgrn_lb,
          hgrn_norm_w, hgrn_w_out, diff_q_norm_w, diff_k_norm_w, diff_lq1, diff_lk1, diff_lq2, diff_lk2,
          diff_subln_w, diff_w_out, mix_w_o, norm3_w, ffn2_w_in, ffn2_w_out, consts, out):
    ds = bass.ds

    def blk(t, i):
        return t[:, ds(i, 1), :].rearrange("p a t -> p (a t)")

    with ExitStack() as ctx:
        def sb(name, shape, dt=F32):
            return ctx.enter_context(nc.sbuf_tensor(name, shape, dt))

        def sem(name):
            return ctx.enter_context(nc.semaphore(name))

        raw = sb("raw", [P, RING, KU, COLS])
        w_hi = sb("w_hi", [P, RING, KU, COLS], F32R)
        w_lo = sb("w_lo", [P, RING, KU, COLS], F32R)
        ada_raw = sb("ada_raw", [P, 2, KU, COLS])
        h = sb("h", [P, KD, SEQ])
        n = sb("n", [P, KD, 2, SEQ], F32R)
        hid = sb("hid", [P, KF, 2, SEQ], F32R)
        tmp = sb("tmp", [P, BLK, SEQ])
        tmp2 = sb("tmp2", [P, BLK, SEQ])
        ada_acc = sb("ada_acc", [P, COLS])
        mods = sb("mods", [P, N_MOD * KD])
        vec = sb("vec", [P, V_END])
        silu_c = sb("silu_c", [P, KD])
        gain = sb("gain", [P, KD])
        gate = sb("gate", [P, KD])
        rstd = sb("rstd", [P, SEQ])
        eps = sb("eps", [P, 1])
        expo = sb("expo", [P, 2 * HEADS + 2])
        bound = sb("bound", [P, 3 * HEADS])
        neg_lam = sb("neg_lam", [P, 1])
        sub_gain = sb("sub_gain", [P, 1])
        row_max = sb("row_max", [P, 8])
        row_sum = sb("row_sum", [P, 8])
        cst = sb("cst", [P, C_FREQ + 1])
        ident, ones, half_ones, rot, freq = (cst[:, a:a + w] for a, w in (
            (C_IDENT, P), (C_ONES, P), (C_HALF, P), (C_ROT, P), (C_FREQ, 1)))

        class Region:
            def __init__(self, host, size):
                self.at = nc.lookup_mloc(host).addr
                self.end = self.at + size

            def take(self, name, shape, dt=F32):
                t = nc.alloc_sbuf_tensor_at(name, [P] + shape, dt, offset=self.at)
                self.at += 4 * int(np.prod(shape))
                assert self.at <= self.end, name
                return t

        before = Region(hid, 8 * KF * SEQ)
        ada_pre = before.take("ada_pre", [PRE_SLOTS, PRE_K, COLS])
        x_in = before.take("x_in", [2, D])
        vec_in = before.take("vec_in", [2, P])
        lvec = before.take("lvec", [4, DH])
        l_prod = before.take("l_prod", [2, DH])
        beside = Region(hid, 8 * KF * SEQ)
        mixs = beside.take("mixs", [MIX_BLOCKS, SEQ])
        score = beside.take("score", [2, 2, 3 * P])
        qk = beside.take("qk", [4, SEQ])
        v_tok2 = beside.take("v_tok2", [4, P])
        trig = beside.take("trig", [2, SEQ])
        causal = beside.take("causal", [3 * P])
        S_full = beside.take("S_full", [P])
        in_score = Region(score, 4 * 4 * 3 * P)
        v_2 = in_score.take("v_2", [2, SEQ])
        sq_k = in_score.take("sq_k", [2, SEQ])
        w_key = nc.alloc_sbuf_tensor_at("w_key", [P, 2, 3, P], F32, offset=nc.lookup_mloc(qk).addr)
        in_h = Region(h, 4 * KD * SEQ)
        X = in_h.take("X", [LEVELS, SEQ])
        masked = in_h.take("masked", [LEVELS, P])
        level_mask = in_h.take("level_mask", [LEVELS, P])
        in_masked = Region(masked, 4 * LEVELS * P)
        v_t = in_masked.take("v_t", [SEQ])
        o_sq = in_masked.take("o_sq", [SEQ])
        turns = Region(qk, 4 * 4 * SEQ)
        angle = turns.take("angle", [SEQ])
        whole = turns.take("whole", [2, SEQ])
        pos = turns.take("pos", [SEQ], I32)
        pre_acc = (ada_acc[:], tmp2[:, 0:2, :].rearrange("p a t -> p (a t)"))
        rt = tmp[:]
        kk, bcum, reset = (tmp2[:, k, :] for k in range(3))
        v_tok = tmp2[:, 3, :].rearrange("p (a v) -> p a v", a=2)
        logf = nc.alloc_sbuf_tensor_at("logf", [P, SEQ], F32, offset=nc.lookup_mloc(rstd).addr)
        S = (rstd[:, 0:P], S_full[:], rstd[:, P:2 * P])
        out_tile = Region(n, 8 * KD * SEQ).take("out_tile", [DJOBS, 2, COLS])

        acc = [ctx.enter_context(nc.psum_tensor(f"acc{i}", [P, BLK, SEQ], F32)) for i in range(2)]
        pm = ctx.enter_context(nc.psum_tensor("pm", [P, 4, COLS], F32))

        raw_landed = [sem(f"raw_landed{i}") for i in range(RING)]
        hi_ready = sem("hi_ready")
        split_ready = sem("split_ready")
        unit_done = sem("unit_done")
        half_free = [sem(f"half_free{i}") for i in range(2)]
        ada_landed = [sem(f"ada_landed{i}") for i in range(2)]
        ada_mac = sem("ada_mac")
        ada_cols = sem("ada_cols")
        ada_taken = sem("ada_taken")
        pre_landed = [sem(f"pre_landed{i}") for i in range(PRE_SLOTS)]
        x_landed, vec_landed, cst_landed, late_landed = (sem(s) for s in ("x_landed", "vec_landed", "cst_landed", "late_landed"))
        lam_landed, h_stored, h_back = sem("lam_landed"), sem("h_stored"), sem("h_back")
        vec_turned, vec_ready, silu_ready, eps_ready = (sem(s) for s in ("vec_turned", "vec_ready", "silu_ready", "eps_ready"))
        x_turned, x_taken = sem("x_turned"), sem("x_taken")
        hid_hi, hid_ready = sem("hid_hi"), sem("hid_ready")
        sq_ready, sq_used = sem("sq_ready"), sem("sq_used")
        ss_part, ss_ready, root_ready, rstd_ready, gain_ready, gate_ready = (
            sem(s) for s in ("ss_part", "ss_ready", "root_ready", "rstd_ready", "gain_ready", "gate_ready"))
        t_ready, n_hi, n_ready = sem("t_ready"), sem("n_hi"), sem("n_ready")
        sig_ready, hg_ready, f_ready = sem("sig_ready"), sem("hg_ready"), sem("f_ready")
        expo_ready, expo_done, angle_ready, trig_ready = (sem(s) for s in ("expo_ready", "expo_done", "angle_ready", "trig_ready"))
        dve_step = sem("dve_step")
        act_step = sem("act_step")
        a_logf, a_vt, a_turn, a_vtok, a_b, a_arg, a_exp, a_x, a_sc, a_masked, a_s, a_o, a_taken, a_ss, a_rstd, a_normed, a_done = (
            sem(f"a_{s}") for s in ("logf", "vt", "turn", "vtok", "b", "arg", "exp", "x", "sc", "masked", "s", "o", "taken",
                                    "ss", "rstd", "normed", "done"))
        b_sq, b_ss, b_rstd, b_vt, b_turn, b_vtok, b_norm, b_rot, b_rope, b_sc, b_masked, b_max, b_exp, b_w = (
            sem(f"b_{s}") for s in ("sq", "ss", "rstd", "vt", "turn", "vtok", "norm", "rot", "rope", "sc", "masked", "max", "exp", "w"))
        b_wturn, b_wkey, b_o, b_osq, b_taken, b_oss, b_orstd, b_done = (
            sem(f"b_{s}") for s in ("wturn", "wkey", "o", "osq", "taken", "oss", "orstd", "done"))
        y_hi, y_ready = sem("y_hi"), sem("y_ready")
        mix_a, mix_sum, mix_hi, mix_ready = (sem(f"mix_{s}") for s in ("a", "sum", "hi", "ready"))
        fin_turned, fin_taken, stored = sem("fin_turned"), sem("fin_taken"), sem("stored")

        h_store = nc.dram_tensor("h_store", (P, KD * SEQ), F32, kind="Internal").ap()

        def units_of(w, k=KU):
            return w[0].rearrange("(a k p) n -> a p k n", p=P, k=k)

        block = ctx.enter_context(nc.Block())

        @block.sync
        def _(sp):
            def rows_of(v):
                return v.rearrange("(r q) -> r q", q=P)

            sp.dma_start(cst[:], consts[:, 0:C_FREQ + 1]).then_inc(cst_landed, 16)
            adab = rows_of(ada_b[0])
            for tile, row, src in ((0, 0, adab[0:P]), (1, 0, adab[P:N_MOD * KD]), (1, V_C - P, rows_of(c[0])),
                                   (1, V_N1 - P, rows_of(norm1_w[0])), (1, V_N2 - P, rows_of(norm2_w[0])),
                                   (1, V_N3 - P, rows_of(norm3_w[0])), (1, V_LB0 - P, rows_of(hgrn_lb[0])),
                                   (1, V_LB1 - P, rows_of(hgrn_lb[1])), (1, V_HN - P, hgrn_norm_w), (1, V_SUB - P, diff_subln_w)):
                sp.dma_start(vec_in[row:row + src.shape[0], tile, :], src).then_inc(vec_landed, 16)
            for row, w in ((V_QN - P, diff_q_norm_w), (V_KN - P, diff_k_norm_w)):
                for s in range(2):
                    sp.dma_start(vec_in[row:row + 1, 1, s * DH:(s + 1) * DH], w).then_inc(vec_landed, 16)

            for k, w in enumerate((diff_lq1, diff_lk1, diff_lq2, diff_lk2)):
                sp.dma_start(lvec[:, k, :], w[0].partition_broadcast(P)).then_inc(lam_landed, 16)

            ada4 = units_of(ada_w, PRE_K)
            for u in range(PRE_SLOTS):
                sp.dma_start(ada_pre[:, u], ada4[u // 2, :, :, u % 2 * D:u % 2 * D + COLS]).then_inc(pre_landed[u], 16)
            sp.dma_start(x_in[:], x[0].rearrange("(t p) d -> p t d", p=P)).then_inc(x_landed, 16)
            with sp.Fori(1, ADA_PRE // 2) as i:
                for u in range(PRE_SLOTS):
                    sp.wait_ge(ada_mac, (i - 1) * (PRE_SLOTS * PRE_K) + (2 * (PRE_K * (u // 2 + 1) - 1) + u % 2 + 1))
                    sp.dma_start(ada_pre[:, u], ada4[u // 2, :, :, ds(i * COLS + u % 2 * D, COLS)])\
                      .then_inc(pre_landed[u], 16)

            def pair(name, i, units, jobs, started=True):
                for s in range(2 * units):
                    src, col = jobs[s // units]
                    if started or s >= RING:
                        sp.wait_ge(split_ready, UNIT0[name] + i * (2 * units) + s - (RING - 1))
                    sp.dma_start(raw[:, s % RING], src[s % units, :, :, ds(col, COLS)]).then_inc(raw_landed[s % RING], 16)

            in1, out1, mixw, in2, out2 = (units_of(w) for w in (ffn1_w_in, ffn1_w_out, mix_w_in, ffn2_w_in, ffn2_w_out))
            how, dow, mow = (units_of(w) for w in (hgrn_w_out, diff_w_out, mix_w_o))
            pair("ffn1_in", 0, U_IN, ((in1, 0), (in1, D_FF)), started=False)
            with sp.Fori(1, PAIRS) as i:
                pair("ffn1_in", i, U_IN, ((in1, i * COLS), (in1, i * COLS + D_FF)))
            with sp.Fori(0, DJOBS // 2) as i:
                pair("ffn1_out", i, U_OUT, ((out1, i * (2 * COLS)), (out1, i * (2 * COLS) + COLS)))
            with sp.Fori(0, HGRN_PAIR) as i:
                pair("mix_in", i, U_IN, ((mixw, i * (2 * COLS)), (mixw, i * (2 * COLS) + COLS)))
            sp.wait_ge(h_stored, 16)
            for dst, src in ((level_mask[:], consts[:, C_LEVEL:C_END].rearrange("p (j t) -> p j t", t=P)),
                             (causal[:], consts[:, C_CAUSAL:C_RESET]), (reset, consts[:, C_RESET:C_LEVEL]),
                             (pos[:], positions[0].partition_broadcast(P))):
                sp.dma_start(dst, src).then_inc(late_landed, 16)
            with sp.Fori(HGRN_PAIR, PAIRS) as i:
                pair("mix_in", i, U_IN, ((mixw, i * (2 * COLS)), (mixw, i * (2 * COLS) + COLS)))
            with sp.Fori(0, DJOBS) as i:
                pair("heads_out", i, U_HEAD, ((how, i * COLS), (dow, i * COLS)))
            with sp.Fori(0, DJOBS // 2) as i:
                pair("mix_out", i, U_IN, ((mow, i * (2 * COLS)), (mow, i * (2 * COLS) + COLS)))
            with sp.Fori(0, PAIRS) as i:
                pair("ffn2_in", i, U_IN, ((in2, i * COLS), (in2, i * COLS + D_FF)))
            with sp.Fori(0, DJOBS // 2) as i:
                pair("ffn2_out", i, U_OUT, ((out2, i * (2 * COLS)), (out2, i * (2 * COLS) + COLS)))

            for j in range(DJOBS):
                for t in range(2):
                    sp.wait_ge(fin_taken, 2 * j + t + 1)
                    sp.dma_start(out[0, t * P:(t + 1) * P, j * COLS:(j + 1) * COLS], out_tile[:, j, t, :])\
                      .then_inc(stored, 16)
            sp.wait_ge(stored, 16 * 2 * DJOBS)

        @block.gpsimd
        def _(pool):
            ada2 = units_of(ada_w)
            used = ADA_PRE * KD

            def fetch(a, i, started=True):
                if started:
                    pool.wait_ge(ada_mac, i * KD + (used + KU * (a - 1)))
                pool.dma_start(ada_raw[:, a % 2], ada2[a % ADA_UNITS, :, :, ds((i + ADA_PRE + a // ADA_UNITS) * COLS, COLS)])\
                    .then_inc(ada_landed[a % 2], 16)

            for a in range(2):
                fetch(a, 0, started=False)
            with pool.Fori(0, ADA_CHUNKS - ADA_PRE - 1) as i:
                for a in range(2, ADA_UNITS + 2):
                    fetch(a, i)
            for a in range(2, ADA_UNITS):
                fetch(a, ADA_CHUNKS - ADA_PRE - 1)

        @block.scalar
        def _(act):
            def settled():
                act.wait_ge(eps_ready, 1)

            def split(slot, u, started=True):
                act.wait_ge(raw_landed[slot], 4 * (u - slot) + 16)
                if started:
                    act.wait_ge(unit_done, u - (RING - 1))
                nc.scalar.activation(w_hi[:, slot], raw[:, slot], ACT.Copy).then_inc(hi_ready, 1)

            act.wait_ge(vec_turned, 1)
            nc.scalar.activation(vec[:], pm[:, 0, 0:V_END], ACT.Copy).then_inc(vec_ready, 1)
            act.wait_ge(vec_ready, 1)
            nc.scalar.activation(silu_c[:], vec[:, V_C:V_C + KD], ACT.Silu).then_inc(silu_ready, 1)
            act.wait_ge(expo_ready, 1)
            nc.scalar.activation(expo[:], expo[:], ACT.Exp).then_inc(expo_done, 1)
            for g in range(KD // 2):
                act.wait_ge(x_turned, g + 1)
                nc.scalar.activation(h[:, 2 * g:2 * g + 2, :], pm[:, 2 + g % 2, :].rearrange("p (c t) -> p c t", c=2),
                                     ACT.Copy).then_inc(x_taken, 1)
            for j in range(DJOBS):
                act.wait_ge(x_taken, 2 * (j + 1))
                if j:
                    act.wait_ge(sq_used, j)
                nc.scalar.activation(tmp[:], h[:, BLK * j:BLK * (j + 1), :], ACT.Square).then_inc(sq_ready, 1)
            for slot in range(RING):
                split(slot, slot, started=False)
            act.wait_ge(eps_ready, 1)

            def normalise(m, shift):
                act.wait_ge(ss_ready, m + 1)
                nc.scalar.activation(rstd[:], rstd[:], ACT.Sqrt, scale=1.0 / D, bias=eps[:]).then_inc(root_ready, 1)
                for k in range(KD):
                    act.wait_ge(t_ready, m * KD + k + 1)
                    nc.scalar.activation(n[:, k, 0, :], tmp[:, k % BLK, :], ACT.Identity,
                                         bias=mods[:, shift + k:shift + k + 1]).then_inc(n_hi, 1)

            def ffn_in(name, ffn):
                with act.Fori(0, PAIRS) as i:
                    for s in range(2 * U_IN):
                        u = UNIT0[name] + i * (2 * U_IN) + s
                        split(s % RING, u + LEAD)
                        if s == U_IN - 1:
                            act.wait_ge(unit_done, u + 1)
                            act.wait_ge(n_ready, (2 * ffn + 1) * KD)
                            nc.scalar.activation(tmp[:], acc[0][:], ACT.Silu).then_inc(half_free[0], 1)
                        if s == 2 * U_IN - 1:
                            act.wait_ge(half_free[1], JOB0[name] // 2 + i + 1)
                            settled()
                            nc.scalar.activation(hid[:, ds(i * BLK, BLK), 0, :], tmp[:], ACT.Copy).then_inc(hid_hi, 1)
                            act.wait_ge(hid_ready, ffn * PAIRS + i + 1)

            def residual_out(name, units, m):
                with act.Fori(0, DJOBS // 2) as i:
                    for s in range(2 * units):
                        split(s % RING, UNIT0[name] + i * (2 * units) + s + LEAD)
                        if s % units == units - 1:
                            b = s // units
                            act.wait_ge(half_free[b], JOB0[name] // 2 + i + 1)
                            act.wait_ge(sq_used, m * DJOBS + 2 * i + b)
                            settled()
                            nc.scalar.activation(tmp[:], h[:, ds(i * (2 * BLK) + b * BLK, BLK), :], ACT.Square)\
                                .then_inc(sq_ready, 1)

            normalise(0, SH1)
            ffn_in("ffn1_in", 0)
            residual_out("ffn1_out", U_OUT, 1)
            normalise(1, SH2)

            act.wait_ge(t_ready, 2 * KD)
            act.dma_start(h_store, h[:].rearrange("p k t -> p (k t)")).then_inc(h_stored, 16)

            def hgrn(s, i, own):
                if s == 0:
                    nc.scalar.activation(logf[:], blk(mixs, i + B_HF), ACT.Ln).then_inc(a_logf, 1)
                    nc.scalar.activation(v_t[:], blk(mixs, i + B_HI), ACT.Copy).then_inc(a_vt, 1)
                if s == 2:
                    act.wait_ge(a_turn, i + 1)
                    nc.scalar.activation(v_tok, pm[:, 0, 0:SEQ].rearrange("p (a v) -> p a v", a=2), ACT.Copy).then_inc(a_vtok, 1)
                if s == 4:
                    act.wait_ge(a_arg, i + 1)
                    nc.scalar.activation(X[:], X[:], ACT.Exp).then_inc(a_exp, 1)
                if s == 12:
                    act.wait_ge(a_o, i + 1)
                    nc.scalar.activation(o_sq[:], acc[0][:, 2, :], ACT.Square)
                    nc.scalar.activation(blk(mixs, i + B_HF), acc[0][:, 2, :], ACT.Copy).then_inc(a_taken, 1)

            def diff(s, i, own):
                if s == 1:
                    nc.scalar.activation(rt[:, 0:2, :], mixs[:, ds(2 * i + B_DQ, 2), :], ACT.Square)
                    nc.scalar.activation(sq_k[:], mixs[:, ds(2 * i + B_DK, 2), :], ACT.Square).then_inc(b_sq, 1)
                    nc.scalar.activation(v_2[:], mixs[:, ds(2 * i + B_DV, 2), :], ACT.Copy).then_inc(b_vt, 1)
                if s == 2:
                    act.wait_ge(b_ss, i + 1)
                    act.wait_ge(a_b, i + (DIFF_PAIR - HGRN_PAIR + 1))
                    own.link(nc.scalar.activation(rt, pm[:, 2:4, :].rearrange("p b (a t) -> p (b a) t", t=SEQ), ACT.Ln, scale=1.0 / DH, bias=eps[:]))
                    nc.scalar.activation(rt, rt, ACT.Exp, scale=-0.5).then_inc(b_rstd, 1)
                if s == 4:
                    act.wait_ge(b_turn, i + 1)
                    nc.scalar.activation(v_tok2[:], pm[:, 2, :].rearrange("p (a v) -> p a v", v=P), ACT.Copy).then_inc(b_vtok, 1)
                if s == 11:
                    act.wait_ge(b_max, i + 1)
                    for hm in range(4):
                        for t in range(2):
                            part = score[:, hm // 2, hm % 2, t * P:(1 + 2 * t) * P]
                            ins = nc.scalar.activation(part, part, ACT.Exp, bias=row_max[:, 2 * hm + t:2 * hm + t + 1],
                                                       accum_out=row_sum[:, 2 * hm + t:2 * hm + t + 1])
                    ins.then_inc(b_exp, 1)
                if s == 14:
                    act.wait_ge(b_wturn, i + 1)
                    nc.scalar.activation(w_key[:], pm[:, 2:4, 0:3 * P].rearrange("p b (g t) -> p b g t", t=P), ACT.Copy).then_inc(b_wkey, 1)
                if s == 15:
                    act.wait_ge(b_o, i + 1)
                    o = pm[:, 2, :].rearrange("p (a t) -> p a t", a=2)
                    nc.scalar.activation(rt[:, 0:2, :], o, ACT.Square).then_inc(b_osq, 1)
                    nc.scalar.activation(mixs[:, ds(2 * i + B_DK, 2), :], o, ACT.Copy).then_inc(b_taken, 1)

            def output_roots(i, diff, own):
                act.wait_ge(a_ss, i - (HGRN_PAIR - 1))
                ins = nc.scalar.activation(o_sq[:], pm[:, 1, 0:SEQ], ACT.Ln, scale=1.0 / P, bias=eps[:])
                if diff:
                    own.mark(ins)
                    act.wait_ge(b_oss, i - (DIFF_PAIR - 1))
                    ins = nc.scalar.activation(rt[:, 2:4, :], pm[:, 3, :].rearrange("p (a t) -> p a t", a=2), ACT.Ln, scale=1.0 / P, bias=eps[:])
                own.link(ins)
                nc.scalar.activation(o_sq[:], o_sq[:], ACT.Exp, scale=-0.5).then_inc(a_rstd, 1)
                if diff:
                    nc.scalar.activation(rt[:, 2:4, :], rt[:, 2:4, :], ACT.Exp, scale=-0.5).then_inc(b_orstd, 1)

            def mix_pairs(first, end, done):
                links = (first >= HGRN_PAIR) + 2 * (first >= DIFF_PAIR)
                with act.Fori(first, end) as i:
                    own = Chain(act, act_step, (i - first) * links + done)
                    for s in range(2 * U_IN):
                        u = UNIT0["mix_in"] + i * (2 * U_IN) + s
                        split(s % RING, u + LEAD)
                        if s % U_IN == U_IN - 1:
                            b = s // U_IN
                            if first == GB_PAIR:
                                place = i * (2 * GB_STRIDE) + (b * GB_STRIDE + B_GB - 2 * GB_STRIDE * GB_PAIR)
                            else:
                                place = i * (2 * BLK) + b * BLK
                            act.wait_ge(unit_done, u + 1)
                            settled()
                            nc.scalar.activation(mixs[:, ds(place, BLK), :], acc[b][:], ACT.Copy)                                .then_inc(half_free[b], 1)
                        if first >= HGRN_PAIR:
                            hgrn(s, i - HGRN_PAIR, own)
                        if first >= DIFF_PAIR:
                            diff(s, i - DIFF_PAIR, own)
                    if first >= HGRN_PAIR:
                        output_roots(i, first >= DIFF_PAIR, own)
                    assert own.k == links
                return done + (end - first) * links

            done = mix_pairs(0, HGRN_PAIR, 0)
            act.wait_ge(half_free[1], JOB0["mix_in"] // 2 + HGRN_PAIR)
            nc.scalar.activation(mixs[:, B_HF:B_HF + HEADS, :], mixs[:, B_HF:B_HF + HEADS, :], ACT.Sigmoid).then_inc(sig_ready, 1)
            act.wait_ge(f_ready, 1)
            done = mix_pairs(HGRN_PAIR, DIFF_PAIR, done)
            act.wait_ge(angle_ready, 1)
            nc.scalar.activation(trig[:], trig[:], ACT.Sin).then_inc(trig_ready, 1)
            nc.scalar.activation(mixs[:, B_HG:B_HG + HEADS, :], mixs[:, B_HG:B_HG + HEADS, :], ACT.Silu).then_inc(hg_ready, 1)
            done = mix_pairs(DIFF_PAIR, GB_PAIR, done)
            mix_pairs(GB_PAIR, PAIRS, done)

            act.wait_ge(a_done, PAIRS - DIFF_PAIR)
            for g, at in enumerate((B_HF, B_HF + BLK, B_DK, B_DK + BLK)):
                if g == 2:
                    act.wait_ge(b_done, HEADS // 2)
                nc.scalar.activation(n[:, g * BLK:(g + 1) * BLK, 0, :], mixs[:, at:at + BLK, :], ACT.Copy).then_inc(y_hi, 1)
            act.dma_start(h[:].rearrange("p k t -> p (k t)"), h_store).then_inc(h_back, 16)

            with act.Fori(0, DJOBS) as i:
                for s in range(2 * U_HEAD):
                    split(s % RING, UNIT0["heads_out"] + i * (2 * U_HEAD) + s + LEAD)
                    if s == 0:
                        for gate_of, stride in ((B_GA, BLK), (B_GB, GB_STRIDE)):
                            g = mixs[:, ds(i * stride + gate_of, BLK), :]
                            nc.scalar.activation(g, g, ACT.Sigmoid).then_inc(sig_ready, 1)
                act.wait_ge(mix_sum, i + 1)
                settled()
                nc.scalar.activation(hid[:, ds(i * BLK, BLK), 0, :], tmp[:], ACT.Copy).then_inc(mix_hi, 1)

            act.wait_ge(mix_ready, DJOBS)
            residual_out("mix_out", U_IN, 2)
            normalise(2, SH3)
            ffn_in("ffn2_in", 1)

            for s in range(DJOBS * U_OUT):
                if UNIT0["ffn2_out"] + s + LEAD < UNITS:
                    split(s % RING, UNIT0["ffn2_out"] + s + LEAD)
                if s % U_OUT == U_OUT - 1:
                    j = s // U_OUT
                    for t in range(2):
                        act.wait_ge(fin_turned, 2 * j + t + 1)
                        nc.scalar.activation(out_tile[:, j, t, :], pm[:, 2 * (j % 2) + t, :], ACT.Copy).then_inc(fin_taken, 1)

        @block.tensor
        def _(pe):
            pe.wait_ge(cst_landed, 16)
            pe.wait_ge(vec_landed, 16 * 14)
            nc.tensor.transpose(pm[:, 0, 0:P], vec_in[:, 0, :], ident)
            nc.tensor.transpose(pm[:, 0, P:V_END], vec_in[0:V_ROWS2, 1, :], ident[0:V_ROWS2, 0:V_ROWS2]).then_inc(vec_turned, 1)
            pe.wait_ge(x_landed, 16)
            for g in range(KD // 2):
                if g >= 2:
                    pe.wait_ge(x_taken, g - 1)
                for k in range(2):
                    for t in range(2):
                        ins = nc.tensor.transpose(pm[:, 2 + g % 2, (2 * k + t) * P:(2 * k + t + 1) * P],
                                                  x_in[:, t, (2 * g + k) * P:(2 * g + k + 1) * P], ident)
                ins.then_inc(x_turned, 1)

            def ada_sum(added, total=ada_acc[:], at=0):
                pe.wait_ge(ada_mac, added)
                for f in range(BLK):
                    ins = nc.tensor.matmul(pm[:, 0, at + f:at + f + 1], total[:, f * P:(f + 1) * P], ones[:, 0:1], start=True, stop=True)
                ins.then_inc(ada_cols, 1)

            def square_sum(m, i, b):
                pe.wait_ge(sq_ready, m * DJOBS + 2 * i + b + 1)
                for f in range(BLK):
                    ins = nc.tensor.matmul(pm[:, 1, ds(i * SEQ, SEQ)], ones, tmp[:, f, :], start=(b == 0 and f == 0),
                                           stop=(b == 1 and f == BLK - 1))
                ins.then_inc(sq_used, 1)

            for j in range(DJOBS):
                square_sum(0, j // 2, j % 2)
            pe.wait_ge(vec_ready, 1)
            with pe.Fori(0, ADA_PRE // 2) as i:
                for k in range(2):
                    ada_sum(i * (2 * KD) + (2 * KD - 1 + k), pre_acc[k], k * BLK)
                pe.wait_ge(ada_taken, 2 * i + 2)

            def unit(slot, u, half, rhs, k0, first, last):
                pe.wait_ge(split_ready, u + 1)
                for k in range(KU):
                    for f in range(BLK):
                        w, o = slice(f * P, (f + 1) * P), acc[half][:, f, :]
                        nc.tensor.matmul(o, w_hi[:, slot, k, w], rhs[:, k0 + k, 0, :], start=(first and k == 0 and f % 2 == 0), stop=False)
                        nc.tensor.matmul(o, w_hi[:, slot, k, w], rhs[:, k0 + k, 1, :], start=False, stop=False)
                        ins = nc.tensor.matmul(o, w_lo[:, slot, k, w], rhs[:, k0 + k, 0, :], start=False,
                                               stop=(last and k == KU - 1 and f % 2 == 1))
                ins.then_inc(unit_done, 1)

            def pair(name, i, units, rhs, ready, after=None, started=True, at=(0, 0)):
                for s in range(2 * units):
                    b, k = divmod(s, units)
                    if k == 0 and started:
                        pe.wait_ge(half_free[b], JOB0[name] // 2 + i)
                    ready(s)
                    unit(s % RING, UNIT0[name] + i * (2 * units) + s, b, rhs, at[b] + KU * k, k == 0, k == units - 1)
                    if after is not None:
                        after(s)

            def normed(m):
                return lambda s: pe.wait_ge(n_ready, m * KD + KU * (s % U_IN + 1))

            def with_ada(name, i):
                return lambda s: ada_sum(i * KD + (ADA0[name] + 1) * KD) if s == ADA_SUM_STEP else None

            def residual_out(name, units, ready, m, ada):
                with pe.Fori(0, DJOBS // 2) as i:
                    def after(s):
                        if s == units + 2:
                            square_sum(m, i, 0)
                        if s == 2 * units - 1:
                            square_sum(m, i, 1)
                        if ada and s in ADA_OUT_SUM:
                            ada_sum(i * (ADA_PER_OUT * KD) + (ADA0[name] + ADA_OUT_SUM.index(s) + 1) * KD)
                    pair(name, i, units, hid, ready, after)

            pair("ffn1_in", 0, U_IN, n, normed(0), with_ada("ffn1_in", 0), started=False)
            with pe.Fori(1, PAIRS) as i:
                pair("ffn1_in", i, U_IN, n, normed(0), with_ada("ffn1_in", i))
            residual_out("ffn1_out", U_OUT, lambda s: pe.wait_ge(hid_ready, PAIRS), 1, True)
            with pe.Fori(0, HGRN_PAIR) as i:
                pair("mix_in", i, U_IN, n, normed(1), with_ada("mix_in", i))

            def hgrn(s, i):
                if s == 2:
                    pe.wait_ge(ada_taken, i + (ADA0["mix_in"] + HGRN_PAIR))
                    pe.wait_ge(a_vt, i + 1)
                    for g in range(2):
                        ins = nc.tensor.transpose(pm[:, 0, g * P:(g + 1) * P], v_t[:, g * P:(g + 1) * P], ident)
                    ins.then_inc(a_turn, 1)
                if s in (8, 9):
                    g = s - 8
                    if g:
                        pe.wait_ge(a_masked, 2 * i + 1)
                        pe.wait_ge(half_free[0], i + (JOB0["mix_in"] // 2 + HGRN_PAIR + 1))
                        nc.tensor.matmul(acc[0][:, 0, 0:P], X[:, LEVELS - 1, 0:P], X[:, LEVELS - 1, P:2 * P], start=True, stop=True)
                    else:
                        pe.wait_ge(a_vtok, i + 1)
                        pe.wait_ge(a_x, i + 1)
                    for j in range(LEVELS - 1):
                        xg = X[:, j, g * P:(g + 1) * P]
                        nc.tensor.matmul(pm[:, j // 4, j % 4 * P:(j % 4 + 1) * P], xg, xg, start=True, stop=True)
                    nc.tensor.matmul(pm[:, 1, 3 * P:4 * P], kk[:, g * P:(g + 1) * P],
                                     mixs[:, ds(i + B_HQ, 1), g * P:(g + 1) * P].rearrange("p a t -> p (a t)"),
                                     start=True, stop=True).then_inc(a_sc, 1)
                if s == 12:
                    pe.wait_ge(a_s, i + 1)
                    nc.tensor.matmul(acc[0][:, 2, 0:P], v_tok[:, 0, :], S[0], start=True, stop=True)
                    nc.tensor.matmul(acc[0][:, 2, P:SEQ], v_tok[:, 0, :], S[1], start=True, stop=False)
                    nc.tensor.matmul(acc[0][:, 2, P:SEQ], v_tok[:, 1, :], S[2], start=False, stop=True).then_inc(a_o, 1)
                if s == 13:
                    pe.wait_ge(a_taken, i + 1)
                    nc.tensor.matmul(pm[:, 1, 0:SEQ], ones, o_sq[:], start=True, stop=True).then_inc(a_ss, 1)

            def diff(s, i):
                if s == 2:
                    pe.wait_ge(b_sq, i + 1)
                    for w in range(2):
                        ins = nc.tensor.matmul(pm[:, 2 + w, :], half_ones, (rt[:, 0:2, :], sq_k)[w].rearrange("p a t -> p (a t)"),
                                               start=True, stop=True)
                    ins.then_inc(b_ss, 1)
                if s == 4:
                    pe.wait_ge(b_vt, i + 1)
                    pe.wait_ge(b_rstd, i + 1)
                    for k in range(4):
                        ins = nc.tensor.transpose(pm[:, 2, k * P:(k + 1) * P], v_2[:, k // 2, k % 2 * P:(k % 2 + 1) * P], ident)
                    ins.then_inc(b_turn, 1)
                if s == 6:
                    pe.wait_ge(b_vtok, i + 1)
                    pe.wait_ge(b_norm, i + 1)
                    for w in range(2):
                        ins = nc.tensor.matmul(pm[:, 2 + w, :], rot, qk[:, 2 * w:2 * w + 2, :].rearrange("p a t -> p (a t)"), start=True, stop=True)
                    ins.then_inc(b_rot, 1)
                if s in (9, 10):
                    a = s - 9
                    if a:
                        pe.wait_ge(b_masked, 2 * i + 1)
                    else:
                        pe.wait_ge(b_rope, i + 1)
                    for m in range(2):
                        r = slice(m * DH, (m + 1) * DH)
                        nc.tensor.matmul(pm[:, 2 + m, 0:P], qk[r, a, 0:P], qk[r, 2 + a, 0:P], start=True, stop=True)
                        ins = nc.tensor.matmul(pm[:, 2 + m, P:3 * P], qk[r, a, P:2 * P], qk[r, 2 + a, :], start=True, stop=True)
                    ins.then_inc(b_sc, 1)
                if s == 14:
                    pe.wait_ge(b_w, i + 1)
                    for a in range(2):
                        for g in range(3):
                            ins = nc.tensor.transpose(pm[:, 2 + a, g * P:(g + 1) * P], score[:, a, 0, g * P:(g + 1) * P], ident)
                    ins.then_inc(b_wturn, 1)
                if s == 15:
                    pe.wait_ge(b_wkey, i + 1)
                    for a in range(2):
                        o = pm[:, 2, a * SEQ:(a + 1) * SEQ]
                        nc.tensor.matmul(o[:, 0:P], v_tok2[:, 2 * a, :], w_key[:, a, 0, :], start=True, stop=True)
                        nc.tensor.matmul(o[:, P:SEQ], v_tok2[:, 2 * a, :], w_key[:, a, 1, :], start=True, stop=False)
                        ins = nc.tensor.matmul(o[:, P:SEQ], v_tok2[:, 2 * a + 1, :], w_key[:, a, 2, :], start=False, stop=True)
                    ins.then_inc(b_o, 1)
                    pe.wait_ge(b_osq, i + 1)
                    nc.tensor.matmul(pm[:, 3, :], ones, rt[:, 0:2, :].rearrange("p a t -> p (a t)"), start=True, stop=True).then_inc(b_oss, 1)

            for first, end in ((HGRN_PAIR, DIFF_PAIR), (DIFF_PAIR, PAIRS)):
                with pe.Fori(first, end) as i:
                    def after(s):
                        if s == HEADS_SUM_STEP:
                            ada_sum(i * KD + (ADA0["mix_in"] + 1) * KD)
                        hgrn(s, i - HGRN_PAIR)
                        if first == DIFF_PAIR:
                            diff(s, i - DIFF_PAIR)
                    pair("mix_in", i, U_IN, n, normed(1), after)

            with pe.Fori(0, DJOBS) as i:
                pair("heads_out", i, U_HEAD, n, lambda s: pe.wait_ge(y_ready, s // 2 + 1), at=(0, HEADS))
            residual_out("mix_out", U_IN, lambda s: pe.wait_ge(mix_ready, DJOBS), 2, False)
            with pe.Fori(0, PAIRS) as i:
                pair("ffn2_in", i, U_IN, n, normed(2))

            with pe.Fori(0, DJOBS // 2) as i:
                def turn(b):
                    pe.wait_ge(half_free[b], JOB0["ffn2_out"] // 2 + i + 1)
                    for t in range(2):
                        for f in range(BLK):
                            ins = nc.tensor.transpose(pm[:, 2 * b + t, f * P:(f + 1) * P], tmp2[:, f, t * P:(t + 1) * P], ident)
                        ins.then_inc(fin_turned, 1)

                def after(s):
                    if s == U_OUT + 2:
                        turn(0)
                    if s == 2 * U_OUT - 1:
                        turn(1)
                        pe.wait_ge(fin_taken, 4 * i + 4)
                pair("ffn2_out", i, U_OUT, hid, lambda s: pe.wait_ge(hid_ready, 2 * PAIRS), after)

        @block.vector
        def _(dve):
            own = Chain(dve, dve_step)

            def split(slot, u):
                dve.wait_ge(hi_ready, u + 1)
                nc.vector.tensor_tensor(w_lo[:, slot], raw[:, slot], w_hi[:, slot], ALU.subtract).then_inc(split_ready, 1)

            def ada_add(total, w, k, before):
                if k == 0:
                    nc.vector.tensor_scalar(total, w, silu_c[:, 0:1], None, ALU.mult).then_inc(ada_mac, 1)
                else:
                    dve.wait_ge(ada_mac, before)
                    nc.vector.scalar_tensor_tensor(out=total, in0=w, scalar=silu_c[:, k:k + 1], in1=total,
                                                   op0=ALU.mult, op1=ALU.add).then_inc(ada_mac, 1)

            def ada_take(chunk, summed, at=0):
                dve.wait_ge(ada_cols, summed)
                nc.vector.tensor_tensor(mods[:, ds(chunk * BLK, BLK)], pm[:, 0, at:at + BLK], vec[:, ds(chunk * BLK + V_ADAB, BLK)],
                                        ALU.add).then_inc(ada_taken, 1)

            def ada_unit(a, name, i):
                g = (ADA0[name] - ADA_PRE + i) * ADA_UNITS + a
                dve.wait_ge(ada_landed[a % 2], 8 * (g - a % 2) + 16)
                for k in range(KU):
                    ada_add(ada_acc[:], ada_raw[:, a % 2, k, :], KU * a + k, i * KD + (ADA0[name] * KD + KU * a + k))

            nc.vector.memset(eps[:], EPS).then_inc(eps_ready, 1)
            dve.wait_ge(silu_ready, 1)
            lb, one_less, div = (bound[:, k * HEADS:(k + 1) * HEADS] for k in range(3))
            rows = [vec[:, a:a + HEADS] for a in (V_LB0, V_LB1)]
            dve.wait_ge(lam_landed, 16 * 4)
            own.link(nc.vector.tensor_tensor(div, rows[0], rows[1], ALU.max))
            for k in range(2):
                nc.vector.tensor_tensor(expo[:, k * HEADS:(k + 1) * HEADS], rows[k], div, ALU.subtract)
            for k in range(2):
                ins = nc.vector.tensor_tensor_reduce(out=l_prod[:, k, :], in0=lvec[:, 2 * k, :], in1=lvec[:, 2 * k + 1, :],
                                                     scale=1.0, scalar=0.0, op0=ALU.mult, op1=ALU.add,
                                                     accum_out=expo[:, 2 * HEADS + k:2 * HEADS + k + 1])
            ins.then_inc(expo_ready, 1)
            own.link(nc.vector.tensor_scalar(sub_gain[:], vec[:, V_SUB:V_SUB + 1], 1.0 - LAM_INIT, None, ALU.mult))
            dve.wait_ge(expo_done, 1)
            own.link(nc.vector.tensor_tensor(div, expo[:, 0:HEADS], expo[:, HEADS:2 * HEADS], ALU.add))
            own.link(nc.vector.reciprocal(div, div))
            own.link(nc.vector.tensor_tensor(lb, expo[:, 0:HEADS], div, ALU.mult))
            own.link(nc.vector.tensor_scalar(one_less, lb, -1.0, 1.0, ALU.mult, ALU.add))
            own.link(nc.vector.tensor_tensor(neg_lam[:], expo[:, 2 * HEADS + 1:], expo[:, 2 * HEADS:2 * HEADS + 1], ALU.subtract))
            own.link(nc.vector.tensor_scalar(neg_lam[:], neg_lam[:], LAM_INIT, None, ALU.subtract))

            with dve.Fori(0, ADA_PRE // 2) as i:
                for a in range(PRE_SLOTS // 2):
                    for c in range(2):
                        dve.wait_ge(pre_landed[2 * a + c], 16 * i + 16)
                    for k in range(PRE_K):
                        for c in range(2):
                            q = PRE_K * a + k
                            ada_add(pre_acc[c], ada_pre[:, 2 * a + c, k, :], q, i * (2 * KD) + (2 * q + c - 1))
                for c in range(2):
                    ada_take(i + c * (KD // BLK), 2 * i + 2, c * BLK)
            for u in range(RING):
                split(u, u)

            def normalise(m, weight, scale):
                dve.wait_ge(ada_taken, (scale + KD) // BLK)
                nc.vector.scalar_tensor_tensor(out=gain[:], in0=mods[:, scale:scale + KD], scalar=1.0,
                                               in1=vec[:, weight:weight + KD], op0=ALU.add, op1=ALU.mult).then_inc(gain_ready, 1)
                dve.wait_ge(sq_used, (m + 1) * DJOBS)
                nc.vector.tensor_copy(rstd[:], pm[:, 1, 0:SEQ]).then_inc(ss_part, 1)
                dve.wait_ge(ss_part, m + 1)
                nc.vector.tensor_tensor(rstd[:], rstd[:], pm[:, 1, SEQ:2 * SEQ], ALU.add).then_inc(ss_ready, 1)
                dve.wait_ge(root_ready, m + 1)
                nc.vector.reciprocal(rstd[:], rstd[:]).then_inc(rstd_ready, 1)
                dve.wait_ge(rstd_ready, m + 1)
                dve.wait_ge(gain_ready, m + 1)
                shift = scale - KD

                def lo(k):
                    dve.wait_ge(n_hi, m * KD + k + 1)
                    nc.vector.scalar_tensor_tensor(out=n[:, k, 1, :], in0=tmp[:, k % BLK, :], scalar=mods[:, shift + k:shift + k + 1],
                                                   in1=n[:, k, 0, :], op0=ALU.add, op1=ALU.subtract).then_inc(n_ready, 1)

                for k in range(KD):
                    if k >= BLK:
                        dve.wait_ge(n_ready, m * KD + k - BLK + 1)
                    nc.vector.scalar_tensor_tensor(out=tmp[:, k % BLK, :], in0=h[:, k, :], scalar=gain[:, k:k + 1],
                                                   in1=rstd[:], op0=ALU.mult, op1=ALU.mult).then_inc(t_ready, 1)
                    if k >= 2:
                        lo(k - 2)
                lo(KD - 2)
                lo(KD - 1)

            def ffn_in(name, ffn, ada):
                with dve.Fori(0, PAIRS) as i:
                    for s in range(2 * U_IN):
                        u = UNIT0[name] + i * (2 * U_IN) + s
                        split(s % RING, u + LEAD)
                        if s == 2 * U_IN - 1:
                            dve.wait_ge(unit_done, u + 1)
                            dve.wait_ge(half_free[0], JOB0[name] // 2 + i + 1)
                            nc.vector.tensor_tensor(tmp[:], acc[1][:], tmp[:], ALU.mult).then_inc(half_free[1], 1)
                            dve.wait_ge(hid_hi, ffn * PAIRS + i + 1)
                            nc.vector.tensor_tensor(hid[:, ds(i * BLK, BLK), 1, :], tmp[:], hid[:, ds(i * BLK, BLK), 0, :],
                                                    ALU.subtract).then_inc(hid_ready, 1)
                        if ada and s in ADA_STEPS:
                            ada_unit(ADA_STEPS.index(s), name, i)
                        if ada and s == ADA_TAKE_STEP:
                            ada_take(i + ADA0[name], i + (ADA0[name] + 1))

            def add_residual(dst, block0, b, factor, at):
                for f in range(BLK):
                    ins = nc.vector.scalar_tensor_tensor(out=dst(f), in0=acc[b][:, f, :], scalar=factor[:, ds(block0 + at + f, 1)],
                                                         in1=blk(h, block0 + f), op0=ALU.mult, op1=ALU.add)
                return ins

            def half_gate(g, count):
                dve.wait_ge(ada_taken, (g + KD) // BLK)
                nc.vector.tensor_scalar(gate[:], mods[:, g:g + KD], 0.5, None, ALU.mult).then_inc(gate_ready, 1)
                dve.wait_ge(gate_ready, count)

            def residual_out(name, units, factor, at, ada):
                with dve.Fori(0, DJOBS // 2) as i:
                    for s in range(2 * units):
                        u = UNIT0[name] + i * (2 * units) + s
                        split(s % RING, u + LEAD)
                        if s % units == units - 1:
                            b = s // units
                            dve.wait_ge(unit_done, u + 1)
                            block0 = i * (2 * BLK) + b * BLK
                            add_residual(lambda f: blk(h, block0 + f), block0, b, factor, at).then_inc(half_free[b], 1)
                        if ada:
                            part, step = divmod(s, ADA_OUT_STRIDE)
                            if part < ADA_PER_OUT and step in ADA_STEPS:
                                ada_unit(ADA_STEPS.index(step), name, i * ADA_PER_OUT + part)
                            if s - 1 in ADA_OUT_SUM:
                                chunk = i * ADA_PER_OUT + (ADA0[name] + ADA_OUT_SUM.index(s - 1))
                                ada_take(chunk, chunk + 1)

            normalise(0, V_N1, SC1)
            ffn_in("ffn1_in", 0, True)
            half_gate(G1, 1)
            residual_out("ffn1_out", U_OUT, gate, 0, True)
            normalise(1, V_N2, SC2)

            def hgrn(s, i, own, gated):
                C = HGRN_CHUNK
                if s == 0:
                    nc.vector.tensor_scalar(kk, blk(mixs, i + B_HF), -1.0, 1.0, ALU.mult, ALU.add)
                    dve.wait_ge(a_logf, i + 1)
                    nc.vector.tensor_tensor_scan(bcum, reset, logf[:], 0.0, ALU.mult, ALU.add).then_inc(a_b, 1)
                if s == 1:
                    dve.wait_ge(a_b, i + 1)
                    for j in range(6):
                        m = 1 << j
                        bv = bcum.rearrange("p (n two m) -> p n two m", two=2, m=m)
                        xv = X[:, j, :].rearrange("p (n two m) -> p n two m", two=2, m=m)
                        r = bv[:, :, 0, m - 1:m].to_broadcast([P, SEQ // (2 * m), m])
                        nc.vector.tensor_tensor(xv[:, :, 0, :], r, bv[:, :, 0, :], ALU.subtract)
                        nc.vector.tensor_tensor(xv[:, :, 1, :], bv[:, :, 1, :], r, ALU.subtract)
                if s == 2:
                    b_at = [bcum[:, C * q:C * (q + 1)] for q in range(4)]
                    last = [bcum[:, C * (q + 1) - 1:C * (q + 1)] for q in range(4)]
                    for q in (0, 2):
                        nc.vector.tensor_scalar(X[:, 6, C * q:C * (q + 1)], b_at[q], -1.0, last[q], ALU.mult, ALU.add)
                        nc.vector.tensor_copy(X[:, 6, C * (q + 1):C * (q + 2)], b_at[q + 1])
                    nc.vector.tensor_scalar(X[:, 7, C:2 * C], b_at[1], -1.0, last[1], ALU.mult, ALU.add)
                    nc.vector.tensor_copy(X[:, 7, 2 * C:3 * C], b_at[2])
                    own.link(nc.vector.tensor_scalar(X[:, 7, 3 * C:4 * C], b_at[3], last[2], None, ALU.add))
                    nc.vector.tensor_scalar(X[:, 7, 0:C], X[:, 6, 0:C], last[1], None, ALU.add).then_inc(a_arg, 1)
                if s == 5:
                    dve.wait_ge(a_exp, i + 1)
                    for j in range(LEVELS):
                        m = 1 << j
                        xv, kv = (t.rearrange("p (n two m) -> p n two m", two=2, m=m) for t in (X[:, j, :], kk))
                        qv = mixs[:, ds(i + B_HQ, 1), :].rearrange("p a (n two m) -> p (a n) two m", two=2, m=m)
                        nc.vector.tensor_tensor(xv[:, :, 0, :], xv[:, :, 0, :], kv[:, :, 0, :], ALU.mult)
                        ins = nc.vector.tensor_tensor(xv[:, :, 1, :], xv[:, :, 1, :], qv[:, :, 1, :], ALU.mult)
                    ins.then_inc(a_x, 1)
                if s in (8, 10):
                    g = s // 10
                    dve.wait_ge(a_sc, 2 * i + g + 1)
                    nc.vector.tensor_tensor(masked[:], pm[:, 0:2, :].rearrange("p b (j t) -> p (b j) t", t=P), level_mask[:], ALU.mult)                      .then_inc(a_masked, 1)
                    dve.wait_ge(a_masked, 2 * i + g + 1)
                    if g:
                        nc.vector.tensor_copy(S[1], acc[0][:, 0, 0:P])
                    ins = nc.vector.tensor_reduce(S[2 * g], masked[:].rearrange("p j t -> p t j"), AX_X, ALU.add)
                    if g:
                        ins.then_inc(a_s, 1)
                    else:
                        own.link(ins)
                if s == 15:
                    dve.wait_ge(a_rstd, i + 1)
                    y = blk(mixs, i + B_HF)
                    nc.vector.scalar_tensor_tensor(out=y, in0=y, scalar=vec[:, V_HN:V_HN + 1], in1=o_sq[:], op0=ALU.mult, op1=ALU.mult)                      .then_inc(a_normed, 1)
                    if gated:
                        dve.wait_ge(hg_ready, 1)
                        dve.wait_ge(a_normed, i + 1)
                        early = DIFF_PAIR - HGRN_PAIR
                        for k in (i, i - early):
                            ins = nc.vector.tensor_tensor(blk(mixs, k + B_HF), blk(mixs, k + B_HF), blk(mixs, k + B_HG), ALU.mult)
                        ins.then_inc(a_done, 1)

            def diff(s, i, own):
                if s == 4:
                    dve.wait_ge(b_rstd, i + 1)
                    for w in range(2):
                        ins = nc.vector.scalar_tensor_tensor(out=qk[:, 2 * w:2 * w + 2, :], in0=mixs[:, ds(2 * i + (B_DQ, B_DK)[w], 2), :],
                                                             scalar=vec[:, V_QN + w:V_QN + w + 1], in1=rt[:, 2 * w:2 * w + 2, :],
                                                             op0=ALU.mult, op1=ALU.mult)
                    ins.then_inc(b_norm, 1)
                if s == 6:
                    dve.wait_ge(trig_ready, 1)
                    dve.wait_ge(b_norm, i + 1)
                    dve.wait_ge(b_rot, i + 1)
                    sin, cos = (trig[:, k:k + 1, :].to_broadcast([P, 4, SEQ]) for k in range(2))
                    nc.vector.tensor_tensor(qk[:], qk[:], cos, ALU.mult)
                    own.link(nc.vector.tensor_tensor(rt, pm[:, 2:4, :].rearrange("p b (a t) -> p (b a) t", t=SEQ), sin, ALU.mult))
                    nc.vector.tensor_tensor(qk[:], qk[:], rt, ALU.add).then_inc(b_rope, 1)
                if s in (9, 10):
                    a = s - 9
                    dve.wait_ge(b_sc, 2 * i + a + 1)
                    nc.vector.scalar_tensor_tensor(out=score[:, a], in0=pm[:, 2:4, 0:3 * P], scalar=DH ** -0.5,
                                                   in1=causal[:].unsqueeze(1).to_broadcast([P, 2, 3 * P]), op0=ALU.mult, op1=ALU.add)                      .then_inc(b_masked, 1)
                if s == 10:
                    dve.wait_ge(b_masked, 2 * i + 2)
                    sv = score[:].rearrange("p a m k -> p (a m) k")
                    mv = row_max[:].rearrange("p (m t) -> p m t", t=2)
                    nc.vector.tensor_reduce(mv[:, :, 0], sv[:, :, 0:P], AX_X, ALU.max)
                    own.link(nc.vector.tensor_reduce(mv[:, :, 1], sv[:, :, P:3 * P], AX_X, ALU.max))
                    nc.vector.tensor_scalar(row_max[:], row_max[:], -1.0, None, ALU.mult).then_inc(b_max, 1)
                if s == 12:
                    dve.wait_ge(b_exp, i + 1)
                    own.link(nc.vector.reciprocal(row_sum[:], row_sum[:]))
                    second = row_sum[:].rearrange("p (a m t) -> p a m t", m=2, t=2)[:, :, 1, :]
                    own.link(nc.vector.tensor_scalar(second, second, neg_lam[:], None, ALU.mult))
                    for m in (1, 0):
                        for a in range(2):
                            for t in range(2):
                                cols, f = slice(t * P, (1 + 2 * t) * P), row_sum[:, 4 * a + 2 * m + t:4 * a + 2 * m + t + 1]
                                if m:
                                    ins = nc.vector.tensor_scalar(score[:, a, 1, cols], score[:, a, 1, cols], f, None, ALU.mult)
                                else:
                                    ins = nc.vector.scalar_tensor_tensor(out=score[:, a, 0, cols], in0=score[:, a, 0, cols], scalar=f,
                                                                         in1=score[:, a, 1, cols], op0=ALU.mult, op1=ALU.add)
                        if m:
                            own.link(ins)
                    ins.then_inc(b_w, 1)
                if s == 15:
                    dve.wait_ge(b_orstd, i + 1)
                    y = mixs[:, ds(2 * i + B_DK, 2), :]
                    nc.vector.scalar_tensor_tensor(out=y, in0=y, scalar=sub_gain[:], in1=rt[:, 2:4, :], op0=ALU.mult, op1=ALU.mult)                      .then_inc(b_done, 1)

            def mix_pairs(first, end, done):
                links = 2 * (first >= HGRN_PAIR) + 5 * (first >= DIFF_PAIR)
                steps, take = (HEADS_ADA_STEPS, HEADS_SUM_STEP) if first >= HGRN_PAIR else (ADA_STEPS, ADA_TAKE_STEP)
                with dve.Fori(first, end) as i:
                    own = Chain(dve, dve_step, (i - first) * links + done)
                    for s in range(2 * U_IN):
                        split(s % RING, UNIT0["mix_in"] + i * (2 * U_IN) + s + LEAD)
                        if s in steps:
                            ada_unit(steps.index(s), "mix_in", i)
                        if s == take:
                            ada_take(i + ADA0["mix_in"], i + (ADA0["mix_in"] + 1))
                        if first >= HGRN_PAIR:
                            hgrn(s, i - HGRN_PAIR, own, first >= DIFF_PAIR)
                        if first >= DIFF_PAIR:
                            diff(s, i - DIFF_PAIR, own)
                    assert own.k == links
                return done + (end - first) * links

            mix_pairs(0, HGRN_PAIR, 0)

            dve.wait_ge(late_landed, 16 * 4)
            dve.wait_ge(sig_ready, 1)
            for k in range(HEADS):
                ins = nc.vector.tensor_scalar(mixs[:, B_HF + k, :], mixs[:, B_HF + k, :], one_less[:, k:k + 1], lb[:, k:k + 1],
                                              ALU.mult, ALU.add)
            ins.then_inc(f_ready, 1)
            dve.wait_ge(f_ready, 1)
            done = mix_pairs(HGRN_PAIR, DIFF_PAIR, own.k)

            own = Chain(dve, dve_step, done)
            turn = (6.28125, 0.0019350051879882812)
            turn += (2 * np.pi - sum(turn),)
            big = 1.5 * 2.0 ** 23
            own.link(nc.vector.tensor_copy(angle[:], pos[:]))
            own.link(nc.vector.tensor_scalar(angle[:], angle[:], freq, None, ALU.mult))
            for k, quarter in enumerate((0.0, 0.25)):
                ins = nc.vector.tensor_scalar(whole[:, k, :], angle[:], 1.0 / (2 * np.pi), quarter, ALU.mult, ALU.add)
            own.link(ins)
            own.link(nc.vector.tensor_scalar(whole[:], whole[:], big, None, ALU.add))
            own.link(nc.vector.tensor_scalar(whole[:], whole[:], big, None, ALU.subtract))
            src = angle[:].unsqueeze(1).to_broadcast([P, 2, SEQ])
            for part in turn:
                own.link(nc.vector.scalar_tensor_tensor(out=trig[:], in0=whole[:], scalar=-float(part), in1=src, op0=ALU.mult, op1=ALU.add))
                src = trig[:]
            own.link(nc.vector.tensor_scalar(trig[:, 1, :], trig[:, 1, :], np.pi / 2, None, ALU.add))
            nc.vector.tensor_scalar(trig[:], trig[:], 3.1415925, -3.1415925, ALU.min, ALU.max).then_inc(angle_ready, 1)
            mix_pairs(DIFF_PAIR, PAIRS, done + own.k)

            for g, at in enumerate((B_HF, B_HF + BLK, B_DK, B_DK + BLK)):
                dve.wait_ge(y_hi, g + 1)
                nc.vector.tensor_tensor(n[:, g * BLK:(g + 1) * BLK, 1, :], mixs[:, at:at + BLK, :], n[:, g * BLK:(g + 1) * BLK, 0, :],
                                        ALU.subtract).then_inc(y_ready, 1)

            with dve.Fori(0, DJOBS) as i:
                for s in range(2 * U_HEAD):
                    u = UNIT0["heads_out"] + i * (2 * U_HEAD) + s
                    split(s % RING, u + LEAD)
                    if s == U_HEAD - 1:
                        dve.wait_ge(sig_ready, 2 * i + 3)
                        dve.wait_ge(unit_done, u + 1)
                        nc.vector.tensor_tensor(tmp2[:], acc[0][:], mixs[:, ds(i * BLK + B_GA, BLK), :], ALU.mult).then_inc(half_free[0], 1)
                    if s == 2 * U_HEAD - 1:
                        dve.wait_ge(unit_done, u + 1)
                        nc.vector.tensor_tensor(tmp[:], acc[1][:], mixs[:, ds(i * GB_STRIDE + B_GB, BLK), :], ALU.mult).then_inc(half_free[1], 1)
                        dve.wait_ge(half_free[0], JOB0["heads_out"] // 2 + i + 1)
                        dve.wait_ge(half_free[1], JOB0["heads_out"] // 2 + i + 1)
                        nc.vector.tensor_tensor(tmp[:], tmp[:], tmp2[:], ALU.add).then_inc(mix_sum, 1)
                dve.wait_ge(mix_hi, i + 1)
                dve.wait_ge(mix_sum, i + 1)
                nc.vector.tensor_tensor(hid[:, ds(i * BLK, BLK), 1, :], tmp[:], hid[:, ds(i * BLK, BLK), 0, :], ALU.subtract)\
                    .then_inc(mix_ready, 1)
                dve.wait_ge(mix_ready, i + 1)

            dve.wait_ge(h_back, 16)
            residual_out("mix_out", U_IN, mods, G2, False)
            normalise(2, V_N3, SC3)
            ffn_in("ffn2_in", 1, False)
            half_gate(G3, 2)
            for s in range(DJOBS * U_OUT):
                u = UNIT0["ffn2_out"] + s
                if u + LEAD < UNITS:
                    split(s % RING, u + LEAD)
                if s % U_OUT == U_OUT - 1:
                    j = s // U_OUT
                    dve.wait_ge(unit_done, u + 1)
                    if j:
                        dve.wait_ge(fin_turned, 2 * j)
                    add_residual(lambda f: tmp2[:, f, :], j * BLK, j % 2, gate, 0).then_inc(half_free[j % 2], 1)


_INS = ["x", "c", "positions", "ada_w", "ada_b", "norm1_w", "ffn1_w_in", "ffn1_w_out", "norm2_w", "mix_w_in", "hgrn_lb",
        "hgrn_norm_w", "hgrn_w_out", "diff_q_norm_w", "diff_k_norm_w", "diff_lq1", "diff_lk1", "diff_lq2", "diff_lk2",
        "diff_subln_w", "diff_w_out", "mix_w_o", "norm3_w", "ffn2_w_in", "ffn2_w_out"]


def kernel(**inputs):
    import concourse.bacc as bacc
    from concourse.bass_utils import run_bass_kernel_spmd

    nc = bacc.Bacc("TRN2", target_bir_lowering=False, num_devices=1)
    arrays, args = {}, []
    for name in _INS + ["consts"]:
        a = constants() if name == "consts" else np.ascontiguousarray(inputs[name])
        arrays[f"in_{name}"] = a
        args.append(nc.dram_tensor(f"in_{name}", a.shape, mybir.dt.from_np(a.dtype), kind="ExternalInput").ap())
    args.append(nc.dram_tensor("out_0", (1, SEQ, D), F32, kind="ExternalOutput").ap())
    build(nc, *args)
    r = run_bass_kernel_spmd(nc, [arrays], core_ids=[0])
    return r.results[0]["out_0"]
```

```python
from contextlib import ExitStack

import numpy as np

import concourse.bass as bass
from concourse import mybir

F32 = mybir.dt.float32
F32R = mybir.dt.float32r
I32 = mybir.dt.int32
ALU = mybir.AluOpType
ACT = mybir.ActivationFunctionType
AX_X = mybir.AxisListType.X

P = 128
D = 2048
SEQ = 256
D_FF = 5632
MIX_WIDTH = 11264
HEADS = 8
HGRN_CHUNK = 64
DH = 64
ROPE_HALF = 8
ROPE_THETA = 500000.0
EPS = 1e-6
LAM_INIT = 0.2

KD = D // P
KF = D_FF // P
COLS = 512
BLK = COLS // P
KU = 2
RING = 4
LEAD = RING

U_IN = KD // KU
U_OUT = KF // KU
U_HEAD = HEADS // KU
PAIRS = D_FF // COLS
DJOBS = D // COLS
assert MIX_WIDTH == 2 * PAIRS * COLS

UNIT0, JOB0 = {}, {}
_u = _j = 0
for _name, _jobs, _units in (("ffn1_in", 2 * PAIRS, U_IN), ("ffn1_out", DJOBS, U_OUT), ("mix_in", 2 * PAIRS, U_IN),
                             ("heads_out", 2 * DJOBS, U_HEAD), ("mix_out", DJOBS, U_IN),
                             ("ffn2_in", 2 * PAIRS, U_IN), ("ffn2_out", DJOBS, U_OUT)):
    UNIT0[_name], JOB0[_name] = _u, _j
    _u += _jobs * _units
    _j += _jobs
UNITS = _u

HGRN_PAIR = 3
VALUE_PAIRS = (2, 6)
DIFF_PAIR = 7
GB_PAIR = 9
assert PAIRS - HGRN_PAIR == HEADS and 2 * (PAIRS - DIFF_PAIR) == HEADS

N_MOD = 9
ADA_CHUNKS = N_MOD * D // COLS
ADA_PRE = 2 * D // COLS
ADA_PER_OUT = 3
ADA0 = {"ffn1_in": ADA_PRE, "ffn1_out": ADA_PRE + PAIRS, "mix_in": ADA_PRE + PAIRS + 2 * ADA_PER_OUT}
ADA0["ffn2_in"] = ADA0["mix_in"] + DIFF_PAIR
ADA_LAST = ADA_CHUNKS - ADA0["ffn2_in"]
ADA_STEPS = (0, 1, 3, 4, 6, 7, 9, 10)
ADA_SUM_STEP = 13
ADA_TAKE_STEP = 14
HEADS_ADA_STEPS, HEADS_SUM_STEP = (0, 3, 4, 6, 7, 9, 10, 12), 15
ADA_OUT_STRIDE = 14
ADA_OUT_SUM = tuple(ADA_OUT_STRIDE * p + 12 for p in range(ADA_PER_OUT))
ADA_UNITS = KD // KU
PRE_SLOTS, PRE_K = 8, 4
PRE_GROUPS = KD // PRE_K
PRE_MACS = (PRE_GROUPS - 1) * PRE_K
PRE_SKIPPED = ADA_PRE * PRE_K
SH1, SC1, G1, SH2, SC2, G2, SH3, SC3, G3 = (m * KD for m in range(N_MOD))

V_ADAB = 0
V_C = N_MOD * KD
V_N1, V_N2, V_N3, V_LB0, V_LB1 = V_C + KD, V_C + 2 * KD, V_C + 3 * KD, V_C + 4 * KD, V_C + 4 * KD + HEADS
V_HN = V_C + 5 * KD
V_QN, V_KN, V_SUB = V_HN + 1, V_HN + 2, V_HN + 3
V_END = V_HN + 4
V_ROWS2 = V_END - P

B_HQ, B_HF, B_HI, B_HG, B_DQ, B_DK, B_DV, B_GA = 0, 8, 16, 24, 32, 40, 48, 56
MIX_BLOCKS = 72
B_GB, GB_STRIDE = B_HQ, 16
LEVELS = 8

C_IDENT, C_ONES, C_HALF, C_ROT, C_FREQ = 0, P, 2 * P, 3 * P, 4 * P
C_CAUSAL = 4 * P + 1
C_RESET = C_CAUSAL + 3 * P
C_LEVEL = C_RESET + SEQ
C_END = C_LEVEL + LEVELS * P
MASKED = -1e30


def constants():
    c = np.zeros((P, C_END), np.float32)
    r = np.arange(P)
    c[:, C_IDENT:C_IDENT + P] = np.eye(P)
    c[:, C_ONES:C_ONES + P] = 1.0
    c[:, C_HALF:C_HALF + P] = (r[:, None] // DH) == (r[None, :] // DH)
    for half in range(2):
        for d in range(ROPE_HALF):
            lo, hi = half * DH + d, half * DH + d + ROPE_HALF
            c[hi, C_ROT + lo] = -1.0
            c[lo, C_ROT + hi] = 1.0
            f = np.float32(ROPE_THETA) ** np.float32(-d / ROPE_HALF)
            c[lo, C_FREQ] = c[hi, C_FREQ] = f
    tri = np.where(r[None, :] <= r[:, None], 0.0, MASKED)
    c[:, C_CAUSAL:C_CAUSAL + P] = tri
    c[:, C_CAUSAL + 2 * P:C_CAUSAL + 3 * P] = tri
    c[:, C_RESET:C_RESET + SEQ] = (np.arange(SEQ) % HGRN_CHUNK != 0)[None, :]
    s, t = r[:, None], r[None, :]
    for j in range(LEVELS - 1):
        m = 1 << j
        c[:, C_LEVEL + j * P:C_LEVEL + (j + 1) * P] = (s // (2 * m) == t // (2 * m)) & ((s // m) % 2 == 0) & ((t // m) % 2 == 1)
    c[:, C_LEVEL + (LEVELS - 1) * P:C_END] = s == t
    return c


class Chain:

    def __init__(self, eng, sem, base=0):
        self.eng, self.sem, self.base, self.k = eng, sem, base, 0

    def mark(self, ins):
        self.k += 1
        ins.then_inc(self.sem, 1)

    def wait(self):
        self.eng.wait_ge(self.sem, self.base + self.k)

    def link(self, ins):
        self.mark(ins)
        self.wait()


def build(nc, x, c, positions, ada_w, ada_b, norm1_w, ffn1_w_in, ffn1_w_out, norm2_w, mix_w_in, hgrn_lb,
          hgrn_norm_w, hgrn_w_out, diff_q_norm_w, diff_k_norm_w, diff_lq1, diff_lk1, diff_lq2, diff_lk2,
          diff_subln_w, diff_w_out, mix_w_o, norm3_w, ffn2_w_in, ffn2_w_out, consts, out):
    ds = bass.ds

    def blk(t, i):
        return t[:, ds(i, 1), :].rearrange("p a t -> p (a t)")

    with ExitStack() as ctx:
        def sb(name, shape, dt=F32):
            return ctx.enter_context(nc.sbuf_tensor(name, shape, dt))

        def sem(name):
            return ctx.enter_context(nc.semaphore(name))

        raw = sb("raw", [P, RING, KU, COLS])
        w_hi = sb("w_hi", [P, RING, KU, COLS], F32R)
        w_lo = sb("w_lo", [P, RING, KU, COLS], F32R)
        ada_raw = sb("ada_raw", [P, 2, KU, COLS])
        h = sb("h", [P, KD, SEQ])
        n = sb("n", [P, KD, 2, SEQ], F32R)
        hid = sb("hid", [P, KF, 2, SEQ], F32R)
        tmp = sb("tmp", [P, BLK, SEQ])
        tmp2 = sb("tmp2", [P, BLK, SEQ])
        ada_acc = sb("ada_acc", [P, COLS])
        ada_col = sb("ada_col", [P, BLK])
        mods = sb("mods", [P, N_MOD * KD])
        vec = sb("vec", [P, V_END])
        silu_c = sb("silu_c", [P, KD])
        gain = sb("gain", [P, KD])
        gate = sb("gate", [P, KD])
        rstd = sb("rstd", [P, SEQ])
        eps = sb("eps", [P, 1])
        junk = sb("junk", [P, 1])
        expo = sb("expo", [P, 2 * HEADS + 2])
        bound = sb("bound", [P, 3 * HEADS])
        neg_lam = sb("neg_lam", [P, 1])
        sub_gain = sb("sub_gain", [P, 1])
        row_max = sb("row_max", [P, 8])
        row_sum = sb("row_sum", [P, 8])
        cst = sb("cst", [P, C_FREQ + 1])
        ident, ones, half_ones, rot, freq = (cst[:, a:a + w] for a, w in (
            (C_IDENT, P), (C_ONES, P), (C_HALF, P), (C_ROT, P), (C_FREQ, 1)))

        class Region:
            def __init__(self, host, size):
                self.at = nc.lookup_mloc(host).addr
                self.end = self.at + size

            def take(self, name, shape, dt=F32):
                t = nc.alloc_sbuf_tensor_at(name, [P] + shape, dt, offset=self.at)
                self.at += 4 * int(np.prod(shape))
                assert self.at <= self.end, name
                return t

        before = Region(hid, 8 * KF * SEQ)
        ada_pre = before.take("ada_pre", [PRE_SLOTS, PRE_K, COLS])
        x_in = before.take("x_in", [2, D])
        vec_in = before.take("vec_in", [2, P])
        lvec = before.take("lvec", [4, DH])
        silu_wide = before.take("silu_wide", [PRE_K, P])
        l_prod = before.take("l_prod", [2, DH])
        beside = Region(hid, 8 * KF * SEQ)
        mixs = beside.take("mixs", [MIX_BLOCKS, SEQ])
        score = beside.take("score", [2, 2, 3 * P])
        qk = beside.take("qk", [4, SEQ])
        v_tok2 = beside.take("v_tok2", [4, P])
        trig = beside.take("trig", [2, SEQ])
        causal = beside.take("causal", [3 * P])
        S_full = beside.take("S_full", [P])
        in_score = Region(score, 4 * 4 * 3 * P)
        sq_k = in_score.take("sq_k", [2, SEQ])
        w_key = nc.alloc_sbuf_tensor_at("w_key", [P, 2, 3, P], F32, offset=nc.lookup_mloc(qk).addr)
        in_h = Region(h, 4 * KD * SEQ)
        X = in_h.take("X", [LEVELS, SEQ])
        masked = in_h.take("masked", [LEVELS, P])
        level_mask = in_h.take("level_mask", [LEVELS, P])
        in_masked = Region(masked, 4 * LEVELS * P)
        o_sq = in_masked.take("o_sq", [SEQ])
        turns = Region(qk, 4 * 4 * SEQ)
        angle = turns.take("angle", [SEQ])
        whole = turns.take("whole", [2, SEQ])
        pos = turns.take("pos", [SEQ], I32)
        pre_acc = (ada_acc[:], tmp2[:, 0:2, :].rearrange("p a t -> p (a t)"))
        rt = tmp[:]
        kk, bcum, reset = (tmp2[:, k, :] for k in range(3))
        v_tok = tmp2[:, 3, :].rearrange("p (a v) -> p a v", a=2)
        logf = nc.alloc_sbuf_tensor_at("logf", [P, SEQ], F32, offset=nc.lookup_mloc(rstd).addr)
        S = (rstd[:, 0:P], S_full[:], rstd[:, P:2 * P])
        out_tile = Region(n, 8 * KD * SEQ).take("out_tile", [DJOBS, 2, COLS])

        acc = [ctx.enter_context(nc.psum_tensor(f"acc{i}", [P, BLK, SEQ], F32)) for i in range(2)]
        pm = ctx.enter_context(nc.psum_tensor("pm", [P, 4, COLS], F32))

        raw_landed = [sem(f"raw_landed{i}") for i in range(RING)]
        hi_ready = sem("hi_ready")
        split_ready = sem("split_ready")
        unit_done = sem("unit_done")
        half_free = [sem(f"half_free{i}") for i in range(2)]
        ada_landed = [sem(f"ada_landed{i}") for i in range(2)]
        ada_mac = sem("ada_mac")
        ada_cols = sem("ada_cols")
        wide_ready = sem("wide_ready")
        ada_own = sem("ada_own")
        ada_taken = sem("ada_taken")
        pre_landed = [sem(f"pre_landed{i}") for i in range(PRE_SLOTS)]
        x_landed, vec_landed, cst_landed, late_landed = (sem(s) for s in ("x_landed", "vec_landed", "cst_landed", "late_landed"))
        lam_landed, h_stored, h_back, pos_landed = sem("lam_landed"), sem("h_stored"), sem("h_back"), sem("pos_landed")
        vec_turned, vec_ready, silu_ready, eps_ready = (sem(s) for s in ("vec_turned", "vec_ready", "silu_ready", "eps_ready"))
        x_turned, x_taken = sem("x_turned"), sem("x_taken")
        hid_hi, hid_ready = sem("hid_hi"), sem("hid_ready")
        sq_ready, sq_used = sem("sq_ready"), sem("sq_used")
        ss_part, ss_ready, root_ready, rstd_ready, gain_ready, gate_ready = (
            sem(s) for s in ("ss_part", "ss_ready", "root_ready", "rstd_ready", "gain_ready", "gate_ready"))
        t_ready, n_hi, n_ready = sem("t_ready"), sem("n_hi"), sem("n_ready")
        sig_ready, hg_ready, f_ready = sem("sig_ready"), sem("hg_ready"), sem("f_ready")
        expo_ready, expo_done, angle_ready, trig_ready = (sem(s) for s in ("expo_ready", "expo_done", "angle_ready", "trig_ready"))
        dve_step = sem("dve_step")
        act_step = sem("act_step")
        a_logf, a_vtok, a_b, a_arg, a_exp, a_x, a_sc, a_masked, a_s, a_o, a_taken, a_ss, a_rstd, a_normed, a_done = (
            sem(f"a_{s}") for s in ("logf", "vtok", "b", "arg", "exp", "x", "sc", "masked", "s", "o", "taken",
                                    "ss", "rstd", "normed", "done"))
        b_sq, b_ss, b_rstd, b_vtok, b_norm, b_rot, b_rope, b_sc, b_masked, b_max, b_exp, b_w = (
            sem(f"b_{s}") for s in ("sq", "ss", "rstd", "vtok", "norm", "rot", "rope", "sc", "masked", "max", "exp", "w"))
        b_wturn, b_wkey, b_o, b_osq, b_taken, b_oss, b_orstd, b_done = (
            sem(f"b_{s}") for s in ("wturn", "wkey", "o", "osq", "taken", "oss", "orstd", "done"))
        y_hi, y_ready = sem("y_hi"), sem("y_ready")
        mix_sum, mix_hi, mix_ready = (sem(f"mix_{s}") for s in ("sum", "hi", "ready"))
        fin_turned, fin_taken, stored = sem("fin_turned"), sem("fin_taken"), sem("stored")

        h_store = nc.dram_tensor("h_store", (P, KD * SEQ), F32, kind="Internal").ap()

        def units_of(w, k=KU):
            return w[0].rearrange("(a k p) n -> a p k n", p=P, k=k)

        block = ctx.enter_context(nc.Block())

        @block.sync
        def _(sp):
            def rows_of(v):
                return v.rearrange("(r q) -> r q", q=P)

            sp.dma_start(cst[:], consts[:, 0:C_FREQ + 1]).then_inc(cst_landed, 16)
            adab = rows_of(ada_b[0])
            for tile, row, src in ((0, 0, adab[0:P]), (1, 0, adab[P:N_MOD * KD]), (1, V_C - P, rows_of(c[0])),
                                   (1, V_N1 - P, rows_of(norm1_w[0])), (1, V_N2 - P, rows_of(norm2_w[0])),
                                   (1, V_N3 - P, rows_of(norm3_w[0])), (1, V_LB0 - P, rows_of(hgrn_lb[0])),
                                   (1, V_LB1 - P, rows_of(hgrn_lb[1])), (1, V_HN - P, hgrn_norm_w), (1, V_SUB - P, diff_subln_w)):
                sp.dma_start(vec_in[row:row + src.shape[0], tile, :], src).then_inc(vec_landed, 16)
            for row, w in ((V_QN - P, diff_q_norm_w), (V_KN - P, diff_k_norm_w)):
                for s in range(2):
                    sp.dma_start(vec_in[row:row + 1, 1, s * DH:(s + 1) * DH], w).then_inc(vec_landed, 16)

            for k, w in enumerate((diff_lq1, diff_lk1, diff_lq2, diff_lk2)):
                sp.dma_start(lvec[:, k, :], w[0].partition_broadcast(P)).then_inc(lam_landed, 16)

            ada4 = units_of(ada_w, PRE_K)
            for u in range(PRE_SLOTS):
                sp.dma_start(ada_pre[:, u], ada4[u // 2, :, :, u % 2 * D:u % 2 * D + COLS]).then_inc(pre_landed[u], 16)
            sp.dma_start(x_in[:], x[0].rearrange("(t p) d -> p t d", p=P)).then_inc(x_landed, 16)
            with sp.Fori(1, ADA_PRE // 2) as i:
                for u in range(PRE_SLOTS):
                    group, which = divmod(u, 2)
                    if group == PRE_GROUPS - 1:
                        sp.wait_ge(ada_cols, 2 * (i - 1) + which + 1)
                    else:
                        sp.wait_ge(ada_mac, (i - 1) * (2 * PRE_MACS) + (2 * (PRE_K * (group + 1) - 1) + which + 1))
                    sp.dma_start(ada_pre[:, u], ada4[u // 2, :, :, ds(i * COLS + u % 2 * D, COLS)])\
                      .then_inc(pre_landed[u], 16)

            def pair(name, i, units, jobs, started=True):
                for s in range(2 * units):
                    src, col = jobs[s // units]
                    if started or s >= RING:
                        sp.wait_ge(split_ready, UNIT0[name] + i * (2 * units) + s - (RING - 1))
                    sp.dma_start(raw[:, s % RING], src[s % units, :, :, ds(col, COLS)]).then_inc(raw_landed[s % RING], 16)

            in1, out1, mixw, in2, out2 = (units_of(w) for w in (ffn1_w_in, ffn1_w_out, mix_w_in, ffn2_w_in, ffn2_w_out))
            how, dow, mow = (units_of(w) for w in (hgrn_w_out, diff_w_out, mix_w_o))
            pair("ffn1_in", 0, U_IN, ((in1, 0), (in1, D_FF)), started=False)
            with sp.Fori(1, PAIRS) as i:
                pair("ffn1_in", i, U_IN, ((in1, i * COLS), (in1, i * COLS + D_FF)))
            with sp.Fori(0, DJOBS // 2) as i:
                pair("ffn1_out", i, U_OUT, ((out1, i * (2 * COLS)), (out1, i * (2 * COLS) + COLS)))
            with sp.Fori(0, HGRN_PAIR) as i:
                pair("mix_in", i, U_IN, ((mixw, i * (2 * COLS)), (mixw, i * (2 * COLS) + COLS)))
            sp.wait_ge(h_stored, 16)
            for dst, src in ((level_mask[:], consts[:, C_LEVEL:C_END].rearrange("p (j t) -> p j t", t=P)),
                             (causal[:], consts[:, C_CAUSAL:C_RESET]), (reset, consts[:, C_RESET:C_LEVEL])):
                sp.dma_start(dst, src).then_inc(late_landed, 16)
            with sp.Fori(HGRN_PAIR, PAIRS) as i:
                pair("mix_in", i, U_IN, ((mixw, i * (2 * COLS)), (mixw, i * (2 * COLS) + COLS)))
            with sp.Fori(0, DJOBS) as i:
                pair("heads_out", i, U_HEAD, ((how, i * COLS), (dow, i * COLS)))
            with sp.Fori(0, DJOBS // 2) as i:
                pair("mix_out", i, U_IN, ((mow, i * (2 * COLS)), (mow, i * (2 * COLS) + COLS)))
            with sp.Fori(0, PAIRS) as i:
                pair("ffn2_in", i, U_IN, ((in2, i * COLS), (in2, i * COLS + D_FF)))
            with sp.Fori(0, DJOBS // 2) as i:
                pair("ffn2_out", i, U_OUT, ((out2, i * (2 * COLS)), (out2, i * (2 * COLS) + COLS)))

            for j in range(DJOBS):
                for t in range(2):
                    sp.wait_ge(fin_taken, 2 * j + t + 1)
                    sp.dma_start(out[0, t * P:(t + 1) * P, j * COLS:(j + 1) * COLS], out_tile[:, j, t, :])\
                      .then_inc(stored, 16)
            sp.wait_ge(stored, 16 * 2 * DJOBS)

        @block.gpsimd
        def _(pool):
            ada2 = units_of(ada_w)
            used = ADA_PRE * KD - PRE_SKIPPED

            def fetch(a, i, started=True):
                if started:
                    pool.wait_ge(ada_mac, i * KD + (used + KU * (a - 1)))
                pool.dma_start(ada_raw[:, a % 2], ada2[a % ADA_UNITS, :, :, ds((i + ADA_PRE + a // ADA_UNITS) * COLS, COLS)])\
                    .then_inc(ada_landed[a % 2], 16)

            for a in range(2):
                fetch(a, 0, started=False)
            with pool.Fori(0, ADA_CHUNKS - ADA_PRE - 1) as i:
                for a in range(2, ADA_UNITS + 2):
                    fetch(a, i)
            for a in range(2, ADA_UNITS):
                fetch(a, ADA_CHUNKS - ADA_PRE - 1)

        @block.scalar
        def _(act):
            def settled():
                act.wait_ge(eps_ready, 1)

            def split(slot, u, started=True):
                act.wait_ge(raw_landed[slot], 4 * (u - slot) + 16)
                if started:
                    act.wait_ge(unit_done, u - (RING - 1))
                nc.scalar.activation(w_hi[:, slot], raw[:, slot], ACT.Copy).then_inc(hi_ready, 1)

            act.wait_ge(vec_turned, 1)
            nc.scalar.activation(vec[:], pm[:, 0, 0:V_END], ACT.Copy).then_inc(vec_ready, 1)
            act.wait_ge(vec_ready, 1)
            nc.scalar.activation(silu_c[:], vec[:, V_C:V_C + KD], ACT.Silu).then_inc(silu_ready, 1)
            act.wait_ge(expo_ready, 1)
            nc.scalar.activation(expo[:], expo[:], ACT.Exp).then_inc(expo_done, 1)
            for g in range(KD // 2):
                act.wait_ge(x_turned, g + 1)
                nc.scalar.activation(h[:, 2 * g:2 * g + 2, :], pm[:, 2 + g % 2, :].rearrange("p (c t) -> p c t", c=2),
                                     ACT.Copy).then_inc(x_taken, 1)
            for j in range(DJOBS):
                act.wait_ge(x_taken, 2 * (j + 1))
                if j:
                    act.wait_ge(sq_used, j)
                nc.scalar.activation(tmp[:], h[:, BLK * j:BLK * (j + 1), :], ACT.Square).then_inc(sq_ready, 1)
            act.wait_ge(eps_ready, 1)

            def root(m):
                nc.scalar.activation(junk[:], eps[:], ACT.Sqrt)
                act.wait_ge(ss_ready, m + 1)
                nc.scalar.activation(rstd[:], rstd[:], ACT.Sqrt, scale=1.0 / D, bias=eps[:]).then_inc(root_ready, 1)

            root(0)
            for slot in range(RING):
                split(slot, slot, started=False)

            def normalise(m, shift):
                if m:
                    root(m)
                for k in range(KD):
                    act.wait_ge(t_ready, m * KD + k + 1)
                    nc.scalar.activation(n[:, k, 0, :], tmp[:, k % BLK, :], ACT.Identity,
                                         bias=mods[:, shift + k:shift + k + 1]).then_inc(n_hi, 1)

            def ffn_in(name, ffn):
                with act.Fori(0, PAIRS) as i:
                    for s in range(2 * U_IN):
                        u = UNIT0[name] + i * (2 * U_IN) + s
                        split(s % RING, u + LEAD)
                        if s == U_IN - 1:
                            act.wait_ge(unit_done, u + 1)
                            act.wait_ge(n_ready, (2 * ffn + 1) * KD)
                            nc.scalar.activation(tmp[:], acc[0][:], ACT.Silu).then_inc(half_free[0], 1)
                        if s == 2 * U_IN - 1:
                            act.wait_ge(half_free[1], JOB0[name] // 2 + i + 1)
                            settled()
                            nc.scalar.activation(hid[:, ds(i * BLK, BLK), 0, :], tmp[:], ACT.Copy).then_inc(hid_hi, 1)
                            act.wait_ge(hid_ready, ffn * PAIRS + i + 1)

            def residual_out(name, units, m):
                with act.Fori(0, DJOBS // 2) as i:
                    for s in range(2 * units):
                        split(s % RING, UNIT0[name] + i * (2 * units) + s + LEAD)
                        if s % units == units - 1:
                            b = s // units
                            act.wait_ge(half_free[b], JOB0[name] // 2 + i + 1)
                            act.wait_ge(sq_used, m * DJOBS + 2 * i + b)
                            settled()
                            nc.scalar.activation(tmp[:], h[:, ds(i * (2 * BLK) + b * BLK, BLK), :], ACT.Square)\
                                .then_inc(sq_ready, 1)

            normalise(0, SH1)
            ffn_in("ffn1_in", 0)
            residual_out("ffn1_out", U_OUT, 1)
            normalise(1, SH2)

            act.wait_ge(t_ready, 2 * KD)
            act.dma_start(h_store, h[:].rearrange("p k t -> p (k t)")).then_inc(h_stored, 16)
            act.dma_start(pos[:], positions[0].partition_broadcast(P)).then_inc(pos_landed, 16)

            def hgrn(s, i, own):
                if s == 0:
                    nc.scalar.activation(logf[:], blk(mixs, i + B_HF), ACT.Ln).then_inc(a_logf, 1)
                    nc.scalar.activation(v_tok, blk(mixs, i + B_HI).rearrange("p (t v) -> p t v", t=2), ACT.Copy).then_inc(a_vtok, 1)
                if s == 4:
                    act.wait_ge(a_arg, i + 1)
                    nc.scalar.activation(X[:], X[:], ACT.Exp).then_inc(a_exp, 1)
                if s == 13:
                    act.wait_ge(a_o, i + 1)
                    nc.scalar.activation(o_sq[:], acc[0][:, 2, :], ACT.Square)
                    nc.scalar.activation(blk(mixs, i + B_HF), acc[0][:, 2, :], ACT.Copy).then_inc(a_taken, 1)

            def diff(s, i, own):
                if s == 1:
                    nc.scalar.activation(rt[:, 0:2, :], mixs[:, ds(2 * i + B_DQ, 2), :], ACT.Square)
                    nc.scalar.activation(sq_k[:], mixs[:, ds(2 * i + B_DK, 2), :], ACT.Square).then_inc(b_sq, 1)
                    nc.scalar.activation(v_tok2[:], mixs[:, ds(2 * i + B_DV, 2), :].rearrange("p a (t v) -> p (a t) v", t=2), ACT.Copy)\
                        .then_inc(b_vtok, 1)
                if s == 3:
                    act.wait_ge(b_ss, i + 1)
                    act.wait_ge(a_b, i + (DIFF_PAIR - HGRN_PAIR + 1))
                    own.link(nc.scalar.activation(rt, pm[:, 2:4, :].rearrange("p b (a t) -> p (b a) t", t=SEQ), ACT.Ln, scale=1.0 / DH, bias=eps[:]))
                    nc.scalar.activation(rt, rt, ACT.Exp, scale=-0.5).then_inc(b_rstd, 1)
                if s == 11:
                    act.wait_ge(b_max, i + 1)
                    for hm in range(4):
                        for t in range(2):
                            part = score[:, hm // 2, hm % 2, t * P:(1 + 2 * t) * P]
                            ins = nc.scalar.activation(part, part, ACT.Exp, bias=row_max[:, 2 * hm + t:2 * hm + t + 1],
                                                       accum_out=row_sum[:, 2 * hm + t:2 * hm + t + 1])
                    ins.then_inc(b_exp, 1)
                if s == 14:
                    act.wait_ge(b_wturn, i + 1)
                    nc.scalar.activation(w_key[:], pm[:, 2:4, 0:3 * P].rearrange("p b (g t) -> p b g t", t=P), ACT.Copy).then_inc(b_wkey, 1)
                if s == 15:
                    act.wait_ge(b_o, i + 1)
                    o = pm[:, 2, :].rearrange("p (a t) -> p a t", a=2)
                    nc.scalar.activation(rt[:, 0:2, :], o, ACT.Square).then_inc(b_osq, 1)
                    nc.scalar.activation(mixs[:, ds(2 * i + B_DK, 2), :], o, ACT.Copy).then_inc(b_taken, 1)

            def output_roots(i, diff, own):
                act.wait_ge(a_ss, i - (HGRN_PAIR - 1))
                ins = nc.scalar.activation(o_sq[:], pm[:, 1, 0:SEQ], ACT.Ln, scale=1.0 / P, bias=eps[:])
                if diff:
                    own.mark(ins)
                    act.wait_ge(b_oss, i - (DIFF_PAIR - 1))
                    ins = nc.scalar.activation(rt[:, 2:4, :], pm[:, 3, :].rearrange("p (a t) -> p a t", a=2), ACT.Ln, scale=1.0 / P, bias=eps[:])
                own.link(ins)
                nc.scalar.activation(o_sq[:], o_sq[:], ACT.Exp, scale=-0.5).then_inc(a_rstd, 1)
                if diff:
                    nc.scalar.activation(rt[:, 2:4, :], rt[:, 2:4, :], ACT.Exp, scale=-0.5).then_inc(b_orstd, 1)

            def mix_pairs(first, end, done):
                links = (first >= HGRN_PAIR) + 2 * (first >= DIFF_PAIR)
                with act.Fori(first, end) as i:
                    own = Chain(act, act_step, (i - first) * links + done)
                    for s in range(2 * U_IN):
                        u = UNIT0["mix_in"] + i * (2 * U_IN) + s
                        split(s % RING, u + LEAD)
                        if s % U_IN == U_IN - 1:
                            b = s // U_IN
                            if first == GB_PAIR:
                                place = i * (2 * GB_STRIDE) + (b * GB_STRIDE + B_GB - 2 * GB_STRIDE * GB_PAIR)
                            else:
                                place = i * (2 * BLK) + b * BLK
                            act.wait_ge(unit_done, u + 1)
                            settled()
                            dst, src = mixs[:, ds(place, BLK), :], acc[b][:]
                            if first in VALUE_PAIRS:
                                dst = dst.rearrange("p a (t v) -> p t a v", t=2)
                                src = src.rearrange("p (t c) (e v) -> p t (c e) v", t=2, e=2)
                            nc.scalar.activation(dst, src, ACT.Copy).then_inc(half_free[b], 1)
                        if first >= HGRN_PAIR:
                            hgrn(s, i - HGRN_PAIR, own)
                        if first >= DIFF_PAIR:
                            diff(s, i - DIFF_PAIR, own)
                    if first >= HGRN_PAIR:
                        output_roots(i, first >= DIFF_PAIR, own)
                    assert own.k == links
                return done + (end - first) * links

            mix_pairs(0, VALUE_PAIRS[0], 0)
            done = mix_pairs(VALUE_PAIRS[0], HGRN_PAIR, 0)
            act.wait_ge(half_free[1], JOB0["mix_in"] // 2 + HGRN_PAIR)
            nc.scalar.activation(mixs[:, B_HF:B_HF + HEADS, :], mixs[:, B_HF:B_HF + HEADS, :], ACT.Sigmoid).then_inc(sig_ready, 1)
            act.wait_ge(angle_ready, 1)
            nc.scalar.activation(trig[:], trig[:], ACT.Sin).then_inc(trig_ready, 1)
            act.wait_ge(f_ready, 1)
            done = mix_pairs(HGRN_PAIR, VALUE_PAIRS[1], done)
            done = mix_pairs(VALUE_PAIRS[1], DIFF_PAIR, done)
            nc.scalar.activation(mixs[:, B_HG:B_HG + HEADS, :], mixs[:, B_HG:B_HG + HEADS, :], ACT.Silu).then_inc(hg_ready, 1)
            done = mix_pairs(DIFF_PAIR, GB_PAIR, done)
            mix_pairs(GB_PAIR, PAIRS, done)

            act.wait_ge(a_done, PAIRS - DIFF_PAIR)
            for g, at in enumerate((B_HF, B_HF + BLK, B_DK, B_DK + BLK)):
                if g == 2:
                    act.wait_ge(b_done, HEADS // 2)
                nc.scalar.activation(n[:, g * BLK:(g + 1) * BLK, 0, :], mixs[:, at:at + BLK, :], ACT.Copy).then_inc(y_hi, 1)
            act.dma_start(h[:].rearrange("p k t -> p (k t)"), h_store).then_inc(h_back, 16)

            with act.Fori(0, DJOBS) as i:
                for s in range(2 * U_HEAD):
                    split(s % RING, UNIT0["heads_out"] + i * (2 * U_HEAD) + s + LEAD)
                    if s == 0:
                        for gate_of, stride in ((B_GA, BLK), (B_GB, GB_STRIDE)):
                            g = mixs[:, ds(i * stride + gate_of, BLK), :]
                            nc.scalar.activation(g, g, ACT.Sigmoid).then_inc(sig_ready, 1)
                act.wait_ge(mix_sum, i + 1)
                settled()
                nc.scalar.activation(hid[:, ds(i * BLK, BLK), 0, :], tmp[:], ACT.Copy).then_inc(mix_hi, 1)

            act.wait_ge(mix_ready, DJOBS)
            residual_out("mix_out", U_IN, 2)
            normalise(2, SH3)
            ffn_in("ffn2_in", 1)

            for s in range(DJOBS * U_OUT):
                if UNIT0["ffn2_out"] + s + LEAD < UNITS:
                    split(s % RING, UNIT0["ffn2_out"] + s + LEAD)
                if s % U_OUT == U_OUT - 1:
                    j = s // U_OUT
                    for t in range(2):
                        act.wait_ge(fin_turned, 2 * j + t + 1)
                        nc.scalar.activation(out_tile[:, j, t, :], pm[:, 2 * (j % 2) + t, :], ACT.Copy).then_inc(fin_taken, 1)

        @block.tensor
        def _(pe):
            pe.wait_ge(cst_landed, 16)
            pe.wait_ge(vec_landed, 16 * 14)
            nc.tensor.transpose(pm[:, 0, 0:P], vec_in[:, 0, :], ident)
            nc.tensor.transpose(pm[:, 0, P:V_END], vec_in[0:V_ROWS2, 1, :], ident[0:V_ROWS2, 0:V_ROWS2]).then_inc(vec_turned, 1)
            def ada_sum(added, total=ada_acc[:], bank=0):
                pe.wait_ge(ada_mac, added)
                ins = nc.tensor.matmul(pm[:, bank, :], ones, total, start=True, stop=True)
                ins.then_inc(ada_cols, 1)

            def square_sum(m, i, b):
                pe.wait_ge(sq_ready, m * DJOBS + 2 * i + b + 1)
                for f in range(BLK):
                    ins = nc.tensor.matmul(pm[:, 1, ds(i * SEQ, SEQ)], ones, tmp[:, f, :], start=(b == 0 and f == 0),
                                           stop=(b == 1 and f == BLK - 1))
                ins.then_inc(sq_used, 1)

            def ada_pair(i):
                for c in range(2):
                    pe.wait_ge(pre_landed[PRE_SLOTS - 2 + c], 16 * i + 16)
                    for k in range(PRE_K):
                        nc.tensor.matmul(pm[:, 2 * c, :], silu_wide[:, k, :], ada_pre[:, PRE_SLOTS - 2 + c, k, :], start=(k == 0), stop=False)
                for c in range(2):
                    pe.wait_ge(ada_mac, i * (2 * PRE_MACS) + (2 * PRE_MACS - 1 + c))
                    nc.tensor.matmul(pm[:, 2 * c, :], ones, pre_acc[c], start=False, stop=True).then_inc(ada_cols, 1)
                pe.wait_ge(ada_taken, 2 * i + 2)

            pe.wait_ge(vec_ready, 1)
            pe.wait_ge(wide_ready, 1)
            ada_pair(0)
            pe.wait_ge(x_landed, 16)
            for g in range(KD // 2):
                if g >= 2:
                    pe.wait_ge(x_taken, g - 1)
                for k in range(2):
                    for t in range(2):
                        ins = nc.tensor.transpose(pm[:, 2 + g % 2, (2 * k + t) * P:(2 * k + t + 1) * P],
                                                  x_in[:, t, (2 * g + k) * P:(2 * g + k + 1) * P], ident)
                ins.then_inc(x_turned, 1)
            for j in range(DJOBS):
                square_sum(0, j // 2, j % 2)
            with pe.Fori(1, ADA_PRE // 2) as i:
                ada_pair(i)

            def unit(slot, u, half, rhs, k0, first, last):
                pe.wait_ge(split_ready, u + 1)
                for k in range(KU):
                    for f in range(BLK):
                        w, o = slice(f * P, (f + 1) * P), acc[half][:, f, :]
                        nc.tensor.matmul(o, w_hi[:, slot, k, w], rhs[:, k0 + k, 0, :], start=(first and k == 0 and f % 2 == 0), stop=False)
                        nc.tensor.matmul(o, w_hi[:, slot, k, w], rhs[:, k0 + k, 1, :], start=False, stop=False)
                        ins = nc.tensor.matmul(o, w_lo[:, slot, k, w], rhs[:, k0 + k, 0, :], start=False,
                                               stop=(last and k == KU - 1 and f % 2 == 1))
                ins.then_inc(unit_done, 1)

            def unit_by_token(slot, u, half, k0, first, last):
                pe.wait_ge(split_ready, u + 1)
                for k in range(KU):
                    for t in range(2):
                        o = acc[half][:, 2 * t:2 * t + 2, :].rearrange("p a t -> p (a t)")
                        hi, lo = (n[:, k0 + k, part, t * P:(t + 1) * P] for part in range(2))
                        nc.tensor.matmul(o, hi, w_hi[:, slot, k, :], start=(first and k == 0), stop=False)
                        nc.tensor.matmul(o, lo, w_hi[:, slot, k, :], start=False, stop=False)
                        ins = nc.tensor.matmul(o, hi, w_lo[:, slot, k, :], start=False, stop=(last and k == KU - 1))
                ins.then_inc(unit_done, 1)

            def pair(name, i, units, rhs, ready, after=None, started=True, at=(0, 0), by_token=False):
                for s in range(2 * units):
                    b, k = divmod(s, units)
                    if k == 0 and started:
                        pe.wait_ge(half_free[b], JOB0[name] // 2 + i)
                    ready(s)
                    if by_token:
                        unit_by_token(s % RING, UNIT0[name] + i * (2 * units) + s, b, KU * k, k == 0, k == units - 1)
                    else:
                        unit(s % RING, UNIT0[name] + i * (2 * units) + s, b, rhs, at[b] + KU * k, k == 0, k == units - 1)
                    if after is not None:
                        after(s)

            def normed(m):
                return lambda s: pe.wait_ge(n_ready, m * KD + KU * (s % U_IN + 1))

            def hidden(ffn):
                return lambda s: pe.wait_ge(hid_ready, ffn * PAIRS + s % U_OUT * KU // BLK + 1)

            def added(name, k=0):
                return (ADA0[name] + k + 1) * KD - PRE_SKIPPED

            def with_ada(name, i):
                return lambda s: ada_sum(i * KD + added(name)) if s == ADA_SUM_STEP else None

            def residual_out(name, units, ready, m, ada):
                with pe.Fori(0, DJOBS // 2) as i:
                    def after(s):
                        if s == units + 2:
                            square_sum(m, i, 0)
                        if s == 2 * units - 1:
                            square_sum(m, i, 1)
                        if ada and s in ADA_OUT_SUM:
                            ada_sum(i * (ADA_PER_OUT * KD) + added(name, ADA_OUT_SUM.index(s)))
                    pair(name, i, units, hid, ready, after)

            pair("ffn1_in", 0, U_IN, n, normed(0), with_ada("ffn1_in", 0), started=False)
            with pe.Fori(1, PAIRS) as i:
                pair("ffn1_in", i, U_IN, n, normed(0), with_ada("ffn1_in", i))
            residual_out("ffn1_out", U_OUT, hidden(0), 1, True)
            with pe.Fori(0, VALUE_PAIRS[0]) as i:
                pair("mix_in", i, U_IN, n, normed(1), with_ada("mix_in", i))
            i = VALUE_PAIRS[0]
            pair("mix_in", i, U_IN, n, normed(1), with_ada("mix_in", i), by_token=True)

            def hgrn(s, i, chunks):
                if s in (8, 10):
                    g = s // 10
                    if g:
                        pe.wait_ge(a_masked, 2 * i + 1)
                        pe.wait_ge(half_free[0], i + (JOB0["mix_in"] // 2 + HGRN_PAIR + 1))
                        nc.tensor.matmul(acc[0][:, 0, 0:P], X[:, LEVELS - 1, 0:P], X[:, LEVELS - 1, P:2 * P], start=True, stop=True)
                    else:
                        pe.wait_ge(ada_taken, chunks)
                        pe.wait_ge(a_x, i + 1)
                    for j in range(LEVELS - 1):
                        xg = X[:, j, g * P:(g + 1) * P]
                        nc.tensor.matmul(pm[:, j // 4, j % 4 * P:(j % 4 + 1) * P], xg, xg, start=True, stop=True)
                    nc.tensor.matmul(pm[:, 1, 3 * P:4 * P], kk[:, g * P:(g + 1) * P],
                                     mixs[:, ds(i + B_HQ, 1), g * P:(g + 1) * P].rearrange("p a t -> p (a t)"),
                                     start=True, stop=True).then_inc(a_sc, 1)
                if s == 13:
                    pe.wait_ge(a_vtok, i + 1)
                    pe.wait_ge(a_s, i + 1)
                    nc.tensor.matmul(acc[0][:, 2, 0:P], v_tok[:, 0, :], S[0], start=True, stop=True)
                    nc.tensor.matmul(acc[0][:, 2, P:SEQ], v_tok[:, 0, :], S[1], start=True, stop=False)
                    nc.tensor.matmul(acc[0][:, 2, P:SEQ], v_tok[:, 1, :], S[2], start=False, stop=True).then_inc(a_o, 1)
                if s == 14:
                    pe.wait_ge(a_taken, i + 1)
                    nc.tensor.matmul(pm[:, 1, 0:SEQ], ones, o_sq[:], start=True, stop=True).then_inc(a_ss, 1)

            def diff(s, i):
                if s == 3:
                    pe.wait_ge(b_sq, i + 1)
                    for w in range(2):
                        ins = nc.tensor.matmul(pm[:, 2 + w, :], half_ones, (rt[:, 0:2, :], sq_k)[w].rearrange("p a t -> p (a t)"),
                                               start=True, stop=True)
                    ins.then_inc(b_ss, 1)
                if s == 6:
                    pe.wait_ge(b_norm, i + 1)
                    for w in range(2):
                        ins = nc.tensor.matmul(pm[:, 2 + w, :], rot, qk[:, 2 * w:2 * w + 2, :].rearrange("p a t -> p (a t)"), start=True, stop=True)
                    ins.then_inc(b_rot, 1)
                if s in (9, 10):
                    a = s - 9
                    if a:
                        pe.wait_ge(b_masked, 2 * i + 1)
                    else:
                        pe.wait_ge(b_rope, i + 1)
                    for m in range(2):
                        r = slice(m * DH, (m + 1) * DH)
                        nc.tensor.matmul(pm[:, 2 + m, 0:P], qk[r, a, 0:P], qk[r, 2 + a, 0:P], start=True, stop=True)
                        ins = nc.tensor.matmul(pm[:, 2 + m, P:3 * P], qk[r, a, P:2 * P], qk[r, 2 + a, :], start=True, stop=True)
                    ins.then_inc(b_sc, 1)
                if s == 14:
                    pe.wait_ge(b_w, i + 1)
                    for a in range(2):
                        for g in range(3):
                            ins = nc.tensor.transpose(pm[:, 2 + a, g * P:(g + 1) * P], score[:, a, 0, g * P:(g + 1) * P], ident)
                    ins.then_inc(b_wturn, 1)
                if s == 15:
                    pe.wait_ge(b_vtok, i + 1)
                    pe.wait_ge(b_wkey, i + 1)
                    for a in range(2):
                        o = pm[:, 2, a * SEQ:(a + 1) * SEQ]
                        nc.tensor.matmul(o[:, 0:P], v_tok2[:, 2 * a, :], w_key[:, a, 0, :], start=True, stop=True)
                        nc.tensor.matmul(o[:, P:SEQ], v_tok2[:, 2 * a, :], w_key[:, a, 1, :], start=True, stop=False)
                        ins = nc.tensor.matmul(o[:, P:SEQ], v_tok2[:, 2 * a + 1, :], w_key[:, a, 2, :], start=False, stop=True)
                    ins.then_inc(b_o, 1)
                    pe.wait_ge(b_osq, i + 1)
                    nc.tensor.matmul(pm[:, 3, :], ones, rt[:, 0:2, :].rearrange("p a t -> p (a t)"), start=True, stop=True).then_inc(b_oss, 1)

            def beside_heads(i, diff_too, by_token=False):
                def after(s):
                    hgrn(s, i - HGRN_PAIR, ADA0["ffn2_in"] if diff_too else i + ADA0["mix_in"])
                    if diff_too:
                        diff(s, i - DIFF_PAIR)
                    if s == HEADS_SUM_STEP and not diff_too:
                        ada_sum(i * KD + added("mix_in"))
                pair("mix_in", i, U_IN, n, normed(1), after, by_token=by_token)

            with pe.Fori(HGRN_PAIR, VALUE_PAIRS[1]) as i:
                beside_heads(i, False)
            beside_heads(VALUE_PAIRS[1], False, by_token=True)
            with pe.Fori(DIFF_PAIR, PAIRS) as i:
                beside_heads(i, True)

            with pe.Fori(0, DJOBS) as i:
                pair("heads_out", i, U_HEAD, n, lambda s: pe.wait_ge(y_ready, s // 2 + 1), at=(0, HEADS))
            residual_out("mix_out", U_IN, lambda s: pe.wait_ge(mix_ready, s % U_IN * KU // BLK + 1), 2, False)
            with pe.Fori(0, ADA_LAST) as i:
                pair("ffn2_in", i, U_IN, n, normed(2), with_ada("ffn2_in", i))
            with pe.Fori(ADA_LAST, PAIRS) as i:
                pair("ffn2_in", i, U_IN, n, normed(2))

            with pe.Fori(0, DJOBS // 2) as i:
                def turn(b):
                    pe.wait_ge(half_free[b], JOB0["ffn2_out"] // 2 + i + 1)
                    for t in range(2):
                        for f in range(BLK):
                            ins = nc.tensor.transpose(pm[:, 2 * b + t, f * P:(f + 1) * P], tmp2[:, f, t * P:(t + 1) * P], ident)
                        ins.then_inc(fin_turned, 1)

                def after(s):
                    if s == U_OUT + 2:
                        turn(0)
                    if s == 2 * U_OUT - 1:
                        turn(1)
                        pe.wait_ge(fin_taken, 4 * i + 4)
                pair("ffn2_out", i, U_OUT, hid, hidden(1), after)

        @block.vector
        def _(dve):
            own = Chain(dve, dve_step)

            def split(slot, u):
                dve.wait_ge(hi_ready, u + 1)
                nc.vector.tensor_tensor(w_lo[:, slot], raw[:, slot], w_hi[:, slot], ALU.subtract).then_inc(split_ready, 1)

            def ada_add(total, w, k, before):
                if k == 0:
                    nc.vector.tensor_scalar(total, w, silu_c[:, 0:1], None, ALU.mult).then_inc(ada_mac, 1)
                else:
                    dve.wait_ge(ada_mac, before)
                    nc.vector.scalar_tensor_tensor(out=total, in0=w, scalar=silu_c[:, k:k + 1], in1=total,
                                                   op0=ALU.mult, op1=ALU.add).then_inc(ada_mac, 1)

            def ada_take(chunk, summed, total=ada_acc[:], bank=0):
                dve.wait_ge(ada_cols, summed)
                diagonal = total.rearrange("p (f t) -> p f t", t=P)
                nc.vector.tensor_tensor(diagonal, pm[:, bank, :].rearrange("p (f t) -> p f t", t=P),
                                        ident.unsqueeze(1).to_broadcast([P, BLK, P]), ALU.mult).then_inc(ada_own, 1)
                dve.wait_ge(ada_own, 2 * (summed - 1) + 1)
                nc.vector.tensor_reduce(ada_col[:], diagonal, AX_X, ALU.add).then_inc(ada_own, 1)
                dve.wait_ge(ada_own, 2 * (summed - 1) + 2)
                nc.vector.tensor_tensor(mods[:, ds(chunk * BLK, BLK)], ada_col[:], vec[:, ds(chunk * BLK + V_ADAB, BLK)],
                                        ALU.add).then_inc(ada_taken, 1)

            def ada_unit(a, name, i):
                g = (ADA0[name] - ADA_PRE + i) * ADA_UNITS + a
                dve.wait_ge(ada_landed[a % 2], 8 * (g - a % 2) + 16)
                for k in range(KU):
                    ada_add(ada_acc[:], ada_raw[:, a % 2, k, :], KU * a + k, i * KD + (ADA0[name] * KD - PRE_SKIPPED + KU * a + k))

            nc.vector.memset(eps[:], EPS).then_inc(eps_ready, 1)
            dve.wait_ge(silu_ready, 1)
            lb, one_less, div = (bound[:, k * HEADS:(k + 1) * HEADS] for k in range(3))
            rows = [vec[:, a:a + HEADS] for a in (V_LB0, V_LB1)]
            dve.wait_ge(lam_landed, 16 * 4)
            own.link(nc.vector.tensor_tensor(div, rows[0], rows[1], ALU.max))
            for k in range(2):
                nc.vector.tensor_tensor(expo[:, k * HEADS:(k + 1) * HEADS], rows[k], div, ALU.subtract)
            for k in range(2):
                ins = nc.vector.tensor_tensor_reduce(out=l_prod[:, k, :], in0=lvec[:, 2 * k, :], in1=lvec[:, 2 * k + 1, :],
                                                     scale=1.0, scalar=0.0, op0=ALU.mult, op1=ALU.add,
                                                     accum_out=expo[:, 2 * HEADS + k:2 * HEADS + k + 1])
            ins.then_inc(expo_ready, 1)
            own.link(nc.vector.tensor_scalar(sub_gain[:], vec[:, V_SUB:V_SUB + 1], 1.0 - LAM_INIT, None, ALU.mult))
            dve.wait_ge(expo_done, 1)
            own.link(nc.vector.tensor_tensor(div, expo[:, 0:HEADS], expo[:, HEADS:2 * HEADS], ALU.add))
            own.link(nc.vector.reciprocal(div, div))
            own.link(nc.vector.tensor_tensor(lb, expo[:, 0:HEADS], div, ALU.mult))
            own.link(nc.vector.tensor_scalar(one_less, lb, -1.0, 1.0, ALU.mult, ALU.add))
            own.link(nc.vector.tensor_tensor(neg_lam[:], expo[:, 2 * HEADS + 1:], expo[:, 2 * HEADS:2 * HEADS + 1], ALU.subtract))
            own.link(nc.vector.tensor_scalar(neg_lam[:], neg_lam[:], LAM_INIT, None, ALU.subtract))

            for k in range(PRE_K):
                ins = nc.vector.tensor_copy(silu_wide[:, k, :], silu_c[:, PRE_MACS + k:PRE_MACS + k + 1].to_broadcast([P, P]))
            ins.then_inc(wide_ready, 1)

            def ada_pair(i):
                for a in range(PRE_GROUPS - 1):
                    for c in range(2):
                        dve.wait_ge(pre_landed[2 * a + c], 16 * i + 16)
                    for k in range(PRE_K):
                        for c in range(2):
                            q = PRE_K * a + k
                            ada_add(pre_acc[c], ada_pre[:, 2 * a + c, k, :], q, i * (2 * PRE_MACS) + (2 * q + c - 1))
                for c in range(2):
                    ada_take(i + c * (KD // BLK), 2 * i + c + 1, pre_acc[c], 2 * c)

            def root(m):
                dve.wait_ge(sq_used, (m + 1) * DJOBS)
                nc.vector.tensor_copy(rstd[:], pm[:, 1, 0:SEQ]).then_inc(ss_part, 1)
                dve.wait_ge(ss_part, m + 1)
                nc.vector.tensor_tensor(rstd[:], rstd[:], pm[:, 1, SEQ:2 * SEQ], ALU.add).then_inc(ss_ready, 1)
                dve.wait_ge(root_ready, m + 1)
                nc.vector.reciprocal(rstd[:], rstd[:]).then_inc(rstd_ready, 1)

            def normalise(m, weight, scale, after=lambda k: None):
                dve.wait_ge(ada_taken, (scale + KD) // BLK)
                nc.vector.scalar_tensor_tensor(out=gain[:], in0=mods[:, scale:scale + KD], scalar=1.0,
                                               in1=vec[:, weight:weight + KD], op0=ALU.add, op1=ALU.mult).then_inc(gain_ready, 1)
                if m:
                    root(m)
                dve.wait_ge(rstd_ready, m + 1)
                dve.wait_ge(gain_ready, m + 1)
                shift = scale - KD

                def lo(k):
                    dve.wait_ge(n_hi, m * KD + k + 1)
                    nc.vector.scalar_tensor_tensor(out=n[:, k, 1, :], in0=tmp[:, k % BLK, :], scalar=mods[:, shift + k:shift + k + 1],
                                                   in1=n[:, k, 0, :], op0=ALU.add, op1=ALU.subtract).then_inc(n_ready, 1)
                    after(k)

                for k in range(KD):
                    if k >= BLK:
                        dve.wait_ge(n_ready, m * KD + k - BLK + 1)
                    nc.vector.scalar_tensor_tensor(out=tmp[:, k % BLK, :], in0=h[:, k, :], scalar=gain[:, k:k + 1],
                                                   in1=rstd[:], op0=ALU.mult, op1=ALU.mult).then_inc(t_ready, 1)
                    if k >= 1:
                        lo(k - 1)
                lo(KD - 1)

            with dve.Fori(0, ADA_PRE // 4) as i:
                ada_pair(i)
            root(0)
            with dve.Fori(ADA_PRE // 4, ADA_PRE // 2) as i:
                ada_pair(i)

            def ffn_in(name, ffn, first, end, ada):
                with dve.Fori(first, end) as i:
                    for s in range(2 * U_IN):
                        u = UNIT0[name] + i * (2 * U_IN) + s
                        split(s % RING, u + LEAD)
                        if s == 2 * U_IN - 1:
                            dve.wait_ge(unit_done, u + 1)
                            dve.wait_ge(half_free[0], JOB0[name] // 2 + i + 1)
                            nc.vector.tensor_tensor(tmp[:], acc[1][:], tmp[:], ALU.mult).then_inc(half_free[1], 1)
                            dve.wait_ge(hid_hi, ffn * PAIRS + i + 1)
                            nc.vector.tensor_tensor(hid[:, ds(i * BLK, BLK), 1, :], tmp[:], hid[:, ds(i * BLK, BLK), 0, :],
                                                    ALU.subtract).then_inc(hid_ready, 1)
                        if ada and s in ADA_STEPS:
                            ada_unit(ADA_STEPS.index(s), name, i)
                        if ada and s == ADA_TAKE_STEP:
                            ada_take(i + ADA0[name], i + (ADA0[name] + 1))

            def add_residual(dst, block0, b, factor, at):
                for f in range(BLK):
                    ins = nc.vector.scalar_tensor_tensor(out=dst(f), in0=acc[b][:, f, :], scalar=factor[:, ds(block0 + at + f, 1)],
                                                         in1=blk(h, block0 + f), op0=ALU.mult, op1=ALU.add)
                return ins

            def half_gate(g, count):
                dve.wait_ge(ada_taken, (g + KD) // BLK)
                nc.vector.tensor_scalar(gate[:], mods[:, g:g + KD], 0.5, None, ALU.mult).then_inc(gate_ready, 1)
                dve.wait_ge(gate_ready, count)

            def residual_out(name, units, factor, at, ada):
                with dve.Fori(0, DJOBS // 2) as i:
                    for s in range(2 * units):
                        u = UNIT0[name] + i * (2 * units) + s
                        if s % units < units - 1:
                            split(s % RING, u + LEAD)
                        else:
                            b = s // units
                            dve.wait_ge(unit_done, u + 1)
                            block0 = i * (2 * BLK) + b * BLK
                            add_residual(lambda f: blk(h, block0 + f), block0, b, factor, at).then_inc(half_free[b], 1)
                            split(s % RING, u + LEAD)
                        if ada:
                            part, step = divmod(s, ADA_OUT_STRIDE)
                            if part < ADA_PER_OUT and step in ADA_STEPS:
                                ada_unit(ADA_STEPS.index(step), name, i * ADA_PER_OUT + part)
                            if s - 1 in ADA_OUT_SUM:
                                chunk = i * ADA_PER_OUT + (ADA0[name] + ADA_OUT_SUM.index(s - 1))
                                ada_take(chunk, chunk + 1)

            normalise(0, V_N1, SC1, lambda k: split(k // 4, k // 4) if k % 4 == 1 else None)
            ffn_in("ffn1_in", 0, 0, PAIRS, True)
            half_gate(G1, 1)
            residual_out("ffn1_out", U_OUT, gate, 0, True)
            normalise(1, V_N2, SC2)

            def hgrn(s, i, own, gated):
                C = HGRN_CHUNK
                if s == 0:
                    nc.vector.tensor_scalar(kk, blk(mixs, i + B_HF), -1.0, 1.0, ALU.mult, ALU.add)
                    dve.wait_ge(a_logf, i + 1)
                    nc.vector.tensor_tensor_scan(bcum, reset, logf[:], 0.0, ALU.mult, ALU.add).then_inc(a_b, 1)
                if s == 1:
                    dve.wait_ge(a_b, i + 1)
                    for j in range(6):
                        m = 1 << j
                        bv = bcum.rearrange("p (n two m) -> p n two m", two=2, m=m)
                        xv = X[:, j, :].rearrange("p (n two m) -> p n two m", two=2, m=m)
                        r = bv[:, :, 0, m - 1:m].to_broadcast([P, SEQ // (2 * m), m])
                        nc.vector.tensor_tensor(xv[:, :, 0, :], r, bv[:, :, 0, :], ALU.subtract)
                        nc.vector.tensor_tensor(xv[:, :, 1, :], bv[:, :, 1, :], r, ALU.subtract)
                if s == 2:
                    b_at = [bcum[:, C * q:C * (q + 1)] for q in range(4)]
                    last = [bcum[:, C * (q + 1) - 1:C * (q + 1)] for q in range(4)]
                    for q in (0, 2):
                        nc.vector.tensor_scalar(X[:, 6, C * q:C * (q + 1)], b_at[q], -1.0, last[q], ALU.mult, ALU.add)
                        nc.vector.tensor_copy(X[:, 6, C * (q + 1):C * (q + 2)], b_at[q + 1])
                    nc.vector.tensor_scalar(X[:, 7, C:2 * C], b_at[1], -1.0, last[1], ALU.mult, ALU.add)
                    nc.vector.tensor_copy(X[:, 7, 2 * C:3 * C], b_at[2])
                    own.link(nc.vector.tensor_scalar(X[:, 7, 3 * C:4 * C], b_at[3], last[2], None, ALU.add))
                    nc.vector.tensor_scalar(X[:, 7, 0:C], X[:, 6, 0:C], last[1], None, ALU.add).then_inc(a_arg, 1)
                if s == 5:
                    dve.wait_ge(a_exp, i + 1)
                    for j in range(LEVELS):
                        m = 1 << j
                        xv, kv = (t.rearrange("p (n two m) -> p n two m", two=2, m=m) for t in (X[:, j, :], kk))
                        qv = mixs[:, ds(i + B_HQ, 1), :].rearrange("p a (n two m) -> p (a n) two m", two=2, m=m)
                        nc.vector.tensor_tensor(xv[:, :, 0, :], xv[:, :, 0, :], kv[:, :, 0, :], ALU.mult)
                        ins = nc.vector.tensor_tensor(xv[:, :, 1, :], xv[:, :, 1, :], qv[:, :, 1, :], ALU.mult)
                    ins.then_inc(a_x, 1)
                if s in (8, 11):
                    g = s // 11
                    dve.wait_ge(a_sc, 2 * i + g + 1)
                    nc.vector.tensor_tensor(masked[:], pm[:, 0:2, :].rearrange("p b (j t) -> p (b j) t", t=P), level_mask[:], ALU.mult)\
                      .then_inc(a_masked, 1)
                    dve.wait_ge(a_masked, 2 * i + g + 1)
                    if g:
                        nc.vector.tensor_copy(S[1], acc[0][:, 0, 0:P])
                    ins = nc.vector.tensor_reduce(S[2 * g], masked[:].rearrange("p j t -> p t j"), AX_X, ALU.add)
                    if g:
                        ins.then_inc(a_s, 1)
                    else:
                        own.link(ins)
                if s == 15:
                    dve.wait_ge(a_rstd, i + 1)
                    y = blk(mixs, i + B_HF)
                    nc.vector.scalar_tensor_tensor(out=y, in0=y, scalar=vec[:, V_HN:V_HN + 1], in1=o_sq[:], op0=ALU.mult, op1=ALU.mult)\
                      .then_inc(a_normed, 1)
                    if gated:
                        dve.wait_ge(hg_ready, 1)
                        dve.wait_ge(a_normed, i + 1)
                        early = DIFF_PAIR - HGRN_PAIR
                        for k in (i, i - early):
                            ins = nc.vector.tensor_tensor(blk(mixs, k + B_HF), blk(mixs, k + B_HF), blk(mixs, k + B_HG), ALU.mult)
                        ins.then_inc(a_done, 1)

            def diff(s, i, own):
                if s == 4:
                    dve.wait_ge(b_rstd, i + 1)
                    for w in range(2):
                        ins = nc.vector.scalar_tensor_tensor(out=qk[:, 2 * w:2 * w + 2, :], in0=mixs[:, ds(2 * i + (B_DQ, B_DK)[w], 2), :],
                                                             scalar=vec[:, V_QN + w:V_QN + w + 1], in1=rt[:, 2 * w:2 * w + 2, :],
                                                             op0=ALU.mult, op1=ALU.mult)
                    ins.then_inc(b_norm, 1)
                if s == 6:
                    dve.wait_ge(trig_ready, 1)
                    dve.wait_ge(b_norm, i + 1)
                    dve.wait_ge(b_rot, i + 1)
                    sin, cos = (trig[:, k:k + 1, :].to_broadcast([P, 4, SEQ]) for k in range(2))
                    nc.vector.tensor_tensor(qk[:], qk[:], cos, ALU.mult)
                    own.link(nc.vector.tensor_tensor(rt, pm[:, 2:4, :].rearrange("p b (a t) -> p (b a) t", t=SEQ), sin, ALU.mult))
                    nc.vector.tensor_tensor(qk[:], qk[:], rt, ALU.add).then_inc(b_rope, 1)
                if s in (9, 10):
                    a = s - 9
                    dve.wait_ge(b_sc, 2 * i + a + 1)
                    nc.vector.scalar_tensor_tensor(out=score[:, a], in0=pm[:, 2:4, 0:3 * P], scalar=DH ** -0.5,
                                                   in1=causal[:].unsqueeze(1).to_broadcast([P, 2, 3 * P]), op0=ALU.mult, op1=ALU.add)\
                      .then_inc(b_masked, 1)
                if s == 10:
                    dve.wait_ge(b_masked, 2 * i + 2)
                    sv = score[:].rearrange("p a m k -> p (a m) k")
                    mv = row_max[:].rearrange("p (m t) -> p m t", t=2)
                    nc.vector.tensor_reduce(mv[:, :, 0], sv[:, :, 0:P], AX_X, ALU.max)
                    own.link(nc.vector.tensor_reduce(mv[:, :, 1], sv[:, :, P:3 * P], AX_X, ALU.max))
                    nc.vector.tensor_scalar(row_max[:], row_max[:], -1.0, None, ALU.mult).then_inc(b_max, 1)
                if s == 12:
                    dve.wait_ge(b_exp, i + 1)
                    own.link(nc.vector.reciprocal(row_sum[:], row_sum[:]))
                    second = row_sum[:].rearrange("p (a m t) -> p a m t", m=2, t=2)[:, :, 1, :]
                    own.link(nc.vector.tensor_scalar(second, second, neg_lam[:], None, ALU.mult))
                    for m in (1, 0):
                        for a in range(2):
                            for t in range(2):
                                cols, f = slice(t * P, (1 + 2 * t) * P), row_sum[:, 4 * a + 2 * m + t:4 * a + 2 * m + t + 1]
                                if m:
                                    ins = nc.vector.tensor_scalar(score[:, a, 1, cols], score[:, a, 1, cols], f, None, ALU.mult)
                                else:
                                    ins = nc.vector.scalar_tensor_tensor(out=score[:, a, 0, cols], in0=score[:, a, 0, cols], scalar=f,
                                                                         in1=score[:, a, 1, cols], op0=ALU.mult, op1=ALU.add)
                        if m:
                            own.link(ins)
                    ins.then_inc(b_w, 1)
                if s == 15:
                    dve.wait_ge(b_orstd, i + 1)
                    y = mixs[:, ds(2 * i + B_DK, 2), :]
                    nc.vector.scalar_tensor_tensor(out=y, in0=y, scalar=sub_gain[:], in1=rt[:, 2:4, :], op0=ALU.mult, op1=ALU.mult)\
                      .then_inc(b_done, 1)

            def mix_pairs(first, end, done):
                links = 2 * (first >= HGRN_PAIR) + 5 * (first >= DIFF_PAIR)
                steps, take = (HEADS_ADA_STEPS, HEADS_SUM_STEP) if first >= HGRN_PAIR else (ADA_STEPS, ADA_TAKE_STEP)
                with dve.Fori(first, end) as i:
                    own = Chain(dve, dve_step, (i - first) * links + done)
                    for s in range(2 * U_IN):
                        split(s % RING, UNIT0["mix_in"] + i * (2 * U_IN) + s + LEAD)
                        if first >= HGRN_PAIR:
                            hgrn(s, i - HGRN_PAIR, own, first >= DIFF_PAIR)
                        if first >= DIFF_PAIR:
                            diff(s, i - DIFF_PAIR, own)
                        if s in steps and first < DIFF_PAIR:
                            ada_unit(steps.index(s), "mix_in", i)
                        if s == take and first < DIFF_PAIR:
                            ada_take(i + ADA0["mix_in"], i + (ADA0["mix_in"] + 1))
                    assert own.k == links
                return done + (end - first) * links

            mix_pairs(0, HGRN_PAIR - 1, 0)

            dve.wait_ge(pos_landed, 16)
            turn = (6.28125, 0.0019350051879882812)
            turn += (2 * np.pi - sum(turn),)
            big = 1.5 * 2.0 ** 23
            own.link(nc.vector.tensor_copy(angle[:], pos[:]))
            own.link(nc.vector.tensor_scalar(angle[:], angle[:], freq, None, ALU.mult))
            for k, quarter in enumerate((0.0, 0.25)):
                ins = nc.vector.tensor_scalar(whole[:, k, :], angle[:], 1.0 / (2 * np.pi), quarter, ALU.mult, ALU.add)
            own.link(ins)
            own.link(nc.vector.tensor_scalar(whole[:], whole[:], big, None, ALU.add))
            own.link(nc.vector.tensor_scalar(whole[:], whole[:], big, None, ALU.subtract))
            src = angle[:].unsqueeze(1).to_broadcast([P, 2, SEQ])
            for part in turn:
                own.link(nc.vector.scalar_tensor_tensor(out=trig[:], in0=whole[:], scalar=-float(part), in1=src, op0=ALU.mult, op1=ALU.add))
                src = trig[:]
            own.link(nc.vector.tensor_scalar(trig[:, 1, :], trig[:, 1, :], np.pi / 2, None, ALU.add))
            nc.vector.tensor_scalar(trig[:], trig[:], 3.1415925, -3.1415925, ALU.min, ALU.max).then_inc(angle_ready, 1)
            mix_pairs(HGRN_PAIR - 1, HGRN_PAIR, 0)

            dve.wait_ge(late_landed, 16 * 3)
            dve.wait_ge(sig_ready, 1)
            for k in range(HEADS):
                ins = nc.vector.tensor_scalar(mixs[:, B_HF + k, :], mixs[:, B_HF + k, :], one_less[:, k:k + 1], lb[:, k:k + 1],
                                              ALU.mult, ALU.add)
            ins.then_inc(f_ready, 1)
            dve.wait_ge(f_ready, 1)
            done = mix_pairs(HGRN_PAIR, DIFF_PAIR, own.k)

            mix_pairs(DIFF_PAIR, PAIRS, done)

            for g, at in enumerate((B_HF, B_HF + BLK, B_DK, B_DK + BLK)):
                dve.wait_ge(y_hi, g + 1)
                nc.vector.tensor_tensor(n[:, g * BLK:(g + 1) * BLK, 1, :], mixs[:, at:at + BLK, :], n[:, g * BLK:(g + 1) * BLK, 0, :],
                                        ALU.subtract).then_inc(y_ready, 1)

            with dve.Fori(0, DJOBS) as i:
                for s in range(2 * U_HEAD):
                    u = UNIT0["heads_out"] + i * (2 * U_HEAD) + s
                    split(s % RING, u + LEAD)
                    if s == U_HEAD - 1:
                        dve.wait_ge(sig_ready, 2 * i + 3)
                        dve.wait_ge(unit_done, u + 1)
                        nc.vector.tensor_tensor(tmp2[:], acc[0][:], mixs[:, ds(i * BLK + B_GA, BLK), :], ALU.mult).then_inc(half_free[0], 1)
                    if s == 2 * U_HEAD - 1:
                        dve.wait_ge(unit_done, u + 1)
                        nc.vector.tensor_tensor(tmp[:], acc[1][:], mixs[:, ds(i * GB_STRIDE + B_GB, BLK), :], ALU.mult).then_inc(half_free[1], 1)
                        dve.wait_ge(half_free[0], JOB0["heads_out"] // 2 + i + 1)
                        dve.wait_ge(half_free[1], JOB0["heads_out"] // 2 + i + 1)
                        nc.vector.tensor_tensor(tmp[:], tmp[:], tmp2[:], ALU.add).then_inc(mix_sum, 1)
                dve.wait_ge(mix_hi, i + 1)
                dve.wait_ge(mix_sum, i + 1)
                nc.vector.tensor_tensor(hid[:, ds(i * BLK, BLK), 1, :], tmp[:], hid[:, ds(i * BLK, BLK), 0, :], ALU.subtract)\
                    .then_inc(mix_ready, 1)
                dve.wait_ge(mix_ready, i + 1)

            dve.wait_ge(h_back, 16)
            residual_out("mix_out", U_IN, mods, G2, False)
            normalise(2, V_N3, SC3)
            ffn_in("ffn2_in", 1, 0, ADA_LAST, True)
            ffn_in("ffn2_in", 1, ADA_LAST, PAIRS, False)
            half_gate(G3, 2)
            for s in range(DJOBS * U_OUT):
                u = UNIT0["ffn2_out"] + s
                if s % U_OUT == U_OUT - 1:
                    j = s // U_OUT
                    dve.wait_ge(unit_done, u + 1)
                    if j:
                        dve.wait_ge(fin_turned, 2 * j)
                    add_residual(lambda f: tmp2[:, f, :], j * BLK, j % 2, gate, 0).then_inc(half_free[j % 2], 1)
                if u + LEAD < UNITS:
                    split(s % RING, u + LEAD)


_INS = ["x", "c", "positions", "ada_w", "ada_b", "norm1_w", "ffn1_w_in", "ffn1_w_out", "norm2_w", "mix_w_in", "hgrn_lb",
        "hgrn_norm_w", "hgrn_w_out", "diff_q_norm_w", "diff_k_norm_w", "diff_lq1", "diff_lk1", "diff_lq2", "diff_lk2",
        "diff_subln_w", "diff_w_out", "mix_w_o", "norm3_w", "ffn2_w_in", "ffn2_w_out"]


def kernel(**inputs):
    import concourse.bacc as bacc
    from concourse.bass_utils import run_bass_kernel_spmd

    nc = bacc.Bacc("TRN2", target_bir_lowering=False, num_devices=1)
    arrays, args = {}, []
    for name in _INS + ["consts"]:
        a = constants() if name == "consts" else np.ascontiguousarray(inputs[name])
        arrays[f"in_{name}"] = a
        args.append(nc.dram_tensor(f"in_{name}", a.shape, mybir.dt.from_np(a.dtype), kind="ExternalInput").ap())
    args.append(nc.dram_tensor("out_0", (1, SEQ, D), F32, kind="ExternalOutput").ap())
    build(nc, *args)
    r = run_bass_kernel_spmd(nc, [arrays], core_ids=[0])
    return r.results[0]["out_0"]
```
